# Optimizing a Trainium2 kernel written in Bass

```python
import math
import jax, jax.numpy as jnp
from jax import lax
import numpy as np

D_MODEL = 1024
BATCH = 1
SEQ = 512
DEPTH = 1

HEAD_DIM = 64
DILATED_GROUPS = ((128, 1), (512, 4), (2048, 16))
N_DIL = len(DILATED_GROUPS)
HEADS_PER_GROUP = 8
N_ATTN_HEADS = N_DIL * HEADS_PER_GROUP
ATTN_WIDTH = N_ATTN_HEADS * HEAD_DIM
ATTN_OUT_WIDTH = HEADS_PER_GROUP * HEAD_DIM
ATTN_BLOCK = 128
N_REL_BUCKETS = 32
REL_MAX_DISTANCE = 2048

D_INNER = 2 * D_MODEL
SSM_HEAD_DIM = 64
N_SSM_HEADS = D_INNER // SSM_HEAD_DIM
N_SSM_GROUPS = 4
HEADS_PER_SSM_GROUP = N_SSM_HEADS // N_SSM_GROUPS
D_STATE = 128
CONV_WIDTH = 4
SSD_CHUNK = 128
XBC_WIDTH = D_INNER + 2 * N_SSM_GROUPS * D_STATE

N_BRANCHES = 2
D_FF = -(-8 * D_MODEL // (3 * 256)) * 256
IN_PROJ_WIDTH = 3 * ATTN_WIDTH + D_INNER + XBC_WIDTH + N_SSM_HEADS + N_BRANCHES * D_MODEL
EPS = 1e-6


def rmsnorm(x, w):
    xf = x.astype(jnp.float32)
    y = xf * lax.rsqrt(jnp.mean(xf * xf, axis=-1, keepdims=True) + EPS)
    return (y * w.astype(jnp.float32)).astype(x.dtype)

def t5_causal_bucket(dist):
    max_exact = N_REL_BUCKETS // 2
    d_f = jnp.maximum(dist, 1).astype(jnp.float32)
    large = max_exact + (jnp.log(d_f / max_exact) / math.log(REL_MAX_DISTANCE / max_exact)
                         * (N_REL_BUCKETS - max_exact)).astype(jnp.int32)
    large = jnp.minimum(large, N_REL_BUCKETS - 1)
    return jnp.where(dist < max_exact, dist, large)

def rel_bias_block(rel_bias_g, dilation, n_steps):
    qi = jnp.arange(ATTN_BLOCK)[:, None]
    kj = jnp.arange(2 * ATTN_BLOCK)[None, :]
    steps = jnp.clip(qi + ATTN_BLOCK - kj, 0, n_steps)
    bucket = t5_causal_bucket(steps * dilation)
    return jnp.transpose(rel_bias_g[bucket], (2, 0, 1)).astype(jnp.float32)

def dilated_window_attention(q, k, v, bias, dilation, n_steps):
    b, s, h, dh = q.shape
    seg = s // dilation
    nb = -(-seg // ATTN_BLOCK)
    segp = nb * ATTN_BLOCK

    def to_blocks(t):
        t = t.reshape(b, seg, dilation, h, dh).transpose(0, 2, 1, 3, 4).reshape(b * dilation, seg, h, dh)
        t = jnp.pad(t, ((0, 0), (0, segp - seg), (0, 0), (0, 0)))
        return t.reshape(b * dilation, nb, ATTN_BLOCK, h, dh)

    def with_prev(t):
        prev = jnp.pad(t[:, :-1], ((0, 0), (1, 0), (0, 0), (0, 0), (0, 0)))
        return jnp.concatenate([prev, t], axis=2)

    qb = to_blocks(q)
    kw = with_prev(to_blocks(k))
    vw = with_prev(to_blocks(v))

    qi = jnp.arange(ATTN_BLOCK)[:, None]
    kj = jnp.arange(2 * ATTN_BLOCK)[None, :]
    steps = qi + ATTN_BLOCK - kj
    blk = jnp.arange(nb)[:, None, None]
    valid = (steps >= 0) & (steps <= n_steps) & (blk * ATTN_BLOCK - ATTN_BLOCK + kj >= 0)

    logits = jnp.einsum('znqhd,znkhd->znhqk', qb, kw).astype(jnp.float32) * (HEAD_DIM ** -0.5) + bias
    logits = jnp.where(valid[None, :, None], logits, -jnp.inf)
    m = jnp.max(logits, axis=-1, keepdims=True)
    p = jnp.exp(logits - m)
    den = jnp.sum(p, axis=-1, keepdims=True)
    o = jnp.einsum('znhqk,znkhd->znqhd', p, vw.astype(jnp.float32)) / jnp.swapaxes(den, 2, 3)
    lse = jnp.swapaxes((m + jnp.log(den))[..., 0], 2, 3)

    o = o.reshape(b, dilation, segp, h, dh)[:, :, :seg]
    o = jnp.swapaxes(o, 1, 2).reshape(b, s, h, dh)
    lse = lse.reshape(b, dilation, segp, h)[:, :, :seg]
    lse = jnp.swapaxes(lse, 1, 2).reshape(b, s, h)
    return o, lse

def causal_depthwise_conv(x, w, bias):
    c = x.shape[-1]
    y = lax.conv_general_dilated(x, w[:, None, :], window_strides=(1,),
                                 padding=((CONV_WIDTH - 1, 0),),
                                 dimension_numbers=('NWC', 'WIO', 'NWC'),
                                 feature_group_count=c)
    return y + bias

def ssd_chunked_scan(xh, dt, a, bm, cm):
    b, s = xh.shape[:2]
    nc = s // SSD_CHUNK

    def chunks(t):
        return jnp.swapaxes(t.reshape(b, nc, SSD_CHUNK, *t.shape[2:]), 0, 1)

    causal = jnp.tril(jnp.ones((SSD_CHUNK, SSD_CHUNK), dtype=bool))[None, :, :, None, None]

    def step(state, inp):
        x_, dt_, b_, c_ = inp
        la = jnp.cumsum(dt_ * a, axis=1)
        seg = la[:, :, None] - la[:, None, :]
        decay = jnp.exp(jnp.where(causal, seg, -jnp.inf))
        cb = jnp.einsum('bign,bjgn->bijg', c_, b_)
        xdt = x_ * dt_[..., None]
        y_intra = jnp.einsum('bijg,bijgh,bjghp->bighp', cb, decay, xdt)
        y_inter = jnp.einsum('bign,bghpn->bighp', c_, state) * jnp.exp(la)[..., None]
        to_end = jnp.exp(la[:, -1:] - la)
        new_state = (state * jnp.exp(la[:, -1])[..., None, None]
                     + jnp.einsum('bjgn,bjgh,bjghp->bghpn', b_, to_end, xdt))
        return new_state, y_intra + y_inter

    state0 = jnp.zeros((b, N_SSM_GROUPS, HEADS_PER_SSM_GROUP, SSM_HEAD_DIM, D_STATE), jnp.float32)
    _, ys = lax.scan(step, state0, (chunks(xh), chunks(dt), chunks(bm), chunks(cm)))
    return jnp.swapaxes(ys, 0, 1).reshape(b, s, N_SSM_GROUPS, HEADS_PER_SSM_GROUP, SSM_HEAD_DIM)

def hybrid_mixer(xn, w_in, conv_w, conv_b, dt_bias, a_log, d_skip, ssm_norm_w,
                 w_attn_branch, w_ssm_branch, w_out, attn_biases):
    b, s, _ = xn.shape
    proj = xn @ w_in
    q, k, v, z, xbc, dt_raw, gate_logits = jnp.split(
        proj, np.cumsum([ATTN_WIDTH, ATTN_WIDTH, ATTN_WIDTH, D_INNER, XBC_WIDTH, N_SSM_HEADS]).tolist(), axis=-1)

    q = q.reshape(b, s, N_DIL, HEADS_PER_GROUP, HEAD_DIM)
    k = k.reshape(b, s, N_DIL, HEADS_PER_GROUP, HEAD_DIM)
    v = v.reshape(b, s, N_DIL, HEADS_PER_GROUP, HEAD_DIM)
    outs, lses = [], []
    for g, (window, dil) in enumerate(DILATED_GROUPS):
        o_g, lse_g = dilated_window_attention(q[:, :, g], k[:, :, g], v[:, :, g],
                                              attn_biases[g], dil, window // dil)
        outs.append(o_g)
        lses.append(lse_g)
    o = jnp.stack(outs, axis=2)
    alpha = jax.nn.softmax(jnp.stack(lses, axis=2), axis=2)
    attn = jnp.sum(alpha[..., None] * o, axis=2).reshape(b, s, ATTN_OUT_WIDTH).astype(xn.dtype)

    xbc = jax.nn.silu(causal_depthwise_conv(xbc, conv_w, conv_b))
    xs, bm, cm = jnp.split(xbc, [D_INNER, D_INNER + N_SSM_GROUPS * D_STATE], axis=-1)
    xh = xs.reshape(b, s, N_SSM_GROUPS, HEADS_PER_SSM_GROUP, SSM_HEAD_DIM).astype(jnp.float32)
    bm = bm.reshape(b, s, N_SSM_GROUPS, D_STATE).astype(jnp.float32)
    cm = cm.reshape(b, s, N_SSM_GROUPS, D_STATE).astype(jnp.float32)
    dt = jax.nn.softplus(dt_raw.astype(jnp.float32) + dt_bias.astype(jnp.float32))
    dt = dt.reshape(b, s, N_SSM_GROUPS, HEADS_PER_SSM_GROUP)
    a = -jnp.exp(a_log.astype(jnp.float32)).reshape(N_SSM_GROUPS, HEADS_PER_SSM_GROUP)
    y = ssd_chunked_scan(xh, dt, a, bm, cm)
    y = y + xh * d_skip.astype(jnp.float32).reshape(N_SSM_GROUPS, HEADS_PER_SSM_GROUP)[..., None]
    yg = (y.reshape(b, s, D_INNER) * jax.nn.silu(z.astype(jnp.float32))).reshape(b, s, N_SSM_GROUPS, D_INNER // N_SSM_GROUPS)
    yg = yg * lax.rsqrt(jnp.mean(yg * yg, axis=-1, keepdims=True) + EPS)
    ssm = (yg.reshape(b, s, D_INNER) * ssm_norm_w.astype(jnp.float32)).astype(xn.dtype)

    gates = jax.nn.sigmoid(gate_logits.astype(jnp.float32)).reshape(b, s, N_BRANCHES, D_MODEL)
    merged = (gates[:, :, 0] * (attn @ w_attn_branch).astype(jnp.float32)
              + gates[:, :, 1] * (ssm @ w_ssm_branch).astype(jnp.float32)).astype(xn.dtype)
    return merged @ w_out

def swiglu(xn, w_ffn_in, w_ffn_out):
    gate, up = jnp.split(xn @ w_ffn_in, 2, axis=-1)
    return (jax.nn.silu(gate) * up) @ w_ffn_out

def first_inputs(seed: int = 0) -> dict:
    key = jax.random.key(seed)
    ks = jax.random.split(key, 20)
    f32 = jnp.float32
    nrm = lambda k, shape, scale: jax.random.normal(k, shape, f32) * scale
    dt0 = jnp.exp(jax.random.uniform(ks[5], (DEPTH, N_SSM_HEADS), f32, math.log(1e-3), math.log(1e-1)))
    return {
        "x": nrm(ks[0], (BATCH, SEQ, D_MODEL), 1.0),
        "norm1_w": 1.0 + nrm(ks[1], (DEPTH, D_MODEL), 0.02),
        "w_in": nrm(ks[2], (DEPTH, D_MODEL, IN_PROJ_WIDTH), D_MODEL ** -0.5),
        "conv_w": nrm(ks[3], (DEPTH, CONV_WIDTH, XBC_WIDTH), CONV_WIDTH ** -0.5),
        "conv_b": nrm(ks[4], (DEPTH, XBC_WIDTH), 0.02),
        "dt_bias": dt0 + jnp.log(-jnp.expm1(-dt0)),
        "a_log": jnp.log(jax.random.uniform(ks[6], (DEPTH, N_SSM_HEADS), f32, 1.0, 16.0)),
        "d_skip": 1.0 + nrm(ks[7], (DEPTH, N_SSM_HEADS), 0.1),
        "ssm_norm_w": 1.0 + nrm(ks[8], (DEPTH, D_INNER), 0.02),
        "w_attn_branch": nrm(ks[9], (DEPTH, ATTN_OUT_WIDTH, D_MODEL), ATTN_OUT_WIDTH ** -0.5),
        "w_ssm_branch": nrm(ks[10], (DEPTH, D_INNER, D_MODEL), D_INNER ** -0.5),
        "w_out": nrm(ks[11], (DEPTH, D_MODEL, D_MODEL), D_MODEL ** -0.5),
        "norm2_w": 1.0 + nrm(ks[12], (DEPTH, D_MODEL), 0.02),
        "w_ffn_in": nrm(ks[13], (DEPTH, D_MODEL, 2 * D_FF), D_MODEL ** -0.5),
        "w_ffn_out": nrm(ks[14], (DEPTH, D_FF, D_MODEL), D_FF ** -0.5),
        "rel_bias": nrm(ks[15], (N_REL_BUCKETS, N_ATTN_HEADS), 0.5),
        "final_norm_w": 1.0 + nrm(ks[16], (D_MODEL,), 0.02),
    }

def first_block(x, norm1_w, w_in, conv_w, conv_b, dt_bias, a_log, d_skip, ssm_norm_w,
              w_attn_branch, w_ssm_branch, w_out, norm2_w, w_ffn_in, w_ffn_out,
              rel_bias, final_norm_w):
    attn_biases = [rel_bias_block(rel_bias[:, g * HEADS_PER_GROUP:(g + 1) * HEADS_PER_GROUP], dil, window // dil)
                   for g, (window, dil) in enumerate(DILATED_GROUPS)]
    h = x
    for layer in range(DEPTH):
        h = h + hybrid_mixer(rmsnorm(h, norm1_w[layer]), w_in[layer], conv_w[layer], conv_b[layer],
                             dt_bias[layer], a_log[layer], d_skip[layer], ssm_norm_w[layer],
                             w_attn_branch[layer], w_ssm_branch[layer], w_out[layer], attn_biases)
        h = h + swiglu(rmsnorm(h, norm2_w[layer]), w_ffn_in[layer], w_ffn_out[layer])
    return rmsnorm(h, final_norm_w)


DEPTH_2 = 2

GRID_W = 64
CTX_LEN = 256
LN_EPS = 64e-5
MIX_W = D_MODEL
CHUNK = 128
A_GROUPS = 4
A_WIDTH = MIX_W // 2
A_GDIM = A_WIDTH // A_GROUPS
B_HEAD = 64
B_WIDTH = MIX_W // 2
B_HEADS = B_WIDTH // B_HEAD
DECAY_LORA = 64
AAA_LORA = 64
GATE_LORA = 128
C_WIDTH = MIX_W
C_HEADS = 4
C_HEAD = C_WIDTH // C_HEADS
QKV_BLOCK = 4
C_CHUNK = 128
D_FF_2 = 2816
N_EVEN = (DEPTH_2 + 1) // 2
N_ODD = DEPTH_2 // 2
AB_IN = 2 * A_WIDTH + 3 * B_WIDTH + 2 * DECAY_LORA + 2 * AAA_LORA + GATE_LORA
C_IN = 2 * C_WIDTH + 4 * C_HEADS


def rmsnorm_2(x, g):
    xf = x.astype(jnp.float32)
    y = xf * lax.rsqrt(jnp.mean(xf * xf, axis=-1, keepdims=True) + EPS)
    return (y * g).astype(x.dtype)

def modulate(h, shift, scale):
    return h * (1 + scale) + shift

def ada_mod(cvec, w, b):
    m = jax.nn.silu(cvec) @ w + b
    m = m.reshape(cvec.shape[:-1] + (6, D_MODEL))
    if cvec.ndim == 2:
        return [m[:, i, None, :] for i in range(6)]
    return [m[i] for i in range(6)]

def dwconv1d(x, w):
    xp = jnp.pad(x, ((0, 0), (1, 1), (0, 0)))
    return xp[:, :-2] * w[0] + xp[:, 1:-1] * w[1] + xp[:, 2:] * w[2]

def dwconv_grid(x, w, rows):
    bn, t, ch = x.shape
    y = lax.conv_general_dilated(x.reshape(bn, rows, GRID_W, ch), w[:, :, None, :],
                                 window_strides=(1, 1), padding='SAME',
                                 dimension_numbers=('NHWC', 'HWIO', 'NHWC'),
                                 feature_group_count=ch)
    return y.reshape(bn, t, ch)

def conv_ffn(h, w_up, conv_w, conv_b, w_down, rows):
    a, b = jnp.split(h @ w_up, 2, axis=-1)
    a = dwconv1d(a, conv_w[1]) if rows is None else dwconv_grid(a, conv_w, rows)
    return (jax.nn.gelu(a + conv_b) * b) @ w_down

def spatial_gate(p, w_s, b_s, g_v):
    bn, t, _ = p.shape
    u, v = jnp.split(jax.nn.gelu(p[..., :2 * A_WIDTH]), 2, axis=-1)
    v = rmsnorm_2(v.reshape(bn, t // CHUNK, CHUNK, A_GROUPS, A_GDIM), g_v)
    z = jnp.einsum('gpq,bnqgc->bnpgc', w_s, v) + b_s.T[None, None, :, :, None]
    return u * z.reshape(bn, t, A_WIDTH)

def rwkv_prep(p, b_shift, b_w0, b_w_up, b_a0, b_a_up, b_g_up, b_kk, b_ka):
    bn, t, _ = p.shape
    o = 2 * A_WIDTH
    r, k, v = jnp.split(dwconv1d(p[..., o:o + 3 * B_WIDTH], b_shift), 3, axis=-1)
    o += 3 * B_WIDTH
    wd = p[..., o:o + 2 * DECAY_LORA].reshape(bn, t, 2, DECAY_LORA)
    o += 2 * DECAY_LORA
    ad = p[..., o:o + 2 * AAA_LORA].reshape(bn, t, 2, AAA_LORA)
    o += 2 * AAA_LORA
    gd = p[..., o:o + GATE_LORA]
    logw = -jax.nn.softplus(-(b_w0 + jnp.einsum('btdr,drc->btdc', jnp.tanh(wd), b_w_up))) - 0.5
    decay = jnp.exp(-jnp.exp(logw.astype(jnp.float32)))
    a = jax.nn.sigmoid(b_a0 + jnp.einsum('btdr,drc->btdc', ad, b_a_up))
    g = jax.nn.sigmoid(gd) @ b_g_up
    hs = lambda u: u.reshape(u.shape[:-1] + (B_HEADS, B_HEAD))
    kk = hs(k * b_kk).astype(jnp.float32)
    kk = (kk * lax.rsqrt(jnp.maximum(jnp.sum(kk * kk, axis=-1, keepdims=True), 1e-12))).astype(k.dtype)
    k_dir = k[:, :, None, :] * (1 + (a - 1) * b_ka)
    return hs(r), hs(decay), hs(k_dir), hs(v), kk, hs(a), g

def rwkv_dir_inputs(prep, d):
    r, w, kd, v, kk, a, _ = prep
    seq = (r, w[:, :, d], kd[:, :, d], v, kk, kk * a[:, :, d])
    return tuple(u[:, ::-1] for u in seq) if d == 1 else seq

def rwkv7_scan(r, w, k, v, kk, b, s0):
    dt = r.dtype
    def step(s, inp):
        r_t, w_t, k_t, v_t, kk_t, b_t = inp
        sa = jnp.einsum('bhvk,bhk->bhv', s, kk_t)
        s = s * w_t[:, :, None, :] - sa[..., None] * b_t[:, :, None, :] + v_t[..., None] * k_t[:, :, None, :]
        return s, jnp.einsum('bhvk,bhk->bhv', s, r_t)
    xs = tuple(jnp.moveaxis(u.astype(jnp.float32), 1, 0) for u in (r, w, k, v, kk, b))
    s, ys = lax.scan(step, s0, xs)
    return jnp.moveaxis(ys, 0, 1).astype(dt), s

def rwkv_out(y, prep, b_rk, ln_g, ln_b):
    r, _, kd, v, _, _, g = prep
    yf = y.astype(jnp.float32)
    mu = jnp.mean(yf, axis=-1, keepdims=True)
    var = jnp.mean(jnp.square(yf - mu), axis=-1, keepdims=True)
    yn = ((yf - mu) * lax.rsqrt(var + LN_EPS)).astype(r.dtype) * ln_g + ln_b
    bonus = jnp.sum(jnp.sum(r[:, :, None] * kd * b_rk, axis=-1, keepdims=True), axis=2) * v
    out = (yn + bonus) * g.reshape(v.shape)
    return out.reshape(v.shape[0], v.shape[1], B_WIDTH)

def rwkv_bidir(pc, pl, need_ctx, b_shift, b_w0, b_w_up, b_a0, b_a_up, b_g_up, b_kk, b_ka, b_rk, b_ln_g, b_ln_b):
    prep_c = rwkv_prep(pc, b_shift, b_w0, b_w_up, b_a0, b_a_up, b_g_up, b_kk, b_ka)
    prep_l = rwkv_prep(pl, b_shift, b_w0, b_w_up, b_a0, b_a_up, b_g_up, b_kk, b_ka)
    bn = pl.shape[0]
    ys_c, ys_l = [], []
    for d in range(2):
        s0 = jnp.zeros((bn, B_HEADS, B_HEAD, B_HEAD), jnp.float32)
        y_c, s_c = rwkv7_scan(*rwkv_dir_inputs(prep_c, d), s0)
        y_l, _ = rwkv7_scan(*rwkv_dir_inputs(prep_l, d), s_c)
        if d == 1:
            y_c, y_l = y_c[:, ::-1], y_l[:, ::-1]
        ys_c.append(y_c)
        ys_l.append(y_l)
    out_l = rwkv_out(ys_l[0] + ys_l[1], prep_l, b_rk, b_ln_g, b_ln_b)
    out_c = rwkv_out(ys_c[0] + ys_c[1], prep_c, b_rk, b_ln_g, b_ln_b) if need_ctx else None
    return out_c, out_l

def mixer_ab(hc, hl, need_ctx, w_in, w_out, a_ws, a_bs, a_gv, b_shift, b_w0, b_w_up, b_a0, b_a_up,
             b_g_up, b_kk, b_ka, b_rk, b_ln_g, b_ln_b):
    pc, pl = hc @ w_in, hl @ w_in
    bc, bl = rwkv_bidir(pc, pl, need_ctx, b_shift, b_w0, b_w_up, b_a0, b_a_up, b_g_up, b_kk, b_ka,
                        b_rk, b_ln_g, b_ln_b)
    yl = jnp.concatenate([spatial_gate(pl, a_ws, a_bs, a_gv), bl], axis=-1) @ w_out
    yc = jnp.concatenate([spatial_gate(pc, a_ws, a_bs, a_gv), bc], axis=-1) @ w_out if need_ctx else None
    return yc, yl

def mlstm_prep(p, conv, conv_b, wq, wk, wv, bi, bf):
    bn, t, _ = p.shape
    xm, z = p[..., :C_WIDTH], p[..., C_WIDTH:2 * C_WIDTH]
    gates = p[..., 2 * C_WIDTH:].reshape(bn, t, 2, 2, C_HEADS)
    xcv = jax.nn.silu(dwconv1d(xm, conv) + conv_b)
    def blockdiag(u, w):
        return jnp.einsum('btgi,gio->btgo', u.reshape(bn, t, C_WIDTH // QKV_BLOCK, QKV_BLOCK), w).reshape(bn, t, C_WIDTH)
    def heads(u):
        return u.reshape(bn, t, C_HEADS, C_HEAD).transpose(0, 2, 1, 3)
    q = heads(blockdiag(xcv, wq))
    k = heads(blockdiag(xcv, wk)) * (C_HEAD ** -0.5)
    v = heads(blockdiag(xm, wv))
    logi = jnp.transpose(gates[:, :, 0] + bi, (2, 0, 3, 1))
    logf = jax.nn.log_sigmoid(jnp.transpose(gates[:, :, 1] + bf, (2, 0, 3, 1)))
    return q, k, v, logi, logf, xcv, z

def mlstm_dir_inputs(prep, d):
    q, k, v, logi, logf = prep[:5]
    seq = (q, k, v, logi[d], logf[d])
    return tuple(u[:, :, ::-1] for u in seq) if d == 1 else seq

def mlstm_chunk_scan(q, k, v, logi, logf, state):
    bn, nh, t, dh = q.shape
    nc = t // C_CHUNK
    dt = q.dtype
    tril = jnp.tril(jnp.ones((C_CHUNK, C_CHUNK), dtype=bool))
    def chunks(u):
        u = u.astype(jnp.float32)
        return jnp.moveaxis(u.reshape((bn, nh, nc, C_CHUNK) + u.shape[3:]), 2, 0)
    def step(carry, inp):
        cmat, nvec, m = carry
        qc, kc, vc, li, lf = inp
        b = jnp.cumsum(lf, axis=-1)
        logd = jnp.where(tril, b[..., :, None] - b[..., None, :] + li[..., None, :], -jnp.inf)
        inter = b + m[..., None]
        m_row = jnp.maximum(inter, jnp.max(logd, axis=-1))
        s = jnp.einsum('bhjd,bhsd->bhjs', qc, kc) * jnp.exp(logd - m_row[..., None])
        w_inter = jnp.exp(inter - m_row)
        num = jnp.einsum('bhjs,bhsv->bhjv', s, vc) + w_inter[..., None] * jnp.einsum('bhvd,bhjd->bhjv', cmat, qc)
        den = jnp.sum(s, axis=-1) + w_inter * jnp.einsum('bhd,bhjd->bhj', nvec, qc)
        h = num / jnp.maximum(jnp.abs(den), jnp.exp(-m_row))[..., None]
        b_last = b[..., -1]
        log_in = b_last[..., None] - b + li
        m_new = jnp.maximum(b_last + m, jnp.max(log_in, axis=-1))
        carry_scale = jnp.exp(b_last + m - m_new)
        kw = kc * jnp.exp(log_in - m_new[..., None])[..., None]
        cmat = carry_scale[..., None, None] * cmat + jnp.einsum('bhsv,bhsd->bhvd', vc, kw)
        nvec = carry_scale[..., None] * nvec + jnp.sum(kw, axis=-2)
        return (cmat, nvec, m_new), h
    state, hs = lax.scan(step, state, tuple(chunks(u) for u in (q, k, v, logi, logf)))
    h = jnp.moveaxis(hs, 0, 2).reshape(bn, nh, t, v.shape[-1])
    return h.astype(dt), state

def mlstm_out(h, xcv, z, c_norm, c_skip, w_out):
    bn, nh, t, dh = h.shape
    hn = rmsnorm_2(h.transpose(0, 2, 1, 3), c_norm).reshape(bn, t, C_WIDTH)
    return ((hn + c_skip * xcv) * jax.nn.sigmoid(z)) @ w_out

def mixer_mlstm(hc, hl, need_ctx, w_in, w_out, conv, conv_b, wq, wk, wv, bi, bf, c_norm, c_skip):
    prep_c = mlstm_prep(hc @ w_in, conv, conv_b, wq, wk, wv, bi, bf)
    prep_l = mlstm_prep(hl @ w_in, conv, conv_b, wq, wk, wv, bi, bf)
    bn = hl.shape[0]
    hs_c, hs_l = [], []
    for d in range(2):
        init = (jnp.zeros((bn, C_HEADS, C_HEAD, C_HEAD), jnp.float32),
                jnp.zeros((bn, C_HEADS, C_HEAD), jnp.float32),
                jnp.zeros((bn, C_HEADS), jnp.float32))
        h_c, st = mlstm_chunk_scan(*mlstm_dir_inputs(prep_c, d), init)
        h_l, _ = mlstm_chunk_scan(*mlstm_dir_inputs(prep_l, d), st)
        if d == 1:
            h_c, h_l = h_c[:, :, ::-1], h_l[:, :, ::-1]
        hs_c.append(h_c)
        hs_l.append(h_l)
    yl = mlstm_out(hs_l[0] + hs_l[1], prep_l[5], prep_l[6], c_norm, c_skip, w_out)
    yc = mlstm_out(hs_c[0] + hs_c[1], prep_c[5], prep_c[6], c_norm, c_skip, w_out) if need_ctx else None
    return yc, yl

def second_inputs(seed: int = 0) -> dict:
    key = jax.random.key(seed)
    ks = iter(jax.random.split(key, 64))
    def nrm(shape, s):
        return jax.random.normal(next(ks), shape, jnp.float32) * s
    D = D_MODEL
    return {
        'x': nrm((BATCH, SEQ, D), 1.0),
        'c': nrm((BATCH, D), 1.0),
        'ctx': nrm((BATCH, CTX_LEN, D), 1.0),
        'c_ctx': nrm((D,), 1.0),
        'ada_w': nrm((DEPTH_2, D, 6 * D), D ** -0.5),
        'ada_b': nrm((DEPTH_2, 6 * D), 0.02),
        'norm_mix_pre': 1.0 + nrm((DEPTH_2, D), 0.05),
        'norm_mix_post': 1.0 + nrm((DEPTH_2, D), 0.05),
        'norm_ffn_pre': 1.0 + nrm((DEPTH_2, D), 0.05),
        'norm_ffn_post': 1.0 + nrm((DEPTH_2, D), 0.05),
        'ffn_up': nrm((DEPTH_2, D, 2 * D_FF_2), D ** -0.5),
        'ffn_conv': nrm((DEPTH_2, 3, 3, D_FF_2), 1.0 / 3.0),
        'ffn_conv_b': nrm((DEPTH_2, D_FF_2), 0.02),
        'ffn_down': nrm((DEPTH_2, D_FF_2, D), D_FF_2 ** -0.5),
        'ab_w_in': nrm((N_EVEN, D, AB_IN), D ** -0.5),
        'ab_w_out': nrm((N_EVEN, MIX_W, D), MIX_W ** -0.5),
        'a_ws': nrm((N_EVEN, A_GROUPS, CHUNK, CHUNK), CHUNK ** -0.5),
        'a_bs': 1.0 + nrm((N_EVEN, A_GROUPS, CHUNK), 0.1),
        'a_gv': 1.0 + nrm((N_EVEN, A_GROUPS, A_GDIM), 0.05),
        'b_shift': nrm((N_EVEN, 3, 3 * B_WIDTH), 0.5),
        'b_w0': jnp.linspace(-6.0, -1.0, B_WIDTH, dtype=jnp.float32) + nrm((N_EVEN, 2, B_WIDTH), 0.1),
        'b_w_up': nrm((N_EVEN, 2, DECAY_LORA, B_WIDTH), 0.5 * DECAY_LORA ** -0.5),
        'b_a0': nrm((N_EVEN, 2, B_WIDTH), 0.1),
        'b_a_up': nrm((N_EVEN, 2, AAA_LORA, B_WIDTH), AAA_LORA ** -0.5),
        'b_g_up': nrm((N_EVEN, GATE_LORA, B_WIDTH), GATE_LORA ** -0.5),
        'b_kk': 0.85 + nrm((N_EVEN, B_WIDTH), 0.05),
        'b_ka': 1.0 + nrm((N_EVEN, B_WIDTH), 0.05),
        'b_rk': nrm((N_EVEN, B_HEADS, B_HEAD), 0.1),
        'b_ln_g': 1.0 + nrm((N_EVEN, B_HEADS, B_HEAD), 0.05),
        'b_ln_b': nrm((N_EVEN, B_HEADS, B_HEAD), 0.02),
        'c_w_in': nrm((N_ODD, D, C_IN), D ** -0.5),
        'c_w_out': nrm((N_ODD, C_WIDTH, D), C_WIDTH ** -0.5),
        'c_conv': nrm((N_ODD, 3, C_WIDTH), 0.5),
        'c_conv_b': nrm((N_ODD, C_WIDTH), 0.02),
        'c_wq': nrm((N_ODD, C_WIDTH // QKV_BLOCK, QKV_BLOCK, QKV_BLOCK), QKV_BLOCK ** -0.5),
        'c_wk': nrm((N_ODD, C_WIDTH // QKV_BLOCK, QKV_BLOCK, QKV_BLOCK), QKV_BLOCK ** -0.5),
        'c_wv': nrm((N_ODD, C_WIDTH // QKV_BLOCK, QKV_BLOCK, QKV_BLOCK), QKV_BLOCK ** -0.5),
        'c_bi': nrm((N_ODD, 2, C_HEADS), 0.1),
        'c_bf': jnp.linspace(3.0, 6.0, C_HEADS, dtype=jnp.float32) + nrm((N_ODD, 2, C_HEADS), 0.1),
        'c_norm': 1.0 + nrm((N_ODD, C_HEADS, C_HEAD), 0.05),
        'c_skip': 1.0 + nrm((N_ODD, C_WIDTH), 0.05),
    }

def second_block(x, c, ctx, c_ctx, ada_w, ada_b, norm_mix_pre, norm_mix_post, norm_ffn_pre, norm_ffn_post,
              ffn_up, ffn_conv, ffn_conv_b, ffn_down, ab_w_in, ab_w_out, a_ws, a_bs, a_gv, b_shift, b_w0,
              b_w_up, b_a0, b_a_up, b_g_up, b_kk, b_ka, b_rk, b_ln_g, b_ln_b, c_w_in, c_w_out, c_conv,
              c_conv_b, c_wq, c_wk, c_wv, c_bi, c_bf, c_norm, c_skip):
    rows = x.shape[1] // GRID_W
    xl, xc = x, ctx
    for layer in range(DEPTH_2):
        need_ctx = layer < DEPTH_2 - 1
        i = layer // 2
        ml = ada_mod(c, ada_w[layer], ada_b[layer])
        mc = ada_mod(c_ctx, ada_w[layer], ada_b[layer])
        hl = modulate(rmsnorm_2(xl, norm_mix_pre[layer]), ml[0], ml[1])
        hc = modulate(rmsnorm_2(xc, norm_mix_pre[layer]), mc[0], mc[1])
        if layer % 2 == 0:
            yc, yl = mixer_ab(hc, hl, need_ctx, ab_w_in[i], ab_w_out[i], a_ws[i], a_bs[i], a_gv[i],
                              b_shift[i], b_w0[i], b_w_up[i], b_a0[i], b_a_up[i], b_g_up[i], b_kk[i],
                              b_ka[i], b_rk[i], b_ln_g[i], b_ln_b[i])
        else:
            yc, yl = mixer_mlstm(hc, hl, need_ctx, c_w_in[i], c_w_out[i], c_conv[i], c_conv_b[i],
                                 c_wq[i], c_wk[i], c_wv[i], c_bi[i], c_bf[i], c_norm[i], c_skip[i])
        xl = xl + ml[2] * rmsnorm_2(yl, norm_mix_post[layer])
        hl = modulate(rmsnorm_2(xl, norm_ffn_pre[layer]), ml[3], ml[4])
        xl = xl + ml[5] * rmsnorm_2(conv_ffn(hl, ffn_up[layer], ffn_conv[layer], ffn_conv_b[layer],
                                           ffn_down[layer], rows), norm_ffn_post[layer])
        if need_ctx:
            xc = xc + mc[2] * rmsnorm_2(yc, norm_mix_post[layer])
            hc = modulate(rmsnorm_2(xc, norm_ffn_pre[layer]), mc[3], mc[4])
            xc = xc + mc[5] * rmsnorm_2(conv_ffn(hc, ffn_up[layer], ffn_conv[layer], ffn_conv_b[layer],
                                               ffn_down[layer], None), norm_ffn_post[layer])
    return xl


_first_inputs = second_inputs


def second_inputs(seed=0):
    import zlib

    import numpy as np

    out = dict(_first_inputs(seed))
    spreads = {}
    factors = {'ffn_conv_b': 4.47,
     'a_gv': 2.835,
     'b_w_up': 2.8,
     'b_a0': 5.301,
     'b_ln_g': 3.787,
     'b_ln_b': 24.932,
     'c_conv_b': 3.583,
     'c_bi': 64.0,
     'c_norm': 10.528,
     'c_skip': 15.883,
     'a_bs': 3.361}
    for name, (base, spread) in spreads.items():
        noise = np.random.default_rng([zlib.crc32(name.encode()), seed]).standard_normal(out[name].shape)
        drawn = base * np.exp(spread * noise) if base else spread * noise
        out[name] = __import__('jax').numpy.asarray(drawn.astype(out[name].dtype))
    for name, factor in factors.items():
        out[name] = (out[name] * factor).astype(out[name].dtype)
    return out


_narrow_inputs = second_inputs


def second_inputs(seed=0):
    out = dict(_narrow_inputs(seed))
    wider = {'a_gv': 3.5, 'b_ln_g': 3.59, 'c_norm': 3.95, 'c_skip': 4.02}
    for name, times in wider.items():
        mean = out[name].mean()
        out[name] = (mean + times * (out[name] - mean)).astype(out[name].dtype)
    return out


def setup_inputs(seed=0):
    out = dict(first_inputs(seed))
    for name, value in second_inputs(seed + 1).items():
        if name != "x":
            out[name + "_2"] = value
    return out


def reference(
    x, norm1_w, w_in, conv_w, conv_b, dt_bias, a_log, d_skip, ssm_norm_w, w_attn_branch,
    w_ssm_branch, w_out, norm2_w, w_ffn_in, w_ffn_out, rel_bias, final_norm_w, c_2, ctx_2,
    c_ctx_2, ada_w_2, ada_b_2, norm_mix_pre_2, norm_mix_post_2, norm_ffn_pre_2, norm_ffn_post_2,
    ffn_up_2, ffn_conv_2, ffn_conv_b_2, ffn_down_2, ab_w_in_2, ab_w_out_2, a_ws_2, a_bs_2,
    a_gv_2, b_shift_2, b_w0_2, b_w_up_2, b_a0_2, b_a_up_2, b_g_up_2, b_kk_2, b_ka_2, b_rk_2,
    b_ln_g_2, b_ln_b_2, c_w_in_2, c_w_out_2, c_conv_2, c_conv_b_2, c_wq_2, c_wk_2, c_wv_2,
    c_bi_2, c_bf_2, c_norm_2, c_skip_2,
):
    x = first_block(
        x, norm1_w, w_in, conv_w, conv_b, dt_bias, a_log, d_skip, ssm_norm_w, w_attn_branch,
        w_ssm_branch, w_out, norm2_w, w_ffn_in, w_ffn_out, rel_bias, final_norm_w,
    )
    return second_block(
        x, c_2, ctx_2, c_ctx_2, ada_w_2, ada_b_2, norm_mix_pre_2, norm_mix_post_2,
        norm_ffn_pre_2, norm_ffn_post_2, ffn_up_2, ffn_conv_2, ffn_conv_b_2, ffn_down_2,
        ab_w_in_2, ab_w_out_2, a_ws_2, a_bs_2, a_gv_2, b_shift_2, b_w0_2, b_w_up_2, b_a0_2,
        b_a_up_2, b_g_up_2, b_kk_2, b_ka_2, b_rk_2, b_ln_g_2, b_ln_b_2, c_w_in_2, c_w_out_2,
        c_conv_2, c_conv_b_2, c_wq_2, c_wk_2, c_wv_2, c_bi_2, c_bf_2, c_norm_2, c_skip_2,
    )


_drawn_inputs = setup_inputs


def setup_inputs(seed=0):
    import zlib

    import numpy as np

    out = dict(_drawn_inputs(seed))
    spreads = {}
    factors = {'conv_b': 2.987, 'ssm_norm_w': 4.274, 'norm2_w': 3.431}
    for name, (base, spread) in spreads.items():
        noise = np.random.default_rng([zlib.crc32(name.encode()), seed]).standard_normal(out[name].shape)
        drawn = base * np.exp(spread * noise) if base else spread * noise
        out[name] = __import__('jax').numpy.asarray(drawn.astype(out[name].dtype))
    for name, factor in factors.items():
        out[name] = (out[name] * factor).astype(out[name].dtype)
    return out
```

```python
from contextlib import ExitStack

import concourse.bass as bass
from concourse import mybir

P = 128
F32 = mybir.dt.float32
ALU = mybir.AluOpType
ACT = mybir.ActivationFunctionType
AX = mybir.AxisListType
NEG = -1e30

D, SEQ, CTX = 1024, 512, 256
KT = D // P
ALLTOK = CTX + SEQ
NCH = SEQ // P
EPS = 1e-6


def broadcast_rows(row, n):
    return bass.AP(tensor=row.tensor, offset=row.offset, ap=[[0, P], [1, n]])


def middle(ap, n):
    return bass.AP(tensor=ap.tensor, offset=ap.offset, ap=[ap.ap[0], [0, n], ap.ap[1]])


def last(ap, n):
    return bass.AP(tensor=ap.tensor, offset=ap.offset, ap=[ap.ap[0], ap.ap[1], [0, n]])


class Stage:

    number = [0]

    def __init__(self, nc, name):
        self.nc, self.name, self.cs, self.sems = nc, name, ExitStack(), []

    def __enter__(self):
        self.cs.__enter__()
        return self

    def __exit__(self, *e):
        self.cs.__exit__(*e)
        if self.sems:
            self.nc.clear_and_free_semaphores(self.sems)

    def sb(self, name, shape, dt=F32):
        return self.cs.enter_context(self.nc.sbuf_tensor(f"{self.name}_{name}", shape, dt))

    def pb(self, name, width=512):
        return self.cs.enter_context(self.nc.psum_tensor(f"{self.name}_{name}", [P, width], F32))

    def sem(self, name):
        free = list(self.nc.free_semaphores)
        later = [n for n in free if n > Stage.number[0]]
        Stage.number[0] = min(later or free)
        self.sems.append(self.nc.alloc_semaphore(f"{self.name}_{name}", num=Stage.number[0]))
        return self.sems[-1]


def project(nc, name, w, parts, cols, steps, unroll, psum_sets=None, temps=None, first=0, count=None):
    M = (w.shape[0] - first) if count is None else count
    width = w.shape[2]
    per = len(parts) * len(cols)
    sets = psum_sets or max(s for s in range(1, unroll + 1) if unroll % s == 0 and s * per <= 8)
    assert M % unroll == 0 and unroll % sets == 0, (name, M, unroll, sets)
    groups = M // unroll
    with Stage(nc, name) as st:
        ring = st.sb("ring", [P, unroll, width])
        banks = [[[st.pb(f"bank{s}_{q}_{c}") for c in range(len(cols))] for q in range(len(parts))]
                 for s in range(sets)]
        tmp = temps(st, sets) if temps else None
        loaded = [st.sem(f"weights_loaded{b}") for b in range(unroll)]
        product_ready = st.sem("product_ready")
        psum_free = st.sem("psum_free")
        done = [st.sem(f"step_done{s}") for s in range(len(steps) - 1)]

        block = st.cs.enter_context(nc.Block())

        @block.sync
        def _(sp):
            for b in range(unroll):
                sp.dma_start(ring[:, b, :], w[first + b]).then_inc(loaded[b], 16)
            if groups > 1:
                with sp.Fori(0, groups - 1) as i:
                    for b in range(unroll):
                        sp.wait_ge(product_ready, i * unroll + (b + 1))
                        sp.dma_start(ring[:, b, :], w[i * unroll + (unroll + b + first)]).then_inc(loaded[b], 16)

        @block.tensor
        def _(pe):
            with pe.Fori(0, groups) as i:
                for b in range(unroll):
                    pe.wait_ge(loaded[b], i * 16 + 16)
                    pe.wait_ge(psum_free, i * unroll + (b + 1))
                    for q, moving in enumerate(parts):
                        at = sum(len(x) for x in parts[:q])
                        for k, x in enumerate(moving):
                            for c, (t0, tw) in enumerate(cols):
                                mm = pe.matmul(banks[b % sets][q][c][:, 0:tw],
                                               ring[:, b, (at + k) * P:(at + k + 1) * P],
                                               x[:, t0:t0 + tw], start=(k == 0), stop=(k == len(moving) - 1))
                    mm.then_inc(product_ready, 1)

        def engine_program(which):
            def program(e):
                if steps[-1][0] == which:
                    e.nop().then_inc(psum_free, sets)
                with e.Fori(0, groups) as i:
                    for b in range(unroll):
                        for s, (who, f) in enumerate(steps):
                            if who != which:
                                continue
                            e.wait_ge(product_ready if s == 0 else done[s - 1], i * unroll + (b + 1))
                            ins = f(e, i * unroll + (b + first), b, banks[b % sets], tmp and tmp[b % sets])
                            ins.then_inc(psum_free if s == len(steps) - 1 else done[s], 1)
            return program

        if any(s[0] == "scalar" for s in steps):
            block.scalar(engine_program("scalar"))
        if any(s[0] == "vector" for s in steps):
            block.vector(engine_program("vector"))
        if any(s[0] == "gpsimd" for s in steps):
            block.gpsimd(engine_program("gpsimd"))


def rms_norm(nc, name, K, T, x, y, one, eps, gain=None, shift=None, residual=None):
    with Stage(nc, name) as st:
        sq = st.sb("squares", [P, 2, T])
        rstd = st.sb("rstd", [P, T])
        tmp = st.sb("scaled", [P, 2, T])
        total = st.pb("total")
        squared, used, rooted, scaled = (st.sem(n) for n in ("squared", "square_used", "rooted", "scaled"))
        block = st.cs.enter_context(nc.Block())

        @block.scalar
        def _(act):
            for k in range(K):
                if k >= 2:
                    act.wait_ge(used, k - 1)
                act.activation(sq[:, k % 2, :], x(k), ACT.Square).then_inc(squared, 1)
            act.wait_ge(used, K)
            act.activation(rstd[:], total[:, 0:T], ACT.Sqrt, bias=eps, scale=1.0 / (K * P)).then_inc(rooted, 1)
            if shift is not None:
                for k in range(K):
                    act.wait_ge(scaled, k + 1)
                    act.activation(y(k), y(k), ACT.Identity, bias=shift(k))

        @block.tensor
        def _(pe):
            for k in range(K):
                pe.wait_ge(squared, k + 1)
                mm = pe.matmul(total[:, 0:T], one[:], sq[:, k % 2, :], start=(k == 0), stop=(k == K - 1))
                mm.then_inc(used, 1)

        @block.vector
        def _(dve):
            dve.wait_ge(rooted, 1)
            dve.reciprocal(rstd[:], rstd[:])
            dve.drain()
            for k in range(K):
                if residual is None:
                    dve.scalar_tensor_tensor(out=y(k), in0=x(k), scalar=gain(k), in1=rstd[:],
                                             op0=ALU.mult, op1=ALU.mult).then_inc(scaled, 1)
                else:
                    dve.scalar_tensor_tensor(out=tmp[:, k % 2, :], in0=x(k), scalar=gain(k), in1=rstd[:],
                                             op0=ALU.mult, op1=ALU.mult)
                    dve.drain()
                    dve.tensor_tensor(residual(k), residual(k), tmp[:, k % 2, :], ALU.add)


HEADS, DH = 8, 64
DIL = 4
TABLES = 2 * DIL - 1 + 2


def bias_tables(nc, name, rel, onehot, neg_row, scratch, flip, table):
    with Stage(nc, name) as st:
        rel_sb = st.sb("rel", [33, 3 * HEADS])
        hot = st.sb("hot", [33, TABLES, 2 * P])
        line = st.sb("line", [HEADS, TABLES, 2 * P])
        shifted = st.sb("shifted", [P, 2, TABLES * P])
        banks = [st.pb(f"bank{i}") for i in range(TABLES // 2 + 1)]
        turned = [st.pb(f"turned{i}") for i in range(3)]
        loaded, made, copied, kept, flipped, taken = (
            st.sem(n) for n in ("loaded", "made", "copied", "kept", "flipped", "taken"))
        spread = [st.sem(f"spread{i}") for i in range(2)]
        block = st.cs.enter_context(nc.Block())
        W = TABLES * P // 3
        assert W <= 512

        @block.sync
        def _(sp):
            sp.dma_start(rel_sb[0:32, :], rel).then_inc(loaded, 16)
            sp.dma_start(rel_sb[32:33, :], neg_row).then_inc(loaded, 16)
            sp.dma_start(hot[:], onehot).then_inc(loaded, 16)
            sp.wait_ge(copied, TABLES)
            sp.dma_start(scratch, line[:]).then_inc(kept, 16)
            sp.wait_ge(kept, 16)
            for h in range(HEADS):
                if h >= 2:
                    sp.wait_ge(flipped, 3 * (h - 1))
                src = bass.AP(tensor=scratch.tensor, offset=scratch.offset + h * TABLES * 2 * P,
                              ap=[[1, P], [2 * P, TABLES], [1, P]])
                sp.dma_start(shifted[:, h % 2, :].rearrange("p (t n) -> p t n", t=TABLES), src).then_inc(spread[h % 2], 16)

        @block.tensor
        def _(pe):
            pe.wait_ge(loaded, 48)
            for t in range(TABLES):
                g = max(0, t - (TABLES - 3))
                pe.matmul(banks[t // 2][0:HEADS, (t % 2) * 2 * P:(t % 2 + 1) * 2 * P],
                          rel_sb[:, g * HEADS:(g + 1) * HEADS], hot[:, t, :], start=True, stop=True).then_inc(made, 1)
            for h in range(HEADS):
                pe.wait_ge(spread[h % 2], 16 * (h // 2 + 1))
                for i in range(3):
                    if h >= 1:
                        pe.wait_ge(taken, 3 * (h - 1) + i + 1)
                    pe.matmul(turned[i][:, 0:W], flip[:], shifted[:, h % 2, i * W:(i + 1) * W], start=True, stop=True).then_inc(flipped, 1)

        @block.vector
        def _(dve):
            for t in range(TABLES):
                dve.wait_ge(made, min(TABLES, t // 2 * 2 + 2))
                dve.tensor_copy(line[:, t, :], banks[t // 2][0:HEADS, (t % 2) * 2 * P:(t % 2 + 1) * 2 * P]).then_inc(copied, 1)
            for h in range(HEADS):
                for i in range(3):
                    dve.wait_ge(flipped, 3 * h + i + 1)
                    dve.tensor_copy(table[:, h, :, :].rearrange("p t n -> p (t n)")[:, i * W:(i + 1) * W], turned[i][:, 0:W]).then_inc(taken, 1)


def attention(nc, name, q, k, v, table, out, ident):
    units = [(h, r) for h in range(HEADS) for r in range(DIL)]
    NU, NK = len(units), SEQ + 2 * P
    with Stage(nc, name) as st:
        logits = st.sb("logits", [P, 2, NK])
        probs = st.sb("probs", [P, 2, NK])
        probs_t = st.sb("probs_t", [P, 2, NK])
        negmax = st.sb("negmax", [P, NU])
        den = st.sb("den", [P, NU])
        rden = st.sb("rden", [P, NU])
        score = [st.pb(f"score{i}", 1024) for i in range(2)]
        turned = st.pb("turned", 1024)
        outs = [st.pb(f"outs{i}") for i in range(2)]
        scored, biased, maxed, exped, normed, transposed, copied, mixed, stored = (
            st.sem(n) for n in ("scored", "biased", "maxed", "exped", "normed", "transposed", "copied", "mixed", "stored"))
        block = st.cs.enter_context(nc.Block())

        @block.tensor
        def _(pe):
            def scores(n):
                h, r = units[n]
                p0, t = DH * (h % 2), h // 2
                if n >= 2:
                    pe.wait_ge(biased, n - 1)
                for g in range(3):
                    qg = q[p0:p0 + DH, 4 * g + t, r * P:(r + 1) * P]
                    kg = k[p0:p0 + DH, 4 * g + t, :] if g == 0 else k[p0:p0 + DH, 4 * g + t, r * P:(r + 1) * P]
                    o = 0 if g == 0 else SEQ + (g - 1) * P
                    mm = pe.matmul(score[n % 2][:, o:o + (SEQ if g == 0 else P)], qg, kg, start=True, stop=True)
                mm.then_inc(scored, 1)

            def mix(n):
                h, r = units[n]
                pe.wait_ge(normed, n + 1)
                if n >= 1:
                    pe.wait_ge(copied, n)
                for t in range(NK // P):
                    mm = pe.transpose(turned[:, t * P:(t + 1) * P], probs[:, n % 2, t * P:(t + 1) * P], ident[:])
                mm.then_inc(transposed, 1)
                pe.wait_ge(copied, n + 1)
                pair = h // 2
                if h % 2 == 0 and r == 0 and pair >= 2:
                    pe.wait_ge(stored, pair - 1)
                for t in range(NK // P):
                    g = max(0, t - 3)
                    row = t if g == 0 else r
                    mm = pe.matmul(outs[pair % 2][DH * (h % 2):DH * (h % 2) + DH, r * P:(r + 1) * P],
                                   v[:, row, (g * HEADS + h) * DH:(g * HEADS + h + 1) * DH],
                                   probs_t[:, n % 2, t * P:(t + 1) * P], start=(t == 0), stop=(t == NK // P - 1))
                mm.then_inc(mixed, 1)

            scores(0)
            for n in range(NU):
                if n + 1 < NU:
                    scores(n + 1)
                mix(n)

        @block.vector
        def _(dve):
            def bias(n):
                h, r = units[n]
                dve.wait_ge(scored, n + 1)
                if n >= 2:
                    dve.wait_ge(exped, n - 1)
                dve.scalar_tensor_tensor(out=logits[:, n % 2, 0:SEQ], in0=score[n % 2][:, 0:SEQ], scalar=DH ** -0.5,
                                         in1=table[:, h, DIL - 1 - r:2 * DIL - 1 - r, :].rearrange("p a b -> p (a b)"),
                                         op0=ALU.mult, op1=ALU.add)
                dve.scalar_tensor_tensor(out=logits[:, n % 2, SEQ:NK], in0=score[n % 2][:, SEQ:NK], scalar=DH ** -0.5,
                                         in1=table[:, h, 2 * DIL - 1:TABLES, :].rearrange("p a b -> p (a b)"),
                                         op0=ALU.mult, op1=ALU.add).then_inc(biased, 1)
                dve.drain()
                dve.tensor_reduce(negmax[:, n:n + 1], logits[:, n % 2, :], AX.X, ALU.max, negate=True).then_inc(maxed, 1)

            def normalise(n):
                dve.wait_ge(exped, n + 1)
                dve.reciprocal(rden[:, n:n + 1], den[:, n:n + 1])
                dve.drain()
                dve.tensor_scalar(probs[:, n % 2, :], probs[:, n % 2, :], rden[:, n:n + 1], None, ALU.mult).then_inc(normed, 1)

            for n in range(NU + 1):
                if n < NU:
                    bias(n)
                if n >= 1:
                    normalise(n - 1)

        @block.scalar
        def _(act):
            def exp(n):
                act.wait_ge(maxed, n + 1)
                if n >= 2:
                    act.wait_ge(transposed, n - 1)
                act.activation(probs[:, n % 2, :], logits[:, n % 2, :], ACT.Exp, bias=negmax[:, n:n + 1],
                               accum_out=den[:, n:n + 1]).then_inc(exped, 1)

            def copy(n):
                act.wait_ge(transposed, n + 1)
                if n >= 2:
                    act.wait_ge(mixed, n - 1)
                act.activation(probs_t[:, n % 2, 0:SEQ], turned[:, 0:SEQ], ACT.Copy)
                act.activation(probs_t[:, n % 2, SEQ:NK], turned[:, SEQ:NK], ACT.Copy).then_inc(copied, 1)
                if n % (2 * DIL) == 2 * DIL - 1:
                    pair = n // (2 * DIL)
                    act.wait_ge(mixed, n + 1)
                    act.activation(out[:, pair, :].rearrange("p (i r) -> p r i", r=DIL),
                                   outs[pair % 2][:].rearrange("p (r i) -> p r i", r=DIL), ACT.Copy).then_inc(stored, 1)

            for n in range(NU + 1):
                if n < NU:
                    exp(n)
                if n >= 1:
                    copy(n - 1)


def token_major(nc, name, w, src, rows, steps, temps=None):
    N, width = w.shape[0], w.shape[2] // len(src)
    R = len(rows)
    with Stage(nc, name) as st:
        ring = st.sb("ring", [P, 2, w.shape[2]])
        banks = [st.pb(f"bank{i}") for i in range(4)]
        tmp = temps(st) if temps else None
        loaded = [st.sem(f"weights_loaded{b}") for b in range(2)]
        product_ready, psum_free = st.sem("product_ready"), st.sem("psum_free")
        done = [st.sem(f"step_done{s}") for s in range(len(steps) - 1)]
        block = st.cs.enter_context(nc.Block())

        @block.sync
        def _(sp):
            for n in range(N):
                if n >= 2:
                    sp.wait_ge(product_ready, (n - 1) * R)
                sp.dma_start(ring[:, n % 2, :], w[n]).then_inc(loaded[n % 2], 16)

        @block.tensor
        def _(pe):
            for n in range(N):
                pe.wait_ge(loaded[n % 2], 16 * (n // 2 + 1))
                for r, row in enumerate(rows):
                    u = n * R + r
                    if u >= 4:
                        pe.wait_ge(psum_free, u - 3)
                    for k, x in enumerate(src):
                        mm = pe.matmul(banks[u % 4][:, 0:width], x[:, row], ring[:, n % 2, k * width:(k + 1) * width],
                                       start=(k == 0), stop=(k == len(src) - 1))
                    mm.then_inc(product_ready, 1)

        def engine_program(which):
            def program(e):
                for u in range(N * R):
                    for s, (who, f) in enumerate(steps):
                        if who == which:
                            e.wait_ge(product_ready if s == 0 else done[s - 1], u + 1)
                            ins = f(e, u // R, u % R, banks[u % 4][:, 0:width], tmp and tmp[u % 2])
                            ins.then_inc(psum_free if s == len(steps) - 1 else done[s], 1)
            return program

        for which, register in (("scalar", block.scalar), ("vector", block.vector)):
            if any(s[0] == which for s in steps):
                register(engine_program(which))


GROUPS, GH, SHD, NSTATE = 4, 8, 64, 128
GW = GH * SHD
SH = GROUPS * GH


def ssd_decays(nc, name, d, dt_raw, dt_bias, a_log, d_skip, one, upper):
    CH = NCH * SH
    with Stage(nc, name) as st:
        bias_sb, alog_sb = (st.sb(n, [P, SH]) for n in ("dt_bias", "a_log"))
        raw, soft = (st.sb(n, [P, CH]) for n in ("raw", "soft"))
        la_ps, last_ps = st.pb("la"), st.pb("last")
        loaded, absd, softened, raised, cumd, prepared = (
            st.sem(n) for n in ("loaded", "absd", "softened", "raised", "cumd", "prepared"))
        block = st.cs.enter_context(nc.Block())

        @block.sync
        def _(sp):
            for dst, src in ((bias_sb, dt_bias), (alog_sb, a_log), (d.skip, d_skip)):
                sp.dma_start(dst[:], broadcast_rows(src, SH)).then_inc(loaded, 16)

        @block.vector
        def _(dve):
            dve.wait_ge(loaded, 48)
            dve.tensor_tensor(raw[:].rearrange("p (c h) -> p c h", c=NCH), dt_raw[:],
                              middle(bias_sb[:], NCH), ALU.add).then_inc(absd, 1)
            dve.wait_ge(softened, 1)
            dve.scalar_tensor_tensor(out=d.dt[:], in0=raw[:], scalar=0.0, in1=soft[:], op0=ALU.max, op1=ALU.add)
            dve.drain()
            dve.scalar_tensor_tensor(out=d.dta[:].rearrange("p (c h) -> p c h", c=NCH),
                                     in0=d.dt[:].rearrange("p (c h) -> p c h", c=NCH), scalar=-1.0,
                                     in1=middle(alog_sb[:], NCH), op0=ALU.mult, op1=ALU.mult).then_inc(raised, 1)
            dve.wait_ge(cumd, 1)
            dve.tensor_scalar(d.negla[:], la_ps[:, 0:CH], -1.0, None, ALU.mult)
            dve.drain()
            dve.tensor_tensor(raw[:], last_ps[:, 0:CH], d.negla[:], ALU.add).then_inc(prepared, 1)
            dve.wait_ge(softened, 2)
            dve.tensor_tensor(d.toend[:], d.toend[:], d.dt[:], ALU.mult)

        @block.scalar
        def _(act):
            act.wait_ge(loaded, 48)
            act.activation(alog_sb[:], alog_sb[:], ACT.Exp)
            act.wait_ge(absd, 1)
            act.activation(soft[:], raw[:], ACT.Abs)
            act.drain()
            act.activation(soft[:], soft[:], ACT.Exp, scale=-1.0)
            act.drain()
            act.activation(soft[:], soft[:], ACT.Ln, bias=one[:, 0:1]).then_inc(softened, 1)
            act.wait_ge(prepared, 1)
            act.activation(d.expla[:], la_ps[:, 0:CH], ACT.Exp)
            act.activation(d.elast[:], last_ps[:, 0:CH], ACT.Exp)
            act.activation(d.toend[:], raw[:], ACT.Exp).then_inc(softened, 1)

        @block.tensor
        def _(pe):
            pe.wait_ge(raised, 1)
            pe.matmul(la_ps[:, 0:CH], upper[:], d.dta[:], start=True, stop=True)
            pe.matmul(last_ps[:, 0:CH], one[:], d.dta[:], start=True, stop=True).then_inc(cumd, 1)


def ssd_scan(nc, name, d, xbc, z, norm_w, out, ident, upper, neg_lower, eps):
    units = [(c, g) for c in range(NCH) for g in range(GROUPS)]
    NU = len(units)
    BM, CM = SH * SHD // P, SH * SHD // P + GROUPS
    TPG = GW // P
    with Stage(nc, name) as st:
        state = st.sb("state", [P, GROUPS, GW])
        xtok = st.sb("xtok", [P, 2, GW])
        xend = st.sb("xend", [P, GW])
        btok = st.sb("btok", [P, 2, P])
        cbt = st.sb("cbt", [P, P])
        decay = st.sb("decay", [P, GH, P])
        mix = st.sb("mix", [P, GH, P])
        y, t1 = st.sb("y", [P, GW]), st.sb("t1", [P, GW])
        sq = st.sb("sq", [P, GW])
        ss, rstd = st.sb("ss", [P, NU]), st.sb("rstd", [P, NU])
        xturn, bturn, la0, la1, yin, yst, upd, yturn = (
            st.pb(n) for n in ("xturn", "bturn", "la0", "la1", "yin", "yst", "upd", "yturn"))
        las = (la0, la1)
        names = ("turned", "tokens", "spread", "decayed", "mixed", "ended", "produced", "gated", "squared",
                 "rooted", "normed", "turned_back", "stored", "stated")
        (turned, tokens, spread, decayed, mixed, ended, produced, gated, squared,
         rooted, normed, turned_back, stored, stated) = (st.sem(n) for n in names)
        block = st.cs.enter_context(nc.Block())

        @block.tensor
        def _(pe):
            for n, (c, g) in enumerate(units):
                ts = slice(c * P, (c + 1) * P)
                if n >= 1:
                    pe.wait_ge(tokens, n)
                    pe.wait_ge(mixed, n)
                    pe.wait_ge(decayed, n)
                for t in range(TPG):
                    pe.transpose(xturn[:, t * P:(t + 1) * P], xbc[:, TPG * g + t, ts], ident[:])
                pe.transpose(bturn[:, 0:P], xbc[:, BM + g, ts], ident[:])
                pe.matmul(bturn[:, P:2 * P], xbc[:, BM + g, ts], xbc[:, CM + g, ts], start=True, stop=True).then_inc(turned, 1)
                for h in range(GH):
                    bank = las[h // 4][:, (h % 4) * P:(h % 4 + 1) * P]
                    col = d.dta[:, c * SH + g * GH + h:c * SH + g * GH + h + 1]
                    pe.matmul(bank, col.to_broadcast([P, P]), upper[:], start=True, stop=False)
                    mm = pe.matmul(bank, ident[:], neg_lower[:], start=False, stop=True)
                mm.then_inc(spread, 1)
                if n >= 1:
                    pe.wait_ge(gated, n)
                    pe.wait_ge(stated, n)
                pe.wait_ge(mixed, n + 1)
                for h in range(GH):
                    pe.matmul(yin[:, h * SHD:(h + 1) * SHD], mix[:, h, :], xtok[:, n % 2, h * SHD:(h + 1) * SHD],
                              start=True, stop=True)
                if c >= 1:
                    pe.matmul(yst[:], xbc[:, CM + g, ts], state[:, g, :], start=True, stop=True)
                pe.wait_ge(ended, n + 1)
                pe.matmul(upd[:], btok[:, n % 2, :], xend[:], start=True, stop=True).then_inc(produced, 1)
                pe.wait_ge(normed, n + 1)
                if n >= 1:
                    pe.wait_ge(stored, n)
                for t in range(TPG):
                    mm = pe.transpose(yturn[:, t * P:(t + 1) * P], y[:, t * P:(t + 1) * P], ident[:])
                mm.then_inc(turned_back, 1)

        @block.scalar
        def _(act):
            for n, (c, g) in enumerate(units):
                act.wait_ge(turned, n + 1)
                if n >= 2:
                    act.wait_ge(produced, n - 1)
                act.activation(xtok[:, n % 2, :], xturn[:], ACT.Copy)
                act.activation(btok[:, n % 2, :], bturn[:, 0:P], ACT.Copy).then_inc(tokens, 1)
                act.wait_ge(spread, n + 1)
                if n >= 1:
                    act.wait_ge(mixed, n)
                for h in range(GH):
                    col = c * SH + g * GH + h
                    ins = act.activation(decay[:, h, :], las[h // 4][:, (h % 4) * P:(h % 4 + 1) * P], ACT.Exp,
                                         bias=d.negla[:, col:col + 1])
                ins.then_inc(decayed, 1)
                act.wait_ge(gated, n + 1)
                act.activation(sq[:], t1[:], ACT.Square, accum_out=ss[:, n:n + 1]).then_inc(squared, 1)
                act.drain()
                act.activation(rstd[:, n:n + 1], ss[:, n:n + 1], ACT.Sqrt, bias=eps, scale=1.0 / GW).then_inc(rooted, 1)
                act.wait_ge(turned_back, n + 1)
                for t in range(TPG):
                    ins = act.activation(out[:, TPG * g + t, c * P:(c + 1) * P], yturn[:, t * P:(t + 1) * P], ACT.Copy,
                                         scale=norm_w[:, TPG * g + t:TPG * g + t + 1])
                ins.then_inc(stored, 1)

        @block.vector
        def _(dve):
            dve.memset(state[:], 0.0)
            dve.drain()
            for n, (c, g) in enumerate(units):
                h0 = c * SH + g * GH
                by_head = lambda ap: ap.rearrange("p (h d) -> p h d", h=GH)
                dve.wait_ge(tokens, n + 1)
                dve.wait_ge(decayed, n + 1)
                for h in range(GH):
                    ins = dve.scalar_tensor_tensor(out=mix[:, h, :], in0=decay[:, h, :], scalar=d.dt[:, h0 + h:h0 + h + 1],
                                                   in1=bturn[:, P:2 * P], op0=ALU.mult, op1=ALU.mult)
                ins.then_inc(mixed, 1)
                dve.tensor_tensor(by_head(xend[:]), by_head(xtok[:, n % 2, :]), last(d.toend[:, h0:h0 + GH], SHD),
                                  ALU.mult).then_inc(ended, 1)
                dve.wait_ge(produced, n + 1)
                sg = by_head(state[:, g, :])
                if c >= 1:
                    dve.tensor_tensor(by_head(t1[:]), by_head(yst[:]), last(d.expla[:, h0:h0 + GH], SHD), ALU.mult)
                    dve.tensor_tensor(sg, sg, last(d.elast[:, h0:h0 + GH], SHD), ALU.mult)
                    dve.drain()
                    dve.tensor_tensor(t1[:], t1[:], yin[:], ALU.add)
                else:
                    dve.tensor_copy(t1[:], yin[:])
                dve.tensor_tensor(state[:, g, :], state[:, g, :], upd[:], ALU.add).then_inc(stated, 1)
                if n >= 1:
                    dve.wait_ge(turned_back, n)
                dve.tensor_tensor(by_head(y[:]), by_head(xtok[:, n % 2, :]), last(d.skip[:, g * GH:(g + 1) * GH], SHD), ALU.mult)
                dve.drain()
                dve.tensor_tensor(t1[:], t1[:], y[:], ALU.add)
                dve.drain()
                dve.tensor_tensor(t1[:], t1[:], z[:, c, g * GW:(g + 1) * GW], ALU.mult).then_inc(gated, 1)
                dve.wait_ge(rooted, n + 1)
                dve.reciprocal(rstd[:, n:n + 1], rstd[:, n:n + 1])
                dve.drain()
                dve.tensor_scalar(y[:], t1[:], rstd[:, n:n + 1], None, ALU.mult).then_inc(normed, 1)


class Decays:
    def __init__(self, st):
        self.dt, self.dta, self.negla, self.expla, self.toend, self.elast = (
            st.sb(n, [P, NCH * SH]) for n in ("dt", "dta", "negla", "expla", "toend", "elast"))
        self.skip = st.sb("d_skip", [P, SH])


def load(nc, name, pairs):
    with Stage(nc, name) as st:
        loaded = st.sem("loaded")
        block = st.cs.enter_context(nc.Block())

        @block.sync
        def _(sp):
            for dst, src in pairs:
                sp.dma_start(dst, src).then_inc(loaded, 16)
            sp.wait_ge(loaded, 16 * len(pairs))


def tiles(buf, n, t0=0, t1=None):
    return [buf[:, k, t0:t1] for k in range(n)] if t1 else [buf[:, k, :] for k in range(n)]


def first_block(nc, a, x, c, tap):
    AT, QT = 12, 24
    with Stage(nc, "mixer1") as mixer:
        xn = mixer.sb("xn", [P, KT, SEQ])
        attn = mixer.sb("attn", [P, HEADS * DH // P, SEQ])
        rms_norm(nc, "norm1", KT, SEQ, lambda k: x[:, k, :], lambda k: xn[:, k, :], c.one, c.eps,
                 gain=lambda k: c.norm1[:, k:k + 1])
        tap("xn1", xn)
        with Stage(nc, "att") as st:
            qk = st.sb("qk", [P, QT, SEQ])
            v = st.sb("v", [P, DIL, AT * P])
            table = st.sb("table", [P, HEADS, TABLES, P])
            bias_tables(nc, "bias", a["rel_bias"], a["bias_onehot"], a["neg_row"], a["line_scratch"], c.flip, table)
            tap("table", table)
            project(nc, "qk", a["w_qk"], [tiles(xn, KT)], [(0, SEQ)],
                    [("scalar", lambda e, m, b, banks, t: e.activation(
                        qk[:, m, :].rearrange("p (r i) -> p r i", r=DIL),
                        banks[0][0][:].rearrange("p (i r) -> p r i", r=DIL), ACT.Copy))], unroll=4)
            tap("qk", qk)
            token_major(nc, "v", a["w_v"], tiles(xn, KT), [slice(r, SEQ, DIL) for r in range(DIL)],
                        [("vector", lambda e, n, r, bank, t: e.tensor_copy(v[:, r, n * 512:(n + 1) * 512], bank))])
            attention(nc, "attend", qk[:, 0:AT, :], qk[:, AT:QT, :], v, table, attn, c.ident)
        tap("attn", attn)
        with Stage(nc, "ssm") as st:
            ssm = st.sb("ssm", [P, SH * SHD // P, SEQ])
            with Stage(nc, "ssmin") as s2:
                xbc = s2.sb("xbc", [P, 24, SEQ])
                z = s2.sb("z", [P, NCH, SH * SHD])
                dt_raw = s2.sb("dt_raw", [P, NCH, SH])
                d = Decays(s2)
                rows = [slice(i * P, (i + 1) * P) for i in range(NCH)]
                token_major(nc, "dt", a["w_dt"], tiles(xn, KT), rows,
                            [("vector", lambda e, n, r, bank, t: e.tensor_copy(dt_raw[:, r, :], bank))])
                ssd_decays(nc, "decays", d, dt_raw, a["dt_bias"], a["a_log"], a["d_skip"], c.one, c.upper)

                def conv(e, m, b, banks, acc):
                    bank = banks[0][0]
                    e.tensor_scalar(acc[:], bank[:], c.conv_w[:, m, 3:4], None, ALU.mult)
                    for j in range(1, 4):
                        e.drain()
                        ins = e.scalar_tensor_tensor(out=acc[:, j:SEQ], in0=bank[:, 0:SEQ - j],
                                                     scalar=c.conv_w[:, m, 3 - j:4 - j], in1=acc[:, j:SEQ],
                                                     op0=ALU.mult, op1=ALU.add)
                    return ins

                project(nc, "xbc", a["w_xbc"], [tiles(xn, KT)], [(0, SEQ)],
                        [("vector", conv),
                         ("scalar", lambda e, m, b, banks, acc: e.activation(xbc[:, m, :], acc[:], ACT.Silu,
                                                                            bias=c.conv_b[:, m, :]))],
                        unroll=4, temps=lambda s, n: [s.sb(f"acc{i}", [P, SEQ]) for i in range(n)])
                tap("xbc", xbc)
                token_major(nc, "z", a["w_z"], tiles(xn, KT), rows,
                            [("scalar", lambda e, n, r, bank, t: e.activation(z[:, r, n * 512:(n + 1) * 512], bank, ACT.Silu))])
                ssd_scan(nc, "scan", d, xbc, z, c.ssm_norm, ssm, c.ident, c.upper, c.neg_lower, c.eps)
            tap("ssm", ssm)
            merged = st.sb("merged", [P, KT, SEQ])

            def merge(e, m, b, banks, t):
                e.tensor_tensor(t[0][:], t[0][:], banks[2][0][:], ALU.mult)
                e.tensor_tensor(t[1][:], t[1][:], banks[3][0][:], ALU.mult)
                e.drain()
                return e.tensor_tensor(merged[:, m, :], t[0][:], t[1][:], ALU.add)

            def gates(e, m, b, banks, t):
                e.activation(t[0][:], banks[0][0][:], ACT.Sigmoid)
                return e.activation(t[1][:], banks[1][0][:], ACT.Sigmoid)

            project(nc, "merge", a["w_merge"], [tiles(xn, KT), tiles(xn, KT), tiles(attn, 4), tiles(ssm, 16)],
                    [(0, SEQ)], [("scalar", gates), ("vector", merge)], unroll=2,
                    temps=lambda s, n: [[s.sb(f"gate{i}_{j}", [P, SEQ]) for j in range(2)] for i in range(n)])
            project(nc, "out", a["w_out"], [tiles(merged, KT)], [(0, SEQ)],
                    [("vector", lambda e, m, b, banks, t: e.tensor_tensor(x[:, m, :], x[:, m, :], banks[0][0][:], ALU.add))],
                    unroll=4)
    tap("h1", x)
    with Stage(nc, "ffn1") as st:
        xn = st.sb("xn", [P, KT, SEQ])
        hidden = st.sb("hidden", [P, 22, SEQ])
        rms_norm(nc, "norm2", KT, SEQ, lambda k: x[:, k, :], lambda k: xn[:, k, :], c.one, c.eps,
                 gain=lambda k: c.norm2[:, k:k + 1])
        project(nc, "up", a["w_ffn_in"], [tiles(xn, KT)] * 2, [(0, SEQ)],
                [("scalar", lambda e, m, b, banks, t: e.activation(t[:], banks[0][0][:], ACT.Silu)),
                 ("vector", lambda e, m, b, banks, t: e.tensor_tensor(hidden[:, m, :], t[:], banks[1][0][:], ALU.mult))],
                unroll=2, temps=lambda s, n: [s.sb(f"gate{i}", [P, SEQ]) for i in range(n)])
        project(nc, "down", a["w_ffn_out"], [tiles(hidden, 22)], [(0, SEQ)],
                [("vector", lambda e, m, b, banks, t: e.tensor_tensor(x[:, m, :], x[:, m, :], banks[0][0][:], ALU.add))],
                unroll=2)
    tap("h2", x)


MOD = 6
SEQS = [(0, CTX), (CTX, SEQ)]
CHUNKS = ALLTOK // P
CTXCH = CTX // P
ORDER = [list(range(CHUNKS)), list(range(CTXCH))[::-1] + list(range(CTXCH, CHUNKS))[::-1]]
UNITS = [(d, ch) for d in range(2) for ch in ORDER[d]]


def modulations(nc, name, w, bias, cvec, mods):
    def add_bias(e, m, b, banks, t):
        return e.tensor_tensor(mods[:, m, :], banks[0][0][:, 0:2], bias[:, m, :], ALU.add)
    project(nc, name, w, [[cvec[:, k, :] for k in range(KT)]], [(0, 2)], [("vector", add_bias)], unroll=8)


def modulation_gains(nc, name, layers):
    with Stage(nc, name) as st:
        block = st.cs.enter_context(nc.Block())

        @block.vector
        def _(dve):
            for L in layers:
                for i, pre, post in ((0, L.mix_pre, L.mix_post), (3, L.ffn_pre, L.ffn_post)):
                    scale, gate = (L.mods[:, (i + j) * KT:(i + j + 1) * KT, :] for j in (1, 2))
                    dve.scalar_tensor_tensor(out=scale, in0=scale, scalar=1.0, in1=last(pre[:], 2), op0=ALU.add, op1=ALU.mult)
                    dve.tensor_tensor(gate, gate, last(post[:], 2), ALU.mult)


def silu_columns(nc, name, buf):
    with Stage(nc, name) as st:
        block = st.cs.enter_context(nc.Block())

        @block.scalar
        def _(act):
            act.activation(buf, buf, ACT.Silu)


def conv3(e, out, x, w, n):
    e.tensor_scalar(out, x, w(1), None, ALU.mult)
    e.drain()
    e.scalar_tensor_tensor(out=out[:, 1:n], in0=x[:, 0:n - 1], scalar=w(0), in1=out[:, 1:n], op0=ALU.mult, op1=ALU.add)
    e.drain()
    return e.scalar_tensor_tensor(out=out[:, 0:n - 1], in0=x[:, 1:n], scalar=w(2), in1=out[:, 0:n - 1],
                                  op0=ALU.mult, op1=ALU.add)


def conv_grid(e, out, x, w):
    R, C = SEQ // 64, 64
    o3, x3 = (ap.rearrange("p (r c) -> p r c", c=C) for ap in (out, x))
    ins = e.tensor_scalar(out, x, w(1, 1), None, ALU.mult)
    for a in range(3):
        for b in range(3):
            if (a, b) == (1, 1):
                continue
            r0, r1 = max(0, 1 - a), min(R, R + 1 - a)
            c0, c1 = max(0, 1 - b), min(C, C + 1 - b)
            e.drain()
            o = o3[:, r0:r1, c0:c1]
            ins = e.scalar_tensor_tensor(out=o, in0=x3[:, r0 + a - 1:r1 + a - 1, c0 + b - 1:c1 + b - 1],
                                         scalar=w(a, b), in1=o, op0=ALU.mult, op1=ALU.add)
    return ins


def spatial_gate(nc, name, u, v, ws_t, bs, gv, out, eps):
    NG, NU = 4, 4 * CHUNKS
    with Stage(nc, name) as st:
        sq = st.sb("sq", [P, P])
        ss, rstd = st.sb("ss", [P, NU]), st.sb("rstd", [P, NU])
        banks = [[st.pb(f"z{i}_{j}") for j in range(2)] for i in range(2)]
        squared, normed, mixed, taken = (st.sem(n) for n in ("squared", "normed", "mixed", "taken"))
        block = st.cs.enter_context(nc.Block())

        @block.scalar
        def _(act):
            for n in range(NU):
                ch, g = n // NG, n % NG
                act.activation(sq[:], v[:, ch, g * P:(g + 1) * P], ACT.Square, accum_out=ss[:, n:n + 1])
                act.drain()
            act.activation(rstd[:], ss[:], ACT.Sqrt, bias=eps, scale=1.0 / P).then_inc(squared, 1)

        @block.vector
        def _(dve):
            dve.wait_ge(squared, 1)
            dve.reciprocal(rstd[:], rstd[:])
            dve.drain()
            for n in range(NU):
                ch, g = n // NG, n % NG
                vs = v[:, ch, g * P:(g + 1) * P]
                ins = dve.scalar_tensor_tensor(out=vs, in0=vs, scalar=rstd[:, n:n + 1], in1=gv[:, g * P:(g + 1) * P],
                                               op0=ALU.mult, op1=ALU.mult)
            ins.then_inc(normed, 1)
            for g in range(NG):
                dve.wait_ge(mixed, g + 1)
                for j, (c0, c1) in enumerate(((0, 4), (4, CHUNKS))):
                    o = out[:, g, c0 * P:c1 * P].rearrange("p (c q) -> p c q", q=P)
                    bank = banks[g % 2][j][:, 0:(c1 - c0) * P].rearrange("p (c q) -> p c q", q=P)
                    dve.tensor_tensor(o, bank, middle(bs[:, g * P:(g + 1) * P], c1 - c0), ALU.add)
                    dve.drain()
                    ins = dve.tensor_tensor(out[:, g, c0 * P:c1 * P], out[:, g, c0 * P:c1 * P], u[:, g, c0 * P:c1 * P], ALU.mult)
                ins.then_inc(taken, 1)

        @block.tensor
        def _(pe):
            pe.wait_ge(normed, 1)
            for g in range(NG):
                if g >= 2:
                    pe.wait_ge(taken, g - 1)
                for ch in range(CHUNKS):
                    mm = pe.matmul(banks[g % 2][ch // 4][:, (ch % 4) * P:(ch % 4 + 1) * P], v[:, ch, g * P:(g + 1) * P],
                                   ws_t[:, g, :], start=True, stop=True)
                mm.then_inc(mixed, 1)


DECAY_RATE = 0.6065306597126334


def rwkv_keys(nc, name, k, v, kk, vtok, b_kk, ident, blk, tiny):
    with Stage(nc, name) as st:
        sq = st.sb("sq", [P, 2, ALLTOK])
        norm = st.sb("norm", [P, 2, ALLTOK])
        sums = [[st.pb(f"sum{i}_{j}") for j in range(2)] for i in range(2)]
        turns = [st.pb(f"turn{i}") for i in range(2)]
        squared, summed, rooted, turned, copied = (st.sem(n) for n in ("squared", "summed", "rooted", "turned", "copied"))
        block = st.cs.enter_context(nc.Block())

        @block.vector
        def _(dve):
            for t in range(4):
                dve.tensor_scalar(kk[:, t, :], k[:, t, :], b_kk[:, t:t + 1], None, ALU.mult)
                dve.drain()
                dve.tensor_tensor(sq[:, t % 2, :], kk[:, t, :], kk[:, t, :], ALU.mult).then_inc(squared, 1)
                dve.wait_ge(summed, t + 1)
                for j, (t0, tw) in enumerate(SEQS):
                    ins = dve.tensor_scalar(norm[:, t % 2, t0:t0 + tw], sums[t % 2][j][:, 0:tw], 1e-12, None, ALU.max)
                ins.then_inc(rooted, 1)
                dve.wait_ge(copied, t + 1)
                dve.reciprocal(norm[:, t % 2, :], norm[:, t % 2, :])
                dve.drain()
                dve.tensor_tensor(kk[:, t, :], kk[:, t, :], norm[:, t % 2, :], ALU.mult)

        @block.tensor
        def _(pe):
            for t in range(4):
                pe.wait_ge(squared, t + 1)
                for j, (t0, tw) in enumerate(SEQS):
                    mm = pe.matmul(sums[t % 2][j][:, 0:tw], blk[:], sq[:, t % 2, t0:t0 + tw], start=True, stop=True)
                mm.then_inc(summed, 1)
            for ch in range(CHUNKS):
                if ch >= 2:
                    pe.wait_ge(copied, 4 + ch - 1)
                for t in range(4):
                    mm = pe.transpose(turns[ch % 2][:, t * P:(t + 1) * P], v[:, t, ch * P:(ch + 1) * P], ident[:])
                mm.then_inc(turned, 1)

        @block.scalar
        def _(act):
            for t in range(4):
                act.wait_ge(rooted, t + 1)
                act.activation(norm[:, t % 2, :], norm[:, t % 2, :], ACT.Sqrt).then_inc(copied, 1)
            for ch in range(CHUNKS):
                act.wait_ge(turned, ch + 1)
                act.activation(vtok[:, ch, :], turns[ch % 2][:], ACT.Copy).then_inc(copied, 1)


def rwkv_scan(nc, name, s):
    LEVELS = [2, 4, 8, 16, 32, 64]
    NL = len(LEVELS)
    NU = len(UNITS)
    with Stage(nc, name) as st:
        sig, aa, w0, w1, kd, qq, inv = (st.sb(n, [P, 4, P]) for n in ("sig", "aa", "w0", "w1", "kd", "qq", "inv"))
        pin, bb, bh, kh, stmp = sig, aa, aa, kd, inv
        half, hdec = st.sb("half", [P, 4, 1]), st.sb("hdec", [P, 4, 1])
        ar = st.sb("ar", [P, 4, 2, P])
        ktok, btok = st.sb("ktok", [P, 4, P]), st.sb("btok", [P, 4, P])
        kb = st.sb("kb", [P, 8, 4, P])
        X, XT, T = st.sb("X", [P, 8, P]), st.sb("XT", [P, 8, P]), st.sb("T", [P, 8, P])
        rhs, un = st.sb("rhs", [P, 512]), st.sb("un", [P, 512])
        state = st.sb("state", [P, 4, P])
        b = [st.pb(f"b{i}") for i in range(8)]
        names = ("lora", "gated", "centred", "exped", "prepared", "bonus_in", "bonus_out", "turned", "tokens", "scored",
                 "masked", "started", "t_ready", "t_copied", "x_ready", "x_taken", "rhs_ready", "rhs_copied",
                 "u_ready", "u_copied", "y_ready", "y_taken", "s_ready", "s_scaled", "s_taken", "keyed", "pooled", "kd_ready")
        S = {n: st.sem(n) for n in names}
        block = st.cs.enter_context(nc.Block())
        v4 = lambda bank: bank[:].rearrange("p (t n) -> p t n", t=4)

        @block.tensor
        def _(pe):
            for n, (d, ch) in enumerate(UNITS):
                cs, ds = slice(ch * P, (ch + 1) * P), slice(64 * d, 64 * d + 64)
                if n >= 1:
                    pe.wait_ge(S["x_taken"], 2 * NL * n)
                for t in range(4):
                    pe.matmul(b[0][:, t * P:(t + 1) * P], s.w_up[ds, t * P:(t + 1) * P], s.wd[ds, cs], start=True, stop=True)
                for t in range(4):
                    mm = pe.matmul(b[1][:, t * P:(t + 1) * P], s.a_up[ds, t * P:(t + 1) * P], s.ad[ds, cs], start=True, stop=True)
                mm.then_inc(S["lora"], 1)
                pe.wait_ge(S["bonus_in"], n + 1)
                if n >= 1:
                    pe.wait_ge(S["u_copied"], n)
                for t in range(4):
                    mm = pe.matmul(b[2][:, t * P:(t + 1) * P], s.blk_rk[:, t, :], qq[:, t, :], start=True, stop=True)
                mm.then_inc(S["bonus_out"], 1)
                pe.wait_ge(S["prepared"], n + 1)
                if n >= 1:
                    pe.wait_ge(S["y_taken"], n)
                    pe.wait_ge(S["s_taken"], n)
                for t in range(4):
                    pe.transpose(b[3][:, t * P:(t + 1) * P], kh[:, t, :], s.ident[:])
                for t in range(4):
                    mm = pe.transpose(b[4][:, t * P:(t + 1) * P], bh[:, t, :], s.ident[:])
                mm.then_inc(S["turned"], 1)
                for t in range(4):
                    if t == 0:
                        pe.wait_ge(S["keyed"], n + 1)
                    if t == 1:
                        pe.wait_ge(S["gated"], n + 1)
                    if t >= 2:
                        pe.wait_ge(S["masked"], 4 * n + t - 1)
                    for lhs, rhs_ap, bank, o in (
                            (kh, None, 0, 0), (bh, None, 0, 256), (None, bh, 1, t * P)):
                        for p in range(2):
                            ps = slice(64 * p, 64 * p + 64)
                            if bank == 0:
                                out, width = b[((5, 6), (0, 1))[t % 2][p]], 256
                                mm = pe.matmul(out[:, o:o + width], lhs[ps, t, :], ar[ps, t, :, :].rearrange("p a n -> p (a n)"),
                                               start=True, stop=True)
                            else:
                                mm = pe.matmul(b[(7, 2)[p]][:, o:o + P], ar[ps, t, 0, :], bh[ps, t, :], start=True, stop=True)
                    mm.then_inc(S["scored"], 1)
                for l in range(NL):
                    for g in range(2):
                        u = (n * NL + l) * 2 + g
                        if l == 0 and g == 0:
                            pe.wait_ge(S["tokens"], n + 1)
                            pe.wait_ge(S["masked"], 4 * n + 4)
                            pe.wait_ge(S["started"], n + 1)
                        if l >= 1:
                            pe.wait_ge(S["x_taken"], u - 1)
                        for h in range(4 * g, 4 * g + 4):
                            mm = pe.matmul(b[3 + g][:, (h % 4) * P:(h % 4 + 1) * P], kb[:, h, 2, :], X[:, h, :], start=True, stop=True)
                        mm.then_inc(S["t_ready"], 1)
                    for g in range(2):
                        u = (n * NL + l) * 2 + g
                        pe.wait_ge(S["t_copied"], u + 1)
                        xb, xtb = ((5, 6), (0, 1))[g]
                        if l < NL - 1:
                            for h in range(4 * g, 4 * g + 4):
                                pe.matmul(b[xb][:, (h % 4) * P:(h % 4 + 1) * P], XT[:, h, :], T[:, h, :], start=True, stop=True)
                        for h in range(4 * g, 4 * g + 4):
                            mm = pe.matmul(b[xtb][:, (h % 4) * P:(h % 4 + 1) * P], T[:, h, :], XT[:, h, :], start=True, stop=True)
                        mm.then_inc(S["x_ready"], 1)
                pe.wait_ge(S["s_scaled"], n + 1)
                for t in range(4):
                    pe.matmul(b[7][:, t * P:(t + 1) * P], ar[:, t, 0, :], state[:, t, :], start=True, stop=False, skip_group_check=True)
                    for h in (2 * t, 2 * t + 1):
                        mm = pe.matmul(b[7][:, h * 64:h * 64 + 64], kb[:, h, 0, :], s.vtok[:, ch, h * 64:h * 64 + 64],
                                       start=False, stop=True, skip_group_check=True)
                mm.then_inc(S["rhs_ready"], 1)
                pe.wait_ge(S["rhs_copied"], n + 1)
                pe.wait_ge(S["x_taken"], 2 * NL * (n + 1))
                for h in range(8):
                    mm = pe.matmul(b[2][:, h * 64:h * 64 + 64], XT[:, h, :], rhs[:, h * 64:h * 64 + 64], start=True, stop=True)
                mm.then_inc(S["u_ready"], 1)
                pe.wait_ge(S["u_copied"], n + 1)
                for t in range(4):
                    pe.matmul(b[3][:, t * P:(t + 1) * P], ar[:, t, 1, :], state[:, t, :], start=True, stop=False, skip_group_check=True)
                    for h in (2 * t, 2 * t + 1):
                        hs = slice(h * 64, h * 64 + 64)
                        pe.matmul(b[3][:, hs], kb[:, h, 1, :], s.vtok[:, ch, hs], start=False, stop=False, skip_group_check=True)
                        mm = pe.matmul(b[3][:, hs], kb[:, h, 3, :], un[:, hs], start=False, stop=True, skip_group_check=True)
                mm.then_inc(S["y_ready"], 1)
                for t in range(4):
                    ts = slice(t * P, (t + 1) * P)
                    pe.matmul(b[4][:, ts], ktok[:, t, :], s.vtok[:, ch, ts], start=True, stop=False)
                    mm = pe.matmul(b[4][:, ts], btok[:, t, :], un[:, ts], start=False, stop=True)
                mm.then_inc(S["s_ready"], 1)

        @block.scalar
        def _(act):
            for n, (d, ch) in enumerate(UNITS):
                act.wait_ge(S["lora"], n + 1)
                if n >= 1:
                    act.wait_ge(S["prepared"], n)
                for t in range(4):
                    act.activation(sig[:, t, :], b[0][:, t * P:(t + 1) * P], ACT.Sigmoid, bias=s.b_w0[:, d, t:t + 1])
                for t in range(4):
                    ins = act.activation(aa[:, t, :], b[1][:, t * P:(t + 1) * P], ACT.Sigmoid, bias=s.b_a0[:, d, t:t + 1])
                ins.then_inc(S["gated"], 1)
                act.wait_ge(S["centred"], n + 1)
                c = DECAY_RATE
                inc, exc, sgn = ((w0, w1, -c), (w1, w0, c))[d]
                act.activation(pin[:], inc[:], ACT.Exp, scale=sgn)
                act.activation(exc[:], exc[:], ACT.Exp, scale=sgn)
                act.activation(inv[:], inc[:], ACT.Exp, scale=-sgn)
                act.activation(hdec[:], half[:], ACT.Exp, scale=-c).then_inc(S["exped"], 1)
                act.wait_ge(S["turned"], n + 1)
                act.activation(ktok[:], v4(b[3]), ACT.Copy)
                act.activation(btok[:], v4(b[4]), ACT.Copy, scale=-1.0).then_inc(S["tokens"], 1)
                for l in range(NL):
                    for g in range(2):
                        u = (n * NL + l) * 2 + g
                        act.wait_ge(S["t_ready"], u + 1)
                        act.activation(T[:, 4 * g:4 * g + 4, :], v4(b[3 + g]), ACT.Copy).then_inc(S["t_copied"], 1)
                act.wait_ge(S["rhs_ready"], n + 1)
                act.activation(rhs[:], b[7][:], ACT.Copy).then_inc(S["rhs_copied"], 1)
                act.wait_ge(S["u_ready"], n + 1)
                act.activation(un[:], b[2][:], ACT.Copy).then_inc(S["u_copied"], 1)

        @block.gpsimd
        def _(pool):
            for n, (d, ch) in enumerate(UNITS):
                cs = slice(ch * P, (ch + 1) * P)
                pool.wait_ge(S["gated"], n + 1)
                if n >= 1:
                    pool.wait_ge(S["prepared"], n)
                pool.wait_ge(S["kd_ready"], n + 1)
                pool.tensor_tensor(bb[:], aa[:], s.kk[:, :, cs], ALU.mult)
                pool.tensor_tensor(kd[:], kd[:], s.k[:, :, cs], ALU.mult).then_inc(S["pooled"], 1)
                pool.wait_ge(S["pooled"], n + 1)
                if n >= 1:
                    pool.wait_ge(S["bonus_out"], n)
                pool.tensor_tensor(qq[:], kd[:], s.r[:, :, cs], ALU.mult).then_inc(S["bonus_in"], 1)

        @block.vector
        def _(dve):
            dve.memset(state[:], 0.0)
            for n, (d, ch) in enumerate(UNITS):
                cs = slice(ch * P, (ch + 1) * P)
                strict, X1, M = s.masks[d]
                dve.wait_ge(S["gated"], n + 1)
                for t in range(4):
                    ins = dve.tensor_scalar(kd[:, t, :], aa[:, t, :], s.b_ka[:, t:t + 1], s.one_ka[:, t:t + 1], ALU.mult, ALU.add)
                ins.then_inc(S["kd_ready"], 1)
                for t in range(4):
                    dve.tensor_tensor_scan(w0[:, t, :], s.one[:], sig[:, t, :], 0.0, ALU.mult, ALU.add)
                dve.drain()
                dve.tensor_scalar(half[:], w0[:, :, P - 1:P], 0.5, None, ALU.mult)
                dve.drain()
                dve.tensor_tensor(w0[:], w0[:], last(half[:, :, 0], P), ALU.subtract)
                dve.drain()
                dve.tensor_tensor(w1[:], w0[:], sig[:], ALU.subtract).then_inc(S["centred"], 1)
                dve.wait_ge(S["exped"], n + 1)
                if d == 0 and ch == 0:
                    pass
                elif ch == ORDER[d][0]:
                    dve.memset(state[:], 0.0)
                    dve.drain()
                dve.wait_ge(S["bonus_in"], n + 1)
                pex = (w1, w0)[d]
                dve.tensor_tensor(ar[:, :, 0, :], s.kk[:, :, cs], pex[:], ALU.mult)
                dve.tensor_tensor(ar[:, :, 1, :], s.r[:, :, cs], pin[:], ALU.mult)
                dve.tensor_tensor(kh[:], kd[:], inv[:], ALU.mult)
                dve.tensor_tensor(bh[:], bb[:], inv[:], ALU.mult).then_inc(S["prepared"], 1)
                dve.tensor_tensor(state[:], state[:], last(hdec[:, :, 0], P), ALU.mult).then_inc(S["s_scaled"], 1)
                dve.wait_ge(S["bonus_out"], n + 1)
                if d == 0:
                    dve.tensor_copy(s.bonus[:, :, cs], v4(b[2])).then_inc(S["keyed"], 1)
                else:
                    dve.tensor_tensor(s.bonus[:, :, cs], s.bonus[:, :, cs], v4(b[2]), ALU.add).then_inc(S["keyed"], 1)
                for t in range(4):
                    dve.wait_ge(S["scored"], 4 * n + t + 1)
                    for p in range(2):
                        ins = dve.tensor_tensor(kb[:, 2 * t + p, :, :].rearrange("p a n -> p (a n)"), b[((5, 6), (0, 1))[t % 2][p]][:],
                                                strict[:], ALU.mult)
                    ins.then_inc(S["masked"], 1)
                for p in range(2):
                    dve.tensor_tensor(X[:, p::2, :], v4(b[(7, 2)[p]]), middle(X1[:, 0, :], 4), ALU.mult)
                dve.drain()
                dve.tensor_tensor(X[:], X[:], middle(s.ident[:], 8), ALU.add)
                dve.tensor_tensor(XT[:], kb[:, :, 2, :], middle(X1[:, 1, :], 8), ALU.mult)
                dve.drain()
                dve.tensor_tensor(XT[:], XT[:], middle(s.ident[:], 8), ALU.add).then_inc(S["started"], 1)
                for l in range(NL):
                    for g in range(2):
                        u = (n * NL + l) * 2 + g
                        dve.wait_ge(S["x_ready"], u + 1)
                        xb, xtb = ((5, 6), (0, 1))[g]
                        hg = slice(4 * g, 4 * g + 4)
                        if l < NL - 1:
                            dve.copy_predicated(X[:, hg, :], middle(M[0][:, l, :], 4), v4(b[xb]))
                        dve.copy_predicated(XT[:, hg, :], middle(M[1][:, l, :], 4), v4(b[xtb])).then_inc(S["x_taken"], 1)
                dve.wait_ge(S["y_ready"], n + 1)
                y = s.y[:, ch, :]
                if d == 0:
                    dve.tensor_copy(y, b[3][:]).then_inc(S["y_taken"], 1)
                else:
                    dve.tensor_tensor(y, y, b[3][:], ALU.add).then_inc(S["y_taken"], 1)
                dve.wait_ge(S["s_ready"], n + 1)
                dve.tensor_tensor(stmp[:], state[:], v4(b[4]), ALU.add).then_inc(S["s_taken"], 1)
                dve.drain()
                dve.tensor_tensor(stmp[:], stmp[:], middle(s.blk[:], 4), ALU.mult)
                dve.drain()
                dve.tensor_tensor(state[:], stmp[:], last(hdec[:, :, 0], P), ALU.mult)
                dve.drain()


LN_EPS = 64e-5


def rwkv_out(nc, name, s, out):
    NH = CHUNKS * 8
    with Stage(nc, name) as st:
        sq = st.sb("sq", [P, CHUNKS * 512])
        mu, var = st.sb("mu", [P, NH]), st.sb("var", [P, NH])
        turned_y = [[st.pb(f"y{i}_{j}") for j in range(2)] for i in range(2)]
        gate = [[st.pb(f"g{i}_{j}") for j in range(2)] for i in range(2)]
        centred, squared, rooted, normed, ready, taken = (
            st.sem(n) for n in ("centred", "squared", "rooted", "normed", "ready", "taken"))
        block = st.cs.enter_context(nc.Block())
        y3 = s.y[:].rearrange("p c (h n) -> p (c h) n", n=64)
        sq3 = sq[:].rearrange("p (h n) -> p h n", n=64)

        @block.vector
        def _(dve):
            dve.tensor_reduce(mu[:], y3, AX.X, ALU.add)
            dve.drain()
            dve.tensor_scalar(mu[:], mu[:], 1.0 / 64, None, ALU.mult)
            dve.drain()
            dve.tensor_tensor(y3, y3, last(mu[:], 64), ALU.subtract).then_inc(centred, 1)
            dve.wait_ge(squared, 1)
            dve.tensor_reduce(var[:], sq3, AX.X, ALU.add).then_inc(rooted, 1)
            dve.wait_ge(squared, 2)
            dve.reciprocal(var[:], var[:])
            dve.drain()
            dve.tensor_tensor(y3, y3, last(var[:], 64), ALU.mult).then_inc(normed, 1)
            for t in range(4):
                for j, (t0, tw) in enumerate(SEQS):
                    n = 2 * t + j
                    o, v, bo = (z[:, t, t0:t0 + tw] for z in (out, s.v, s.bonus))
                    dve.tensor_tensor(v, v, bo, ALU.mult)
                    dve.wait_ge(ready, n + 1)
                    dve.drain()
                    dve.scalar_tensor_tensor(out=o, in0=turned_y[t % 2][j][:, 0:tw], scalar=s.ln_g[:, t:t + 1], in1=v,
                                             op0=ALU.mult, op1=ALU.add)
                    dve.drain()
                    dve.scalar_tensor_tensor(out=o, in0=o, scalar=s.ln_b[:, t:t + 1], in1=gate[t % 2][j][:, 0:tw],
                                             op0=ALU.add, op1=ALU.mult).then_inc(taken, 1)

        @block.scalar
        def _(act):
            act.wait_ge(centred, 1)
            act.activation(sq[:], s.y[:].rearrange("p c n -> p (c n)"), ACT.Square).then_inc(squared, 1)
            act.wait_ge(rooted, 1)
            act.activation(var[:], var[:], ACT.Sqrt, bias=s.ln_eps, scale=1.0 / 64).then_inc(squared, 1)

        @block.tensor
        def _(pe):
            pe.wait_ge(normed, 1)
            for t in range(4):
                for j, (t0, tw) in enumerate(SEQS):
                    n = 2 * t + j
                    if n >= 4:
                        pe.wait_ge(taken, n - 3)
                    for i in range(tw // P):
                        ch = t0 // P + i
                        pe.transpose(turned_y[t % 2][j][:, i * P:(i + 1) * P], s.y[:, ch, t * P:(t + 1) * P], s.ident[:])
                    pe.matmul(gate[t % 2][j][:, 0:tw], s.g_up[:, t * P:(t + 1) * P], s.gd[:, t0:t0 + tw],
                              start=True, stop=True).then_inc(ready, 1)


class Parts:
    pass


def ffn2(nc, name, a, c, L, x, y, h, seqs, w_up, w_down):
    t_min, t_max = seqs[0][0], seqs[-1][0] + seqs[-1][1]
    with Stage(nc, name) as st:
        hidden = st.sb("hidden", [P, 22, t_max - t_min])
        with Stage(nc, name + "_in") as s2:
            h = s2.sb("h", [P, KT, ALLTOK])
            cw, cb = s2.sb("cw", [P, 22, 9]), s2.sb("cb", [P, 22, 1])
            load(nc, name + "load", [(cw[:], a[f"ffn_conv{L.i}"]), (cb[:], a[f"ffn_conv_b{L.i}"])])
            pre_norm(nc, name, c, L, 3, x, h, seqs)

            def conv(e, m, b, banks, t):
                for j, (t0, tw) in enumerate(seqs):
                    acc = t[0][:, t0:t0 + tw]
                    if tw == SEQ:
                        ins = conv_grid(e, acc, banks[0][j][:, 0:tw], lambda p, q: cw[:, m, 3 * p + q:3 * p + q + 1])
                    else:
                        ins = conv3(e, acc, banks[0][j][:, 0:tw], lambda q: cw[:, m, 3 + q:4 + q], tw)
                return ins

            def gelu(e, m, b, banks, t):
                return e.activation(t[1][:, t_min:t_max], t[0][:, t_min:t_max], ACT.Gelu_apprx_tanh, bias=cb[:, m, :])

            def mult(e, m, b, banks, t):
                for j, (t0, tw) in enumerate(seqs):
                    ins = e.tensor_tensor(hidden[:, m, t0 - t_min:t0 - t_min + tw], t[1][:, t0:t0 + tw], banks[1][j][:, 0:tw], ALU.mult)
                return ins

            project(nc, name + "up", w_up, [tiles(h, KT)] * 2, seqs, [("vector", conv), ("scalar", gelu), ("vector", mult)],
                    unroll=2, temps=lambda s, n: [[s.sb(f"t{i}_{j}", [P, ALLTOK]) for j in range(2)] for i in range(n)])
        y = st.sb("y", [P, KT, ALLTOK])
        down(nc, name + "down", w_down, [hidden[:, k, :] for k in range(22)], y, seqs, t_min)
        post_norm(nc, name + "p", c, L, 5, x, y, seqs)


def down(nc, name, w, src, y, seqs, t_min):
    def keep(e, m, b, banks, t):
        for j, (t0, tw) in enumerate(seqs):
            ins = e.activation(y[:, m, t0:t0 + tw], banks[0][j][:, 0:tw], ACT.Copy)
        return ins
    project(nc, name, w, [src], [(t0 - t_min, tw) for t0, tw in seqs], [("scalar", keep)], unroll=2)


def pre_norm(nc, name, c, L, i, x, h, seqs):
    for t0, tw in seqs:
        s = 0 if t0 == 0 else 1
        at = lambda buf: lambda k: buf[:, k, t0:t0 + tw]
        mod = lambda j: lambda k: L.mods[:, (i + j) * KT + k, s:s + 1]
        rms_norm(nc, f"{name}pre{s}", KT, tw, at(x), at(h), c.one, c.eps, gain=mod(1), shift=mod(0))


def post_norm(nc, name, c, L, i, x, y, seqs):
    for t0, tw in seqs:
        s = 0 if t0 == 0 else 1
        at = lambda buf: lambda k: buf[:, k, t0:t0 + tw]
        rms_norm(nc, f"{name}post{s}", KT, tw, at(y), None, c.one, c.eps,
                 gain=lambda k: L.mods[:, i * KT + k, s:s + 1], residual=at(x))


def mixer_ab(nc, a, c, L, x, tap):
    with Stage(nc, "ab") as st:
        cat = st.sb("cat", [P, 8, ALLTOK])
        with Stage(nc, "ab2") as s1:
            s = Parts()
            rkv = s1.sb("rkv", [P, 12, ALLTOK])
            s.r, s.k, s.v = rkv[:, 0:4, :], rkv[:, 4:8, :], rkv[:, 8:12, :]
            s.bonus = cat[:, 4:8, :]
            lora = s1.sb("lora", [P, 3, ALLTOK])
            s.wd, s.ad, s.gd = lora[:, 0, :], lora[:, 1, :], lora[:, 2, :]
            with Stage(nc, "ab3") as s2:
                h = s2.sb("h", [P, KT, ALLTOK])
                pre_norm(nc, "ab", c, L, 0, x, h, SEQS)
                tap("hab", h)
                u = s2.sb("u", [P, 4, ALLTOK])
                vg = s2.sb("vg", [P, CHUNKS, 512])
                shift = s2.sb("shift", [P, 12, 3])
                ws, bs, gv = s2.sb("ws", [P, 4, P]), s2.sb("bs", [P, 512]), s2.sb("gv", [P, 512])
                load(nc, "abload", [(shift[:], a["b_shift"]), (ws[:], a["a_ws"]), (bs[:], broadcast_rows(a["a_bs"], 512)),
                                    (gv[:], broadcast_rows(a["a_gv"], 512))])

                def each(f):
                    def g(e, m, b, banks, t):
                        for j, (t0, tw) in enumerate(SEQS):
                            ins = f(e, m, b, banks[0][j][:, 0:tw], t0, tw)
                        return ins
                    return g

                project(nc, "abu", a["w_ab_u"], [tiles(h, KT)], SEQS, [("scalar", each(
                    lambda e, m, b, bank, t0, tw: e.activation(u[:, m, t0:t0 + tw], bank, ACT.Gelu_apprx_tanh)))], unroll=4)
                project(nc, "abrkv", a["w_ab_rkv"], [tiles(h, KT)], SEQS, [("vector", each(
                    lambda e, m, b, bank, t0, tw: conv3(e, rkv[:, m, t0:t0 + tw], bank, lambda j: shift[:, m, j:j + 1], tw)))],
                    unroll=4)
                project(nc, "ablora", a["w_ab_lora"], [tiles(h, KT)], SEQS, [("scalar", each(
                    lambda e, m, b, bank, t0, tw: e.activation(lora[:, b, t0:t0 + tw], bank, (ACT.Tanh, ACT.Copy, ACT.Sigmoid)[b])))],
                    unroll=3)
                token_major(nc, "abv", a["w_ab_v"], tiles(h, KT), [slice(i * P, (i + 1) * P) for i in range(CHUNKS)],
                            [("scalar", lambda e, n, r, bank, t: e.activation(vg[:, r, :], bank, ACT.Gelu_apprx_tanh))])
                spatial_gate(nc, "gate", u, vg, ws, bs, gv, cat, c.eps)
            tap("rkv", rkv)
            tap("lora", lora)
            with Stage(nc, "rw") as s2:
                pairs = []

                def const(name, shape, dt=F32):
                    buf = s2.sb("c_" + name, shape, dt)
                    pairs.append((buf[:], a[name]))
                    return buf

                s.y = s2.sb("y", [P, CHUNKS, 512])
                s.kk = s2.sb("kk", [P, 4, ALLTOK])
                s.vtok = s2.sb("vtok", [P, CHUNKS, 512])
                s.ident, s.one = c.ident, c.one
                s.blk = const("blk64", [P, P])
                s.w_up, s.a_up = const("b_w_up", [P, 512]), const("b_a_up", [P, 512])
                s.b_w0, s.b_a0 = const("b_w0", [P, 2, 4]), const("b_a0", [P, 2, 4])
                s.b_ka, kkw, rk = const("b_ka", [P, 4]), const("b_kk", [P, 4]), const("b_rk", [P, 4])
                s.ln_g, s.ln_b = const("b_ln_g", [P, 4]), const("b_ln_b", [P, 4])
                lneps = const("ln_eps", [P, 1])
                s.ln_eps = lneps[:, 0:1]
                strict, x1 = const("strict", [P, 2, 4 * P]), const("x1", [P, 2, 2, P])
                lev = s2.sb("lev", [P, 2, 6, P], mybir.dt.uint8)
                s.masks = [(strict[:, d], x1[:, d], (lev[:, d], lev[:, 1 - d])) for d in range(2)]
                s.one_ka = s2.sb("one_ka", [P, 4])
                s.blk_rk = s2.sb("blk_rk", [P, 4, P])
                load(nc, "rwload", pairs)
                with Stage(nc, "rwprep") as s3:
                    levels, loaded = s3.sb("levels", [P, 2, 6, P]), s3.sem("loaded")
                    block = s3.cs.enter_context(nc.Block())

                    @block.sync
                    def _(sp):
                        sp.dma_start(levels[:], a["levels"]).then_inc(loaded, 16)

                    @block.vector
                    def _(dve):
                        dve.tensor_scalar(s.one_ka[:], s.b_ka[:], -1.0, 1.0, ALU.mult, ALU.add)
                        dve.tensor_tensor(s.blk_rk[:], middle(s.blk[:], 4), last(rk[:], P), ALU.mult)
                        dve.wait_ge(loaded, 16)
                        dve.tensor_copy(lev[:], levels[:])
                rwkv_keys(nc, "keys", s.k, s.v, s.kk, s.vtok, kkw, c.ident, s.blk, None)
                tap("kk", s.kk)
                tap("vtok", s.vtok)
                rwkv_scan(nc, "rwkv", s)
                tap("yrw", s.y)
                s.g_up = s2.sb("g_up", [P, 512])
                load(nc, "gload", [(s.g_up[:], a["b_g_up"])])
                rwkv_out(nc, "rwout", s, cat[:, 4:8, :])
        tap("cat", cat)
        y = st.sb("y", [P, KT, ALLTOK])
        down(nc, "about", a["w_ab_out"], tiles(cat, 8), y, SEQS, 0)
        tap("yab", y)
        post_norm(nc, "abp", c, L, 2, x, y, SEQS)


def second_block(nc, a, c, x, tap):
    with Stage(nc, "mods") as st:
        layers = []
        for i in range(2):
            L = Parts()
            L.i = i
            L.mods = st.sb(f"mods{i}", [P, MOD * KT, 2])
            L.bias = st.sb(f"bias{i}", [P, MOD * KT, 2])
            L.mix_pre, L.mix_post, L.ffn_pre, L.ffn_post = (st.sb(f"{n}{i}", [P, KT]) for n in ("mix_pre", "mix_post", "ffn_pre", "ffn_post"))
            layers.append(L)
        cvec = st.sb("cvec", [P, KT, 2])
        load(nc, "modload", [(cvec[:], a["cvec"])] + [(b[:], a[f"{n}{L.i}"]) for L in layers for b, n in (
            (L.bias, "ada_b"), (L.mix_pre, "norm_mix_pre"), (L.mix_post, "norm_mix_post"),
            (L.ffn_pre, "norm_ffn_pre"), (L.ffn_post, "norm_ffn_post"))])
        silu_columns(nc, "silu", cvec[:])
        for L in layers:
            modulations(nc, f"mod{L.i}", a[f"w_ada{L.i}"], L.bias, cvec, L.mods)
        modulation_gains(nc, "gains", layers)
        mixer_ab(nc, a, c, layers[0], x, tap)
        tap("x_ab", x)
        ffn2(nc, "f0", a, c, layers[0], x, None, None, SEQS, a["w_ffn_up0"], a["w_ffn_down0"])
        tap("x_l0", x)
        mixer_mlstm(nc, a, c, layers[1], x, tap)
        tap("x_ml", x)
        ffn2(nc, "f1", a, c, layers[1], x, None, None, SEQS[1:], a["w_ffn_up1"], a["w_ffn_down1"])
        tap("x_l1", x)


MH, MD = 4, 256


def expand_blocks(nc, name, compact, mask, out):
    with Stage(nc, name) as st:
        block = st.cs.enter_context(nc.Block())

        @block.vector
        def _(dve):
            for t in range(KT):
                dve.tensor_tensor(out[:, t, :].rearrange("p (g o) -> p g o", o=4), middle(compact[:, t, :], P // 4),
                                  mask[:].rearrange("p (g o) -> p g o", o=4), ALU.mult)


def mlstm_heads(nc, name, xm, xcv, wq, wk, wv, q, k, ktok, vtok, cb):
    with Stage(nc, name) as st:
        banks = [st.pb(f"bank{i}") for i in range(8)]
        made, taken_a, taken_v = st.sem("made"), st.sem("taken_a"), st.sem("taken_v")
        block = st.cs.enter_context(nc.Block())
        scale = MD ** -0.5
        jobs = [(w, t) for t in range(KT) for w in ("q", "k")]
        jobs += [(w, ch, half) for w in ("vt", "kt") for ch in range(CHUNKS) for half in range(2)]

        @block.tensor
        def _(pe):
            for n, job in enumerate(jobs):
                if n >= 8:
                    pe.wait_ge((taken_a, taken_v)[n % 2], (n - 8) // 2 + 1)
                bank = banks[n % 8]
                if job[0] in ("q", "k"):
                    mm = pe.matmul(bank[:], (wq if job[0] == "q" else wk)[:, job[1], :], xcv[:, job[1], CTX:ALLTOK], start=True, stop=True)
                else:
                    w, ch, half = job
                    for i in range(4):
                        t = 4 * half + i
                        mm = pe.matmul(bank[:, i * P:(i + 1) * P], (xcv if w == "kt" else xm)[:, t, ch * P:(ch + 1) * P],
                                       (wk if w == "kt" else wv)[:, t, :], start=True, stop=True)
                mm.then_inc(made, 1)

        def place(job):
            if job[0] in ("q", "k"):
                return (q if job[0] == "q" else k)[:, job[1], :], 1.0 if job[0] == "q" else scale
            if job[0] == "kt":
                return ktok[:, job[1], job[2] * 512:job[2] * 512 + 512].rearrange("p (h n) -> p h n", h=2), scale
            return vtok[:, job[1], 2 * job[2]:2 * job[2] + 2, 0:MD], 1.0

        def source(n):
            return banks[n % 8][:] if jobs[n][0] in ("q", "k") else banks[n % 8][:].rearrange("p (h n) -> p h n", h=2)

        @block.scalar
        def _(act):
            for n in range(0, len(jobs), 2):
                act.wait_ge(made, n + 1)
                dst, factor = place(jobs[n])
                act.activation(dst, source(n), ACT.Copy, scale=factor).then_inc(taken_a, 1)

        @block.vector
        def _(dve):
            dve.memset(vtok[:, :, :, MD:MD + 1], 1.0)
            for n in range(1, len(jobs), 2):
                dve.wait_ge(made, n + 1)
                dst, factor = place(jobs[n])
                dve.tensor_scalar(dst, source(n), factor, None, ALU.mult).then_inc(taken_v, 1)


def mlstm_gates(nc, name, raw, bias, tri, m, one):
    G = 2 * MH
    with Stage(nc, name) as st:
        x, ab, lf = st.sb("x", [P, CHUNKS, 2, G]), st.sb("ab", [P, CHUNKS, G]), st.sb("lf", [P, CHUNKS, G])
        ps = [st.pb(f"ps{i}") for i in range(2)]
        added, logged, forgot, summed = (st.sem(n) for n in ("added", "logged", "forgot", "summed"))
        block = st.cs.enter_context(nc.Block())
        W = CHUNKS * MH

        @block.vector
        def _(dve):
            dve.tensor_tensor(x[:].rearrange("p c a g -> p c (a g)"), raw[:], middle(bias[:], CHUNKS), ALU.add).then_inc(added, 1)
            dve.wait_ge(logged, 1)
            dve.scalar_tensor_tensor(out=lf[:], in0=x[:, :, 1, :], scalar=0.0, in1=ab[:], op0=ALU.min, op1=ALU.subtract).then_inc(forgot, 1)
            dve.wait_ge(summed, 1)
            for d in range(2):
                dve.tensor_copy(m.b[:, :, d, :], ps[d][:, 0:W].rearrange("p (c h) -> p c h", h=MH))
            dve.drain()
            dve.tensor_tensor(m.cc[:].rearrange("p c d h -> p c (d h)"), x[:, :, 0, :], m.b[:].rearrange("p c d h -> p c (d h)"), ALU.subtract)

        @block.scalar
        def _(act):
            act.wait_ge(added, 1)
            act.activation(ab[:], x[:, :, 1, :], ACT.Abs)
            act.drain()
            act.activation(ab[:], ab[:], ACT.Exp, scale=-1.0)
            act.drain()
            act.activation(ab[:], ab[:], ACT.Ln, bias=one[:, 0:1]).then_inc(logged, 1)

        @block.tensor
        def _(pe):
            pe.wait_ge(forgot, 1)
            for d in range(2):
                mm = pe.matmul(ps[d][:, 0:W], tri[d][:], lf[:, :, d * MH:(d + 1) * MH], start=True, stop=True)
            mm.then_inc(summed, 1)


def mlstm_scan(nc, name, m, q, k, ktok, vtok, hsum, ident, neg, edge):
    NU = len(UNITS)
    V = MD + 1
    with Stage(nc, name) as st:
        mm_b = st.sb("mm_b", [P, 2 * MH])
        nmm, rmax, mprev, win, floor, kco, carry, den = (
            st.sb(n, [P, MH]) for n in ("nmm", "rmax", "mprev", "win", "floor", "kco", "carry", "den"))
        args = st.sb("args", [P, 4, MH])
        edge_sb = st.sb("edge_sb", [P, 2 * MH])
        E, Sm, St = (st.sb(n, [P, MH, P]) for n in ("E", "Sm", "St"))
        num = st.sb("num", [P, MH, V])
        kw = st.sb("kw", [P, MH * MD])
        state = st.sb("state", [P, 2 * MH, V])
        cbank, sbank, ebank, tbank = (st.pb(n) for n in ("cbank", "sbank", "ebank", "tbank"))
        work = [st.pb(f"work{i}") for i in range(4)]
        names = ("spread", "maxed", "picked", "argued", "exped", "weighed", "scored", "masked", "turned", "copied",
                 "inner", "outer", "scaled", "summed", "updated", "taken", "keyed", "read")
        S = {n: st.sem(n) for n in names}
        block = st.cs.enter_context(nc.Block())
        xn = [n for n, (d, ch) in enumerate(UNITS) if ch >= CTXCH]
        before = lambda n: sum(1 for i in xn if i < n)

        @block.tensor
        def _(pe):
            for n, (d, ch) in enumerate(UNITS):
                i = before(n)
                js = slice((ch - CTXCH) * P, (ch - CTXCH + 1) * P)
                if n >= 1:
                    pe.wait_ge(S["exped"], n)
                for h in range(MH):
                    bank = cbank[:, h * P:(h + 1) * P]
                    pe.matmul(bank, m.cc[:, ch, d, h:h + 1].to_broadcast([P, P]), ident[:], start=True, stop=False)
                    mm = pe.matmul(bank, ident[:], neg[d][:], start=False, stop=True)
                mm.then_inc(S["spread"], 1)
                pe.wait_ge(S["maxed"], n + 1)
                if n >= 1:
                    pe.wait_ge(S["argued"], n)
                pe.matmul(ebank[:, 0:2 * MH], edge[d][:], mm_b[:], start=True, stop=True).then_inc(S["picked"], 1)
                if ch >= CTXCH:
                    if i >= 1:
                        pe.wait_ge(S["masked"], i)
                    for h in range(MH):
                        for kt in range(2):
                            mm = pe.matmul(sbank[:, h * P:(h + 1) * P], q[:, 2 * h + kt, js], k[:, 2 * h + kt, js],
                                           start=(kt == 0), stop=(kt == 1))
                    mm.then_inc(S["scored"], 1)
                    pe.wait_ge(S["masked"], i + 1)
                    for h in range(MH):
                        mm = pe.transpose(tbank[:, h * P:(h + 1) * P], Sm[:, h, :], ident[:])
                    mm.then_inc(S["turned"], 1)
                    pe.wait_ge(S["copied"], i + 1)
                    for h in range(MH):
                        inner, outer = work[2 * (h % 2)], work[2 * (h % 2) + 1]
                        if h >= 2:
                            pe.wait_ge(S["summed"], i * MH + h - 1)
                        pe.matmul(inner[:, 0:V], St[:, h, :], vtok[:, ch, h, :], start=True, stop=True).then_inc(S["inner"], 1)
                        for kt in range(2):
                            mm = pe.matmul(outer[:, 0:V], q[:, 2 * h + kt, js], state[:, 2 * h + kt, :], start=(kt == 0), stop=(kt == 1))
                        mm.then_inc(S["outer"], 1)
                    pe.wait_ge(S["summed"], i * MH + MH)
                pe.wait_ge(S["keyed"], n + 1)
                for u in range(2 * MH):
                    if u >= 4:
                        pe.wait_ge(S["taken"], n * 2 * MH + u - 3)
                    pe.matmul(work[u % 4][:, 0:V], kw[:, u * P:(u + 1) * P], vtok[:, ch, u // 2, :], start=True, stop=True).then_inc(S["updated"], 1)
                pe.wait_ge(S["taken"], (n + 1) * 2 * MH)

        @block.scalar
        def _(act):
            for n, (d, ch) in enumerate(UNITS):
                i = before(n)
                act.wait_ge(S["maxed"], n + 1)
                if ch >= CTXCH and i >= 1:
                    act.wait_ge(S["masked"], i)
                if n >= 1:
                    act.wait_ge(S["keyed"], n)
                    act.wait_ge(S["read"], n)
                for h in range(MH):
                    act.activation(E[:, h, :], cbank[:, h * P:(h + 1) * P], ACT.Exp, bias=nmm[:, h:h + 1])
                act.activation(win[:], args[:, 0, :], ACT.Exp)
                act.activation(floor[:], args[:, 1, :], ACT.Exp).then_inc(S["exped"], 1)
                act.wait_ge(S["argued"], n + 1)
                act.activation(kco[:], args[:, 2, :], ACT.Exp)
                act.activation(carry[:], args[:, 3, :], ACT.Exp).then_inc(S["weighed"], 1)
                if ch >= CTXCH:
                    act.wait_ge(S["turned"], i + 1)
                    act.activation(St[:], tbank[:].rearrange("p (h n) -> p h n", h=MH), ACT.Copy).then_inc(S["copied"], 1)
                    for h in range(MH):
                        act.wait_ge(S["outer"], i * MH + h + 1)
                        act.activation(num[:, h, :], work[2 * (h % 2) + 1][:, 0:V], ACT.Copy, scale=win[:, h:h + 1]).then_inc(S["scaled"], 1)

        @block.vector
        def _(dve):
            for n, (d, ch) in enumerate(UNITS):
                i = before(n)
                if n in (0, NU // 2):
                    dve.memset(state[:], 0.0)
                    dve.memset(mprev[:], 0.0)
                    dve.drain()
                dve.wait_ge(S["spread"], n + 1)
                dve.tensor_reduce(rmax[:], cbank[:].rearrange("p (h n) -> p h n", h=MH), AX.X, ALU.max)
                dve.tensor_copy(mm_b[:, MH:2 * MH], m.b[:, ch, d, :])
                dve.drain()
                dve.tensor_tensor(mm_b[:, 0:MH], rmax[:], mprev[:], ALU.max)
                dve.drain()
                dve.tensor_scalar(nmm[:], mm_b[:, 0:MH], -1.0, None, ALU.mult)
                dve.tensor_tensor(args[:, 0, :], mprev[:], mm_b[:, 0:MH], ALU.subtract)
                dve.drain()
                dve.tensor_tensor(args[:, 1, :], nmm[:], mm_b[:, MH:2 * MH], ALU.subtract).then_inc(S["maxed"], 1)
                dve.wait_ge(S["picked"], n + 1)
                dve.tensor_copy(edge_sb[:], ebank[:, 0:2 * MH])
                dve.drain()
                dve.tensor_tensor(args[:, 2, :], m.cc[:, ch, d, :], edge_sb[:, 0:MH], ALU.subtract)
                dve.tensor_tensor(args[:, 3, :], mprev[:], edge_sb[:, 0:MH], ALU.subtract).then_inc(S["argued"], 1)
                dve.drain()
                dve.tensor_tensor(mprev[:], edge_sb[:, 0:MH], edge_sb[:, MH:2 * MH], ALU.add)
                dve.wait_ge(S["exped"], n + 1)
                dve.wait_ge(S["weighed"], n + 1)
                dve.tensor_tensor(kw[:].rearrange("p (h n) -> p h n", h=MH), ktok[:, ch, :].rearrange("p (h n) -> p h n", h=MH),
                                  last(kco[:], MD), ALU.mult).then_inc(S["keyed"], 1)
                if ch >= CTXCH:
                    dve.wait_ge(S["scored"], i + 1)
                    dve.tensor_tensor(Sm[:], sbank[:].rearrange("p (h n) -> p h n", h=MH), E[:], ALU.mult).then_inc(S["masked"], 1)
                    for h in range(MH):
                        dve.wait_ge(S["scaled"], i * MH + h + 1)
                        dve.tensor_tensor(num[:, h, :], num[:, h, :], work[2 * (h % 2)][:, 0:V], ALU.add).then_inc(S["summed"], 1)
                    dve.drain()
                    dcol = num[:, :, MD]
                    dve.scalar_tensor_tensor(out=den[:], in0=dcol, scalar=-1.0, in1=dcol, op0=ALU.mult, op1=ALU.max)
                    dve.drain()
                    dve.tensor_tensor(den[:], den[:], floor[:], ALU.max)
                    dve.drain()
                    dve.reciprocal(den[:], den[:])
                    dve.drain()
                    h4 = hsum[:, ch - CTXCH, :].rearrange("p (h n) -> p h n", h=MH)
                    if d == 0:
                        dve.tensor_tensor(h4, num[:, :, 0:MD], last(den[:], MD), ALU.mult)
                    else:
                        dve.tensor_tensor(num[:, :, 0:MD], num[:, :, 0:MD], last(den[:], MD), ALU.mult)
                        dve.drain()
                        dve.tensor_tensor(h4, h4, num[:, :, 0:MD], ALU.add)
                dve.drain()
                for u in range(2 * MH):
                    dve.wait_ge(S["updated"], n * 2 * MH + u + 1)
                    ins = dve.scalar_tensor_tensor(out=state[:, u, :], in0=state[:, u, :], scalar=carry[:, u // 2:u // 2 + 1],
                                                   in1=work[u % 4][:, 0:V], op0=ALU.mult, op1=ALU.add)
                    ins.then_inc(S["taken"], 1)
                dve.drain()
                dve.nop().then_inc(S["read"], 1)


def mlstm_out(nc, name, hsum, xcv, z, c_norm, c_skip, out, ident, eps):
    NU = NCH * MH
    with Stage(nc, name) as st:
        sq = st.sb("sq", [P, MD])
        ss = st.sb("ss", [P, NU])
        tmp = st.sb("tmp", [P, 2, SEQ])
        banks = [st.pb(f"bank{i}") for i in range(2)]
        rooted, normed, turned, taken, scaled = (st.sem(n) for n in ("rooted", "normed", "turned", "taken", "scaled"))
        block = st.cs.enter_context(nc.Block())

        @block.scalar
        def _(act):
            for n in range(NU):
                act.activation(sq[:], hsum[:, n // MH, (n % MH) * MD:(n % MH + 1) * MD], ACT.Square, accum_out=ss[:, n:n + 1])
                act.drain()
            act.activation(ss[:], ss[:], ACT.Sqrt, bias=eps, scale=1.0 / MD).then_inc(rooted, 1)
            for t in range(KT):
                act.wait_ge(turned, t + 1)
                if t >= 2:
                    act.wait_ge(taken, t - 1)
                act.activation(tmp[:, t % 2, :], banks[t % 2][:], ACT.Copy, scale=c_norm[:, t:t + 1]).then_inc(scaled, 1)

        @block.vector
        def _(dve):
            dve.wait_ge(rooted, 1)
            dve.reciprocal(ss[:], ss[:])
            dve.drain()
            h3 = hsum[:].rearrange("p c (h n) -> p (c h) n", h=MH)
            dve.tensor_tensor(h3, h3, last(ss[:], MD), ALU.mult).then_inc(normed, 1)
            for t in range(KT):
                dve.wait_ge(scaled, t + 1)
                dve.scalar_tensor_tensor(out=out[:, t, :], in0=xcv[:, t, CTX:ALLTOK], scalar=c_skip[:, t:t + 1], in1=tmp[:, t % 2, :],
                                         op0=ALU.mult, op1=ALU.add).then_inc(taken, 1)
                dve.drain()
                dve.tensor_tensor(out[:, t, :], out[:, t, :], z[:, t, :], ALU.mult)

        @block.tensor
        def _(pe):
            pe.wait_ge(normed, 1)
            for t in range(KT):
                if t >= 2:
                    pe.wait_ge(scaled, t - 1)
                for i in range(NCH):
                    mm = pe.transpose(banks[t % 2][:, i * P:(i + 1) * P], hsum[:, i, t * P:(t + 1) * P], ident[:])
                mm.then_inc(turned, 1)


def mixer_mlstm(nc, a, c, L, x, tap):
    with Stage(nc, "ml") as st:
        xcv = st.sb("xcv", [P, KT, ALLTOK])
        z = st.sb("z", [P, KT, SEQ])
        q = st.sb("q", [P, KT, SEQ])
        hsum = st.sb("hsum", [P, NCH, D])
        with Stage(nc, "ml2") as s1:
            m = Parts()
            m.b, m.cc = s1.sb("b", [P, CHUNKS, 2, MH]), s1.sb("cc", [P, CHUNKS, 2, MH])
            lower = s1.sb("lower", [P, P])
            neg = [s1.sb(f"neg{d}", [P, P]) for d in range(2)]
            edge = [s1.sb(f"edge{d}", [P, P]) for d in range(2)]
            load(nc, "mlload", [(lower[:], a["lower"]), (neg[0][:], a["neg_later0"]), (neg[1][:], a["neg_later1"]),
                                (edge[0][:], a["edge0"]), (edge[1][:], a["edge1"])])
            xm = s1.sb("xm", [P, KT, ALLTOK])
            with Stage(nc, "ml3") as s2:
                h = s2.sb("h", [P, KT, ALLTOK])
                raw, gbias = s2.sb("raw", [P, CHUNKS, 16]), s2.sb("gbias", [P, 16])
                cw, cb = s2.sb("cw", [P, KT, 3]), s2.sb("cb", [P, KT, 1])
                load(nc, "mlload2", [(cw[:], a["c_conv"]), (cb[:], a["c_conv_b"]), (gbias[:, 0:8], broadcast_rows(a["c_bi"], 8)),
                                     (gbias[:, 8:16], broadcast_rows(a["c_bf"], 8))])
                pre_norm(nc, "ml", c, L, 0, x, h, SEQS)

                def conv(e, m_, b, banks, t):
                    for j, (t0, tw) in enumerate(SEQS):
                        ins = conv3(e, t[:, t0:t0 + tw], banks[0][j][:, 0:tw], lambda i: cw[:, m_, i:i + 1], tw)
                    return ins

                def keep(e, m_, b, banks, t):
                    e.activation(xcv[:, m_, :], t[:], ACT.Silu, bias=cb[:, m_, :])
                    for j, (t0, tw) in enumerate(SEQS):
                        ins = e.activation(xm[:, m_, t0:t0 + tw], banks[0][j][:, 0:tw], ACT.Copy)
                    return ins

                project(nc, "xm", a["w_c_xm"], [tiles(h, KT)], SEQS, [("vector", conv), ("scalar", keep)], unroll=4,
                        temps=lambda s, n: [s.sb(f"acc{i}", [P, ALLTOK]) for i in range(n)])
                project(nc, "mz", a["w_c_z"], [tiles(h, KT)], SEQS[1:],
                        [("scalar", lambda e, m_, b, banks, t: e.activation(z[:, m_, :], banks[0][0][:], ACT.Sigmoid))], unroll=4)
                token_major(nc, "mg", a["w_c_gates"], tiles(h, KT), [slice(i * P, (i + 1) * P) for i in range(CHUNKS)],
                            [("vector", lambda e, n, r, bank, t: e.tensor_copy(raw[:, r, :], bank))])
                mlstm_gates(nc, "mgates", raw, gbias, (c.upper, lower), m, c.one)
            tap("xcv", xcv)
            tap("m_cc", m.cc)
            k = s1.sb("k", [P, KT, SEQ])
            ktok = xm[:].rearrange("p k t -> p (k t)").rearrange("p (c n) -> p c n", c=CHUNKS)
            vtok = s1.sb("vtok", [P, CHUNKS, MH, MD + 1])
            with Stage(nc, "ml4") as s2:
                mask = s2.sb("mask", [P, P])
                ws = []
                compact = [s2.sb(f"compact{i}", [P, KT, 4]) for i in range(3)]
                load(nc, "mlload3", [(mask[:], a["block4"])] + [(compact[i][:], a[n]) for i, n in enumerate(("c_wq", "c_wk", "c_wv"))])
                for i in range(3):
                    ws.append(s2.sb(f"w{i}", [P, KT, P]))
                    expand_blocks(nc, f"expand{i}", compact[i], mask, ws[i])
                mlstm_heads(nc, "mheads", xm, xcv, *ws, q, k, ktok, vtok, None)
            mlstm_scan(nc, "mscan", m, q, k, ktok, vtok, hsum, c.ident, neg, edge)
        tap("hsum", hsum)
        cn, ck = st.sb("cn", [P, KT]), st.sb("ck", [P, KT])
        load(nc, "mlload4", [(cn[:], a["c_norm"]), (ck[:], a["c_skip"])])
        mlstm_out(nc, "mout", hsum, xcv, z, cn, ck, q, c.ident, c.eps)
        y = st.sb("y", [P, KT, ALLTOK])
        down(nc, "mlout", a["w_c_out"], tiles(q, KT), y, SEQS[1:], CTX)
        post_norm(nc, "mlp", c, L, 2, x, y, SEQS[1:])


class Constants:
    pass


def build(nc, a, out, tap=lambda name, buf: None, start=0):
    Stage.number[0] = 0
    with Stage(nc, "whole") as st:
        c = Constants()
        pairs = []

        def const(name, shape):
            buf = st.sb(name, shape)
            pairs.append((buf[:], a[name]))
            return buf

        c.ident, c.flip, c.one, c.upper, c.neg_lower = (
            const(n, [P, P]) for n in ("ident", "flip", "one", "upper", "neg_lower"))
        c.eps_buf = const("eps", [P, 1])
        c.eps = c.eps_buf[:, 0:1]
        c.norm1, c.norm2 = const("norm1_w", [P, KT]), const("norm2_w", [P, KT])
        c.final = const("final_norm_w", [P, KT])
        c.ssm_norm = const("ssm_norm_w", [P, 16])
        c.conv_w, c.conv_b = const("conv_w", [P, 24, 4]), const("conv_b", [P, 24, 1])
        streams = st.sb("streams", [P, KT, ALLTOK])
        x = streams[:, :, CTX:ALLTOK]
        pairs += [(x, a["x"]), (streams[:, :, 0:CTX], a["ctx"])]
        load(nc, "load", pairs)
        if start == 0:
            first_block(nc, a, x, c, tap)
        rms_norm(nc, "final", KT, SEQ, lambda k: x[:, k, :], lambda k: x[:, k, :], c.one, c.eps,
                 gain=lambda k: c.final[:, k:k + 1])
        second_block(nc, a, c, streams, tap)
        with Stage(nc, "store") as last_stage:
            stored = last_stage.sem("stored")
            block = last_stage.cs.enter_context(nc.Block())

            @block.sync
            def _(sp):
                sp.dma_start(out, x).then_inc(stored, 16)
                sp.wait_ge(stored, 16)


def chan(v, extra=()):
    import numpy as np
    return np.ascontiguousarray(np.moveaxis(v.reshape(-1, P, *v.shape[1:]), 1, 0))


def by_tile(w, width=P):
    import numpy as np
    K, M = w.shape
    return np.ascontiguousarray(w.reshape(K // P, P, M // width, width).transpose(2, 1, 0, 3)).reshape(M // width, P, -1)


def shape_constants():
    import numpy as np
    i = np.arange(P)
    c = {"ident": np.eye(P), "flip": np.eye(P)[::-1], "one": np.ones((P, P)), "upper": i[:, None] <= i[None, :],
         "neg_lower": np.where(i[:, None] > i[None, :], NEG, 0.0), "eps": np.full((P, 1), EPS),
         "neg_row": np.ones((1, 3 * HEADS))}

    def bucket(dist):
        f = np.maximum(dist, 1).astype(np.float32)
        large = 16 + (np.log(f / np.float32(16)) / np.float32(np.log(128.0)) * np.float32(16)).astype(np.int32)
        return np.where(dist < 16, dist, np.minimum(large, 31))

    u = P - 1 - np.arange(2 * P)
    hot = np.zeros((33, TABLES, 2 * P))
    for t in range(TABLES):
        if t < 2 * DIL - 1:
            s, ok, dil = DIL * u + DIL - 1 - t, True, 1
        elif t == 2 * DIL - 1:
            s, ok, dil = u, True, DIL
        else:
            s, ok, dil = u // 4, u % 4 == 0, 16
        ok = ok & (s >= 0) & (s <= P)
        b = bucket(np.where(ok, s, 0) * dil)
        for w in range(2 * P):
            hot[b[w] if ok[w] else 32, t, w] = 1.0 if ok[w] else NEG
    c["bias_onehot"] = hot
    before, same = i[:, None] < i[None, :], i[:, None] == i[None, :]
    c["lower"] = i[:, None] >= i[None, :]
    c["blk64"] = i[:, None] // 64 == i[None, :] // 64
    c["block4"] = i[:, None] // 4 == i[None, :] // 4
    c["ln_eps"] = np.full((P, 1), LN_EPS)
    c["neg_later0"] = np.where(before, NEG, 0.0)
    c["neg_later1"] = np.where(before.T, NEG, 0.0)
    c["edge0"], c["edge1"] = (np.broadcast_to((i == e)[:, None], (P, P)) for e in (P - 1, 0))
    strict = np.zeros((P, 2, 2, 2 * P))
    for d, bf in enumerate((before, before.T)):
        for s, sign in enumerate((1.0, -1.0)):
            strict[:, d, s] = sign * np.concatenate([bf, bf | same], axis=1)
    c["strict"] = strict.reshape(P, 2, 4 * P)

    def level(m):
        return (i[:, None] // (2 * m) == i[None, :] // (2 * m)) & (i[:, None] // m % 2 == 1) & (i[None, :] // m % 2 == 0)

    c["x1"] = np.stack([np.stack([-1.0 * level(1), 1.0 * level(1).T]), np.stack([-1.0 * level(1).T, 1.0 * level(1)])]).transpose(2, 0, 1, 3)
    levels = np.stack([np.stack([level(m), level(m).T]) for m in (2, 4, 8, 16, 32, 64)], axis=1).transpose(2, 0, 1, 3)
    c["levels"] = levels
    return {n: np.ascontiguousarray(v, np.float32) for n, v in c.items()}


def lay_out(i):
    import numpy as np
    f = {n: np.asarray(v) for n, v in i.items()}
    w = f["w_in"][0]
    cut = np.cumsum([1536, 1536, 1536, 2048, 3072, 32])
    a = {
        "x": chan(np.ascontiguousarray(f["x"][0].T)),
        "norm1_w": chan(f["norm1_w"][0]), "norm2_w": chan(f["norm2_w"][0]), "final_norm_w": chan(f["final_norm_w"]),
        "ssm_norm_w": chan(f["ssm_norm_w"][0]),
        "conv_w": chan(np.ascontiguousarray(f["conv_w"][0].T)), "conv_b": chan(f["conv_b"][0][:, None]),
        "dt_bias": f["dt_bias"][0], "a_log": f["a_log"][0], "d_skip": f["d_skip"][0], "rel_bias": f["rel_bias"],
        "w_qk": by_tile(w[:, :cut[1]]), "w_v": by_tile(w[:, cut[1]:cut[2]], 512), "w_z": by_tile(w[:, cut[2]:cut[3]], 512),
        "w_xbc": by_tile(w[:, cut[3]:cut[4]]), "w_dt": by_tile(w[:, cut[4]:cut[5]], 32),
        "w_merge": np.concatenate([by_tile(w[:, cut[5]:cut[5] + D]), by_tile(w[:, cut[5] + D:]),
                                   by_tile(f["w_attn_branch"][0]), by_tile(f["w_ssm_branch"][0])], axis=2),
        "w_out": by_tile(f["w_out"][0]),
        "w_ffn_in": np.concatenate([by_tile(f["w_ffn_in"][0][:, :2816]), by_tile(f["w_ffn_in"][0][:, 2816:])], axis=2),
        "w_ffn_out": by_tile(f["w_ffn_out"][0]),
    }
    a["ctx"] = chan(np.ascontiguousarray(f["ctx_2"][0].T))
    a["cvec"] = np.ascontiguousarray(np.stack([chan(f["c_ctx_2"]), chan(f["c_2"][0])], axis=2))
    for i in range(2):
        a[f"w_ada{i}"] = by_tile(f["ada_w_2"][i])
        a[f"ada_b{i}"] = np.repeat(chan(f["ada_b_2"][i])[:, :, None], 2, axis=2)
        for n in ("norm_mix_pre", "norm_mix_post", "norm_ffn_pre", "norm_ffn_post"):
            a[f"{n}{i}"] = chan(f[n + "_2"][i])
        up = f["ffn_up_2"][i]
        a[f"w_ffn_up{i}"] = np.concatenate([by_tile(up[:, :2816]), by_tile(up[:, 2816:])], axis=2)
        a[f"w_ffn_down{i}"] = by_tile(f["ffn_down_2"][i])
        a[f"ffn_conv{i}"] = chan(np.ascontiguousarray(f["ffn_conv_2"][i].reshape(9, -1).T))
        a[f"ffn_conv_b{i}"] = chan(f["ffn_conv_b_2"][i][:, None])
    w = f["ab_w_in_2"][0]
    a["w_ab_u"], a["w_ab_v"] = by_tile(w[:, :512]), by_tile(w[:, 512:1024], 512)
    a["w_ab_rkv"], a["w_ab_lora"], a["w_ab_out"] = by_tile(w[:, 1024:2560]), by_tile(w[:, 2560:]), by_tile(f["ab_w_out_2"][0])
    a["b_shift"] = chan(np.ascontiguousarray(f["b_shift_2"][0].T))
    a["a_ws"] = np.ascontiguousarray(f["a_ws_2"][0].transpose(2, 0, 1))
    a["a_bs"], a["a_gv"] = f["a_bs_2"][0].reshape(-1), f["a_gv_2"][0].reshape(-1)
    a["b_w_up"], a["b_a_up"] = f["b_w_up_2"][0].reshape(P, 512), f["b_a_up_2"][0].reshape(P, 512)
    a["b_g_up"] = f["b_g_up_2"][0]
    for n in ("b_w0", "b_a0"):
        a[n] = np.ascontiguousarray(f[n + "_2"][0].reshape(2, 4, P).transpose(2, 0, 1))
    for n in ("b_ka", "b_kk", "b_rk", "b_ln_g", "b_ln_b", "c_norm", "c_skip"):
        a[n] = chan(f[n + "_2"][0].reshape(-1))
    w = f["c_w_in_2"][0]
    a["w_c_xm"], a["w_c_z"], a["w_c_gates"] = by_tile(w[:, :D]), by_tile(w[:, D:2 * D]), by_tile(w[:, 2 * D:], 16)
    a["w_c_out"] = by_tile(f["c_w_out_2"][0])
    a["c_conv"], a["c_conv_b"] = chan(np.ascontiguousarray(f["c_conv_2"][0].T)), chan(f["c_conv_b_2"][0][:, None])
    a["c_bi"], a["c_bf"] = f["c_bi_2"][0].reshape(-1), f["c_bf_2"][0].reshape(-1)
    for n in ("c_wq", "c_wk", "c_wv"):
        a[n] = chan(f[n + "_2"][0].reshape(D, 4))
    return {n: np.ascontiguousarray(v) for n, v in a.items()}


SCRATCH = {"line_scratch": (HEADS, TABLES, 2 * P)}
OUT = (P, KT, SEQ)


def kernel(**inputs):
    import numpy as np
    import concourse.bacc as bacc
    from concourse.bass_utils import run_bass_kernel_spmd

    nc = bacc.Bacc("TRN2", target_bir_lowering=False, num_devices=1)
    arrays = {**lay_out(inputs), **shape_constants()}
    aps = {n: nc.dram_tensor(f"in_{n}", v.shape, mybir.dt.from_np(v.dtype), kind="ExternalInput").ap() for n, v in arrays.items()}
    aps.update({n: nc.dram_tensor(n, s, F32, kind="Internal").ap() for n, s in SCRATCH.items()})
    out = nc.dram_tensor("out", OUT, F32, kind="ExternalOutput").ap()
    build(nc, aps, out)
    r = run_bass_kernel_spmd(nc, [{f"in_{n}": v for n, v in arrays.items()}], core_ids=[0])
    y = r.results[0]["out"]
    return np.ascontiguousarray(np.moveaxis(y, 1, 0).reshape(D, SEQ).T)[None]
```

```python
from contextlib import ExitStack

import concourse.bass as bass
from concourse import mybir

P = 128
F32 = mybir.dt.float32
F32R = mybir.dt.float32r
ALU = mybir.AluOpType
ACT = mybir.ActivationFunctionType
AX = mybir.AxisListType
NEG = -1e30

D, SEQ, CTX = 1024, 512, 256
KT = D // P
ALLTOK = CTX + SEQ
NCH = SEQ // P
EPS = 1e-6


def broadcast_rows(row, n):
    return bass.AP(tensor=row.tensor, offset=row.offset, ap=[[0, P], [1, n]])


def middle(ap, n):
    return bass.AP(tensor=ap.tensor, offset=ap.offset, ap=[ap.ap[0], [0, n], ap.ap[1]])


def last(ap, n):
    return bass.AP(tensor=ap.tensor, offset=ap.offset, ap=[ap.ap[0], ap.ap[1], [0, n]])


class Stage:

    number = [0]

    def __init__(self, nc, name):
        self.nc, self.name, self.cs, self.sems = nc, name, ExitStack(), []

    def __enter__(self):
        self.cs.__enter__()
        return self

    def __exit__(self, *e):
        self.cs.__exit__(*e)
        if self.sems:
            self.nc.clear_and_free_semaphores(self.sems)

    def sb(self, name, shape, dt=F32):
        return self.cs.enter_context(self.nc.sbuf_tensor(f"{self.name}_{name}", shape, dt))

    def pb(self, name, width=512):
        return self.cs.enter_context(self.nc.psum_tensor(f"{self.name}_{name}", [P, width], F32))

    def sem(self, name):
        free = list(self.nc.free_semaphores)
        later = [n for n in free if n > Stage.number[0]]
        Stage.number[0] = min(later or free)
        self.sems.append(self.nc.alloc_semaphore(f"{self.name}_{name}", num=Stage.number[0]))
        return self.sems[-1]


class Split:

    def __init__(self, st, name, shape):
        self.hi, self.lo = st.sb(name + "_hi", shape, F32R), st.sb(name + "_lo", shape, F32R)

    def tiles(self, n):
        return [(self.hi[:, k, :], self.lo[:, k, :]) for k in range(n)]


def products(nc, name, w, pieces, banks, steps, unroll, temps=None, raw_slots=2, split=True, lo_engine="gpsimd", tall=P, extra=0):
    M, NP = w.shape[0], len(pieces)
    pw = w.shape[2] // NP
    sets = max(s for s in range(1, unroll + 1) if s * banks <= 8 and (unroll % s == 0 or unroll == M))
    assert M % unroll == 0 and pw * NP == w.shape[2], (name, M, unroll)
    groups, C = M // unroll, unroll * NP
    R = min(raw_slots, C)
    HS = 2
    AHEAD = NP + extra
    assert groups == 1 or (C % R == 0 and (C % HS == 0 or not split)), name
    with Stage(nc, name) as st:
        raw = st.sb("raw", [P, R, pw])
        if split:
            hi, lo = st.sb("hi", [P, HS, pw], F32R), st.sb("lo", [P, HS, pw], F32R)
        bank = [[st.pb(f"bank{s}_{i}") for i in range(banks)] for s in range(sets)]
        tmp = temps(st, sets) if temps else None
        raw_loaded = [st.sem(f"raw_loaded{r}") for r in range(R)]
        hi_made, lo_made = st.sem("hi_made"), st.sem("lo_made")
        piece_used = st.sem("piece_used")
        psum_free = st.sem("psum_free")
        done = [st.sem(f"step_done{s}") for s in range(len(steps) - 1)]
        block = st.cs.enter_context(nc.Block())
        raw_used, credit = (lo_made, 0) if split else (piece_used, HS)

        def over_groups(e, body):
            if groups > 1:
                with e.Fori(0, groups - 1) as i:
                    body(i, False)
            body(groups - 1, True)

        def make_hi(act, i, j):
            act.wait_ge(raw_loaded[j % R], i * (16 * (C // R)) + 16 * (j // R + 1))
            act.wait_ge(piece_used, i * C + (j + 1))
            act.activation(hi[:, j % HS, :], raw[:, j % R, :], ACT.Copy).then_inc(hi_made, 1)

        def make_lo(e, i, j):
            e.wait_ge(hi_made, i * C + (j + 1))
            e.tensor_tensor(lo[:, j % HS, :], raw[:, j % R, :], hi[:, j % HS, :].bitcast(F32), ALU.subtract).then_inc(lo_made, 1)

        @block.sync
        def _(sp):
            def fetch(i, j):
                m = i * unroll + j // NP
                sp.dma_start(raw[:, j % R, :], w[m][:, (j % NP) * pw:(j % NP + 1) * pw]).then_inc(raw_loaded[j % R], 16)

            for j in range(R):
                fetch(0, j)

            def body(i, end):
                for j in range(C - R if end else C):
                    sp.wait_ge(raw_used, i * C + (j + 1 + credit))
                    fetch(i, j + R)
            over_groups(sp, body)

        @block.tensor
        def _(pe):
            pe.nop().then_inc(piece_used, HS)

            def body(i, end):
                for b in range(unroll):
                    pe.wait_ge(psum_free, i * unroll + (b + 1))
                    for p, items in enumerate(pieces):
                        j = b * NP + p
                        if split:
                            pe.wait_ge(lo_made, i * C + (j + 1))
                        else:
                            pe.wait_ge(raw_loaded[j % R], i * (16 * (C // R)) + 16 * (j // R + 1))
                        for to, width, c0, c1, x, weights_move, start, stop in items:
                            out = bank[b % sets][to][0:tall, 0:width]
                            if split:
                                wh, wl, (xh, xl) = hi[:, j % HS, c0:c1], lo[:, j % HS, c0:c1], x
                                terms = [(wh, xh), (wh, xl), (wl, xh)]
                            else:
                                terms = [(raw[:, j % R, c0:c1], x)]
                            if weights_move:
                                terms = [(xx, ww) for ww, xx in terms]
                            for n, (stationary, moving) in enumerate(terms):
                                mm = pe.matmul(out, stationary, moving, start=start and n == 0, stop=stop and n == len(terms) - 1)
                        mm.then_inc(piece_used, 1)
            over_groups(pe, body)

        def engine_program(which):
            def program(e):
                if steps[-1][0] == which:
                    e.nop().then_inc(psum_free, sets)
                make = {"scalar": make_hi, lo_engine: make_lo}.get(which) if split else None
                if make:
                    for j in range(min(AHEAD, M * NP)):
                        make(e, 0, j)

                def body(i, end):
                    for b in range(unroll):
                        for j in range(b * NP + AHEAD, (b + 1) * NP + AHEAD):
                            if make and not (end and j >= C):
                                make(e, i, j)
                        for s, (who, f) in enumerate(steps):
                            if who == which:
                                if s == 0:
                                    e.wait_ge(piece_used, i * C + ((b + 1) * NP + HS))
                                else:
                                    e.wait_ge(done[s - 1], i * unroll + (b + 1))
                                ins = f(e, i * unroll + b, b, bank[b % sets], tmp and tmp[b % sets])
                                ins.then_inc(psum_free if s == len(steps) - 1 else done[s], 1)
                over_groups(e, body)
            return program

        working = {s[0] for s in steps} | ({"scalar", lo_engine} if split else set())
        for which, register in (("scalar", block.scalar), ("vector", block.vector), ("gpsimd", block.gpsimd)):
            if which in working:
                register(engine_program(which))


def project(nc, name, w, parts, cols, steps, unroll, per_piece=None, **kw):
    ks = [(q, k, x) for q, moving in enumerate(parts) for k, x in enumerate(moving)]
    per_piece = per_piece or len(parts[0])
    split = kw.get("split", True)
    pieces = []
    for n, (q, k, x) in enumerate(ks):
        if n % per_piece == 0:
            pieces.append([])
        o = (n % per_piece) * P
        for c, (t0, tw) in enumerate(cols):
            xs = tuple(z[:, t0:t0 + tw] for z in x) if split else x[:, t0:t0 + tw]
            pieces[-1].append((q * len(cols) + c, tw, o, o + P, xs, 0, k == 0, k == len(parts[q]) - 1))
    nested = lambda banks: [banks[q * len(cols):(q + 1) * len(cols)] for q in range(len(parts))]
    wrap = lambda f: lambda e, m, b, banks, t: f(e, m, b, nested(banks), t)
    products(nc, name, w, pieces, len(parts) * len(cols), [(who, wrap(f)) for who, f in steps], unroll, **kw)


def token_major(nc, name, w, src, rows, step, unroll, per_piece, engine="scalar", **kw):
    width = w.shape[2] // len(src)
    pieces = []
    for k, x in enumerate(src):
        if k % per_piece == 0:
            pieces.append([])
        o = (k % per_piece) * width
        for r, row in enumerate(rows):
            pieces[-1].append((r, width, o, o + width, tuple(z[:, row] for z in x), 1, k == 0, k == len(src) - 1))

    def all_rows(e, n, b, banks, t):
        for r in range(len(rows)):
            ins = step(e, n, r, banks[r][0:kw.get("tall", P), 0:width])
        return ins
    products(nc, name, w, pieces, len(rows), [(engine, all_rows)], unroll, **kw)


def split_up(nc, name, src, dst, n):
    with Stage(nc, name) as st:
        rounded = st.sem("rounded")
        block = st.cs.enter_context(nc.Block())

        @block.scalar
        def _(act):
            for k in range(n):
                act.activation(dst.hi[:, k, :], src[:, k, :], ACT.Copy).then_inc(rounded, 1)

        @block.vector
        def _(dve):
            for k in range(n):
                dve.wait_ge(rounded, k + 1)
                dve.tensor_tensor(dst.lo[:, k, :], src[:, k, :], dst.hi[:, k, :].bitcast(F32), ALU.subtract)


def rms_norm(nc, name, K, T, x, y, one, eps, gain=None, shift=None, residual=None):
    pair = y is not None and isinstance(y(0), tuple)
    with Stage(nc, name) as st:
        sq = st.sb("squares", [P, 2, T])
        rstd = st.sb("rstd", [P, T])
        tmp = st.sb("scaled", [P, 2, T])
        total = st.pb("total")
        squared, used, rooted, scaled, rounded = (st.sem(n) for n in ("squared", "square_used", "rooted", "scaled", "rounded"))
        block = st.cs.enter_context(nc.Block())

        @block.scalar
        def _(act):
            for k in range(K):
                if k >= 2:
                    act.wait_ge(used, k - 1)
                act.activation(sq[:, k % 2, :], x(k), ACT.Square).then_inc(squared, 1)
            act.wait_ge(used, K)
            act.activation(rstd[:], total[:, 0:T], ACT.Sqrt, bias=eps, scale=1.0 / (K * P)).then_inc(rooted, 1)
            if pair:
                for k in range(K):
                    act.wait_ge(scaled, k + 1)
                    if shift is None:
                        act.activation(y(k)[0], tmp[:, k % 2, :], ACT.Copy).then_inc(rounded, 1)
                    else:
                        act.activation(y(k)[0], tmp[:, k % 2, :], ACT.Identity, bias=shift(k)).then_inc(rounded, 1)

        @block.tensor
        def _(pe):
            for k in range(K):
                pe.wait_ge(squared, k + 1)
                mm = pe.matmul(total[:, 0:T], one[:], sq[:, k % 2, :], start=(k == 0), stop=(k == K - 1))
                mm.then_inc(used, 1)

        @block.vector
        def _(dve):
            def scale(k, to):
                return dve.scalar_tensor_tensor(out=to, in0=x(k), scalar=gain(k), in1=rstd[:], op0=ALU.mult, op1=ALU.mult)

            def rest(k):
                dve.wait_ge(rounded, k + 1)
                h = y(k)[0].bitcast(F32)
                if shift is None:
                    dve.tensor_tensor(y(k)[1], tmp[:, k % 2, :], h, ALU.subtract)
                else:
                    dve.scalar_tensor_tensor(out=y(k)[1], in0=tmp[:, k % 2, :], scalar=shift(k), in1=h,
                                             op0=ALU.add, op1=ALU.subtract)

            dve.wait_ge(rooted, 1)
            dve.reciprocal(rstd[:], rstd[:])
            dve.drain()
            for k in range(K):
                if pair:
                    scale(k, tmp[:, k % 2, :]).then_inc(scaled, 1)
                    if k >= 1:
                        rest(k - 1)
                        dve.drain()
                elif residual is None:
                    scale(k, y(k))
                else:
                    scale(k, tmp[:, k % 2, :])
                    dve.drain()
                    dve.tensor_tensor(residual(k), residual(k), tmp[:, k % 2, :], ALU.add)
            if pair:
                rest(K - 1)


HEADS, DH = 8, 64
DIL = 4
TABLES = 2 * DIL - 1 + 2


def bias_tables(nc, name, rel, onehot, neg_row, scratch, flip, table):
    with Stage(nc, name) as st:
        rel_sb = st.sb("rel", [33, 3 * HEADS])
        hot = st.sb("hot", [33, TABLES, 2 * P])
        line = st.sb("line", [HEADS, TABLES, 2 * P])
        shifted = st.sb("shifted", [P, 2, TABLES * P])
        banks = [st.pb(f"bank{i}") for i in range(TABLES // 2 + 1)]
        turned = [st.pb(f"turned{i}") for i in range(3)]
        loaded, made, copied, kept, flipped, taken = (
            st.sem(n) for n in ("loaded", "made", "copied", "kept", "flipped", "taken"))
        spread = [st.sem(f"spread{i}") for i in range(2)]
        block = st.cs.enter_context(nc.Block())
        W = TABLES * P // 3
        assert W <= 512

        @block.sync
        def _(sp):
            sp.dma_start(rel_sb[0:32, :], rel).then_inc(loaded, 16)
            sp.dma_start(rel_sb[32:33, :], neg_row).then_inc(loaded, 16)
            sp.dma_start(hot[:], onehot).then_inc(loaded, 16)
            sp.wait_ge(copied, TABLES)
            sp.dma_start(scratch, line[:]).then_inc(kept, 16)
            sp.wait_ge(kept, 16)
            for h in range(HEADS):
                if h >= 2:
                    sp.wait_ge(flipped, 3 * (h - 1))
                src = bass.AP(tensor=scratch.tensor, offset=scratch.offset + h * TABLES * 2 * P,
                              ap=[[1, P], [2 * P, TABLES], [1, P]])
                sp.dma_start(shifted[:, h % 2, :].rearrange("p (t n) -> p t n", t=TABLES), src).then_inc(spread[h % 2], 16)

        @block.tensor
        def _(pe):
            pe.wait_ge(loaded, 48)
            for t in range(TABLES):
                g = max(0, t - (TABLES - 3))
                pe.matmul(banks[t // 2][0:HEADS, (t % 2) * 2 * P:(t % 2 + 1) * 2 * P],
                          rel_sb[:, g * HEADS:(g + 1) * HEADS], hot[:, t, :], start=True, stop=True).then_inc(made, 1)
            for h in range(HEADS):
                pe.wait_ge(spread[h % 2], 16 * (h // 2 + 1))
                for i in range(3):
                    if h >= 1:
                        pe.wait_ge(taken, 3 * (h - 1) + i + 1)
                    pe.matmul(turned[i][:, 0:W], flip[:], shifted[:, h % 2, i * W:(i + 1) * W], start=True, stop=True).then_inc(flipped, 1)

        @block.vector
        def _(dve):
            for t in range(TABLES):
                dve.wait_ge(made, min(TABLES, t // 2 * 2 + 2))
                dve.tensor_copy(line[:, t, :], banks[t // 2][0:HEADS, (t % 2) * 2 * P:(t % 2 + 1) * 2 * P]).then_inc(copied, 1)
            for h in range(HEADS):
                for i in range(3):
                    dve.wait_ge(flipped, 3 * h + i + 1)
                    dve.tensor_copy(table[:, h, :, :].rearrange("p t n -> p (t n)")[:, i * W:(i + 1) * W], turned[i][:, 0:W]).then_inc(taken, 1)


def attention(nc, name, q, k, v, table, out, ident):
    units = [(h, r) for h in range(HEADS) for r in range(DIL)]
    NU, NK = len(units), SEQ + 2 * P
    with Stage(nc, name) as st:
        logits = st.sb("logits", [P, 2, NK])
        probs = st.sb("probs", [P, 2, NK])
        probs_t = st.sb("probs_t", [P, 2, NK])
        negmax = st.sb("negmax", [P, NU])
        den = st.sb("den", [P, NU])
        rden = st.sb("rden", [P, NU])
        score = [st.pb(f"score{i}", 1024) for i in range(2)]
        turned = st.pb("turned", 1024)
        outs = [st.pb(f"outs{i}") for i in range(2)]
        scored, biased, maxed, exped, normed, transposed, copied, mixed, stored = (
            st.sem(n) for n in ("scored", "biased", "maxed", "exped", "normed", "transposed", "copied", "mixed", "stored"))
        block = st.cs.enter_context(nc.Block())

        @block.tensor
        def _(pe):
            def scores(n):
                h, r = units[n]
                p0, t = DH * (h % 2), h // 2
                if n >= 2:
                    pe.wait_ge(biased, n - 1)
                for g in range(3):
                    qg = q[p0:p0 + DH, 4 * g + t, r * P:(r + 1) * P]
                    kg = k[p0:p0 + DH, 4 * g + t, :] if g == 0 else k[p0:p0 + DH, 4 * g + t, r * P:(r + 1) * P]
                    o = 0 if g == 0 else SEQ + (g - 1) * P
                    mm = pe.matmul(score[n % 2][:, o:o + (SEQ if g == 0 else P)], qg, kg, start=True, stop=True)
                mm.then_inc(scored, 1)

            def mix(n):
                h, r = units[n]
                pe.wait_ge(normed, n + 1)
                if n >= 1:
                    pe.wait_ge(copied, n)
                for t in range(NK // P):
                    mm = pe.transpose(turned[:, t * P:(t + 1) * P], probs[:, n % 2, t * P:(t + 1) * P], ident[:])
                mm.then_inc(transposed, 1)
                pe.wait_ge(copied, n + 1)
                pair = h // 2
                if h % 2 == 0 and r == 0 and pair >= 2:
                    pe.wait_ge(stored, pair - 1)
                for t in range(NK // P):
                    g = max(0, t - 3)
                    row = t if g == 0 else r
                    mm = pe.matmul(outs[pair % 2][DH * (h % 2):DH * (h % 2) + DH, r * P:(r + 1) * P],
                                   v[:, row, (g * HEADS + h) * DH:(g * HEADS + h + 1) * DH],
                                   probs_t[:, n % 2, t * P:(t + 1) * P], start=(t == 0), stop=(t == NK // P - 1))
                mm.then_inc(mixed, 1)

            scores(0)
            for n in range(NU):
                if n + 1 < NU:
                    scores(n + 1)
                mix(n)

        @block.vector
        def _(dve):
            def bias(n):
                h, r = units[n]
                dve.wait_ge(scored, n + 1)
                if n >= 2:
                    dve.wait_ge(exped, n - 1)
                dve.scalar_tensor_tensor(out=logits[:, n % 2, 0:SEQ], in0=score[n % 2][:, 0:SEQ], scalar=DH ** -0.5,
                                         in1=table[:, h, DIL - 1 - r:2 * DIL - 1 - r, :].rearrange("p a b -> p (a b)"),
                                         op0=ALU.mult, op1=ALU.add)
                dve.scalar_tensor_tensor(out=logits[:, n % 2, SEQ:NK], in0=score[n % 2][:, SEQ:NK], scalar=DH ** -0.5,
                                         in1=table[:, h, 2 * DIL - 1:TABLES, :].rearrange("p a b -> p (a b)"),
                                         op0=ALU.mult, op1=ALU.add).then_inc(biased, 1)
                dve.drain()
                dve.tensor_reduce(negmax[:, n:n + 1], logits[:, n % 2, :], AX.X, ALU.max, negate=True).then_inc(maxed, 1)

            def normalise(n):
                dve.wait_ge(exped, n + 1)
                dve.reciprocal(rden[:, n:n + 1], den[:, n:n + 1])
                dve.drain()
                dve.tensor_scalar(probs[:, n % 2, :], probs[:, n % 2, :], rden[:, n:n + 1], None, ALU.mult).then_inc(normed, 1)

            for n in range(NU + 1):
                if n < NU:
                    bias(n)
                if n >= 1:
                    normalise(n - 1)

        @block.scalar
        def _(act):
            def exp(n):
                act.wait_ge(maxed, n + 1)
                if n >= 2:
                    act.wait_ge(transposed, n - 1)
                act.activation(probs[:, n % 2, :], logits[:, n % 2, :], ACT.Exp, bias=negmax[:, n:n + 1],
                               accum_out=den[:, n:n + 1]).then_inc(exped, 1)

            def copy(n):
                act.wait_ge(transposed, n + 1)
                if n >= 2:
                    act.wait_ge(mixed, n - 1)
                act.activation(probs_t[:, n % 2, 0:SEQ], turned[:, 0:SEQ], ACT.Copy)
                act.activation(probs_t[:, n % 2, SEQ:NK], turned[:, SEQ:NK], ACT.Copy).then_inc(copied, 1)
                if n % (2 * DIL) == 2 * DIL - 1:
                    pair = n // (2 * DIL)
                    act.wait_ge(mixed, n + 1)
                    act.activation(out[:, pair, :].rearrange("p (i r) -> p r i", r=DIL),
                                   outs[pair % 2][:].rearrange("p (r i) -> p r i", r=DIL), ACT.Copy).then_inc(stored, 1)

            for n in range(NU + 1):
                if n < NU:
                    exp(n)
                if n >= 1:
                    copy(n - 1)


GROUPS, GH, SHD, NSTATE = 4, 8, 64, 128
GW = GH * SHD
SH = GROUPS * GH


def ssd_decays(nc, name, d, dt_raw, dt_bias, a_log, d_skip, one, upper):
    CH = NCH * SH
    with Stage(nc, name) as st:
        bias_sb, alog_sb = (st.sb(n, [P, SH]) for n in ("dt_bias", "a_log"))
        raw, soft = (st.sb(n, [P, CH]) for n in ("raw", "soft"))
        la_ps, last_ps = st.pb("la"), st.pb("last")
        loaded, absd, softened, raised, cumd, prepared = (
            st.sem(n) for n in ("loaded", "absd", "softened", "raised", "cumd", "prepared"))
        block = st.cs.enter_context(nc.Block())

        @block.sync
        def _(sp):
            for dst, src in ((bias_sb, dt_bias), (alog_sb, a_log), (d.skip, d_skip)):
                sp.dma_start(dst[:], broadcast_rows(src, SH)).then_inc(loaded, 16)

        @block.vector
        def _(dve):
            dve.wait_ge(loaded, 48)
            dve.tensor_tensor(raw[:].rearrange("p (c h) -> p c h", c=NCH), dt_raw[:],
                              middle(bias_sb[:], NCH), ALU.add).then_inc(absd, 1)
            dve.wait_ge(softened, 1)
            dve.scalar_tensor_tensor(out=d.dt[:], in0=raw[:], scalar=0.0, in1=soft[:], op0=ALU.max, op1=ALU.add)
            dve.drain()
            dve.scalar_tensor_tensor(out=d.dta[:].rearrange("p (c h) -> p c h", c=NCH),
                                     in0=d.dt[:].rearrange("p (c h) -> p c h", c=NCH), scalar=-1.0,
                                     in1=middle(alog_sb[:], NCH), op0=ALU.mult, op1=ALU.mult).then_inc(raised, 1)
            dve.wait_ge(cumd, 1)
            dve.tensor_scalar(d.negla[:], la_ps[:, 0:CH], -1.0, None, ALU.mult)
            dve.drain()
            dve.tensor_tensor(raw[:], last_ps[:, 0:CH], d.negla[:], ALU.add).then_inc(prepared, 1)
            dve.wait_ge(softened, 2)
            dve.tensor_tensor(d.toend[:], d.toend[:], d.dt[:], ALU.mult)

        @block.scalar
        def _(act):
            act.wait_ge(loaded, 48)
            act.activation(alog_sb[:], alog_sb[:], ACT.Exp)
            act.wait_ge(absd, 1)
            act.activation(soft[:], raw[:], ACT.Abs)
            act.drain()
            act.activation(soft[:], soft[:], ACT.Exp, scale=-1.0)
            act.drain()
            act.activation(soft[:], soft[:], ACT.Ln, bias=one[:, 0:1]).then_inc(softened, 1)
            act.wait_ge(prepared, 1)
            act.activation(d.expla[:], la_ps[:, 0:CH], ACT.Exp)
            act.activation(d.elast[:], last_ps[:, 0:CH], ACT.Exp)
            act.activation(d.toend[:], raw[:], ACT.Exp).then_inc(softened, 1)

        @block.tensor
        def _(pe):
            pe.wait_ge(raised, 1)
            pe.matmul(la_ps[:, 0:CH], upper[:], d.dta[:], start=True, stop=True)
            pe.matmul(last_ps[:, 0:CH], one[:], d.dta[:], start=True, stop=True).then_inc(cumd, 1)


def ssd_scan(nc, name, d, x, bc, z, norm_w, ident, upper, neg_lower, eps):
    units = [(c, g) for c in range(NCH) for g in range(GROUPS)]
    NU = len(units)
    BM, CM = 0, GROUPS
    TPG = GW // P
    with Stage(nc, name) as st:
        state = st.sb("state", [P, GROUPS, GW])
        xtok = st.sb("xtok", [P, 2, GW])
        xend = st.sb("xend", [P, GW])
        btok = st.sb("btok", [P, 2, P])
        cbt = st.sb("cbt", [P, P])
        decay = st.sb("decay", [P, GH, P])
        mix = st.sb("mix", [P, GH, P])
        y, t1 = st.sb("y", [P, GW]), st.sb("t1", [P, GW])
        sq = st.sb("sq", [P, GW])
        ss, rstd = st.sb("ss", [P, NU]), st.sb("rstd", [P, NU])
        xturn, bturn, la0, la1, yin, yst, upd, yturn = (
            st.pb(n) for n in ("xturn", "bturn", "la0", "la1", "yin", "yst", "upd", "yturn"))
        las = (la0, la1)
        names = ("turned", "tokens", "spread", "decayed", "mixed", "ended", "produced", "gated", "squared",
                 "rooted", "normed", "turned_back", "stored", "stated")
        (turned, tokens, spread, decayed, mixed, ended, produced, gated, squared,
         rooted, normed, turned_back, stored, stated) = (st.sem(n) for n in names)
        block = st.cs.enter_context(nc.Block())

        @block.tensor
        def _(pe):
            for n, (c, g) in enumerate(units):
                ts = slice(c * P, (c + 1) * P)
                if n >= 1:
                    pe.wait_ge(tokens, n)
                    pe.wait_ge(mixed, n)
                    pe.wait_ge(decayed, n)
                for t in range(TPG):
                    pe.transpose(xturn[:, t * P:(t + 1) * P], x[:, TPG * g + t, ts], ident[:])
                pe.transpose(bturn[:, 0:P], bc[:, BM + g, ts], ident[:])
                pe.matmul(bturn[:, P:2 * P], bc[:, BM + g, ts], bc[:, CM + g, ts], start=True, stop=True).then_inc(turned, 1)
                for h in range(GH):
                    bank = las[h // 4][:, (h % 4) * P:(h % 4 + 1) * P]
                    col = d.dta[:, c * SH + g * GH + h:c * SH + g * GH + h + 1]
                    pe.matmul(bank, col.to_broadcast([P, P]), upper[:], start=True, stop=False)
                    mm = pe.matmul(bank, ident[:], neg_lower[:], start=False, stop=True)
                mm.then_inc(spread, 1)
                if n >= 1:
                    pe.wait_ge(gated, n)
                    pe.wait_ge(stated, n)
                pe.wait_ge(mixed, n + 1)
                for h in range(GH):
                    pe.matmul(yin[:, h * SHD:(h + 1) * SHD], mix[:, h, :], xtok[:, n % 2, h * SHD:(h + 1) * SHD],
                              start=True, stop=True)
                if c >= 1:
                    pe.matmul(yst[:], bc[:, CM + g, ts], state[:, g, :], start=True, stop=True)
                pe.wait_ge(ended, n + 1)
                pe.matmul(upd[:], btok[:, n % 2, :], xend[:], start=True, stop=True).then_inc(produced, 1)
                pe.wait_ge(normed, n + 1)
                if n >= 1:
                    pe.wait_ge(stored, n)
                for t in range(TPG):
                    mm = pe.transpose(yturn[:, t * P:(t + 1) * P], y[:, t * P:(t + 1) * P], ident[:])
                mm.then_inc(turned_back, 1)

        @block.scalar
        def _(act):
            for n, (c, g) in enumerate(units):
                act.wait_ge(turned, n + 1)
                if n >= 2:
                    act.wait_ge(produced, n - 1)
                act.activation(xtok[:, n % 2, :], xturn[:], ACT.Copy)
                act.activation(btok[:, n % 2, :], bturn[:, 0:P], ACT.Copy).then_inc(tokens, 1)
                act.wait_ge(spread, n + 1)
                if n >= 1:
                    act.wait_ge(mixed, n)
                for h in range(GH):
                    col = c * SH + g * GH + h
                    ins = act.activation(decay[:, h, :], las[h // 4][:, (h % 4) * P:(h % 4 + 1) * P], ACT.Exp,
                                         bias=d.negla[:, col:col + 1])
                ins.then_inc(decayed, 1)
                act.wait_ge(gated, n + 1)
                act.activation(sq[:], t1[:], ACT.Square, accum_out=ss[:, n:n + 1]).then_inc(squared, 1)
                act.drain()
                act.activation(rstd[:, n:n + 1], ss[:, n:n + 1], ACT.Sqrt, bias=eps, scale=1.0 / GW).then_inc(rooted, 1)
                act.wait_ge(turned_back, n + 1)
                for t in range(TPG):
                    ins = act.activation(x[:, TPG * g + t, c * P:(c + 1) * P], yturn[:, t * P:(t + 1) * P], ACT.Copy,
                                         scale=norm_w[:, TPG * g + t:TPG * g + t + 1])
                ins.then_inc(stored, 1)

        @block.vector
        def _(dve):
            dve.memset(state[:], 0.0)
            dve.drain()
            for n, (c, g) in enumerate(units):
                h0 = c * SH + g * GH
                by_head = lambda ap: ap.rearrange("p (h d) -> p h d", h=GH)
                dve.wait_ge(tokens, n + 1)
                dve.wait_ge(decayed, n + 1)
                for h in range(GH):
                    ins = dve.scalar_tensor_tensor(out=mix[:, h, :], in0=decay[:, h, :], scalar=d.dt[:, h0 + h:h0 + h + 1],
                                                   in1=bturn[:, P:2 * P], op0=ALU.mult, op1=ALU.mult)
                ins.then_inc(mixed, 1)
                dve.tensor_tensor(by_head(xend[:]), by_head(xtok[:, n % 2, :]), last(d.toend[:, h0:h0 + GH], SHD),
                                  ALU.mult).then_inc(ended, 1)
                dve.wait_ge(produced, n + 1)
                sg = by_head(state[:, g, :])
                if c >= 1:
                    dve.tensor_tensor(by_head(t1[:]), by_head(yst[:]), last(d.expla[:, h0:h0 + GH], SHD), ALU.mult)
                    dve.tensor_tensor(sg, sg, last(d.elast[:, h0:h0 + GH], SHD), ALU.mult)
                    dve.drain()
                    dve.tensor_tensor(t1[:], t1[:], yin[:], ALU.add)
                else:
                    dve.tensor_copy(t1[:], yin[:])
                dve.tensor_tensor(state[:, g, :], state[:, g, :], upd[:], ALU.add).then_inc(stated, 1)
                if n >= 1:
                    dve.wait_ge(turned_back, n)
                dve.tensor_tensor(by_head(y[:]), by_head(xtok[:, n % 2, :]), last(d.skip[:, g * GH:(g + 1) * GH], SHD), ALU.mult)
                dve.drain()
                dve.tensor_tensor(t1[:], t1[:], y[:], ALU.add)
                dve.drain()
                dve.tensor_tensor(t1[:], t1[:], z[:, c, g * GW:(g + 1) * GW], ALU.mult).then_inc(gated, 1)
                dve.wait_ge(rooted, n + 1)
                dve.reciprocal(rstd[:, n:n + 1], rstd[:, n:n + 1])
                dve.drain()
                dve.tensor_scalar(y[:], t1[:], rstd[:, n:n + 1], None, ALU.mult).then_inc(normed, 1)


class Decays:
    def __init__(self, st):
        self.dt, self.dta, self.negla, self.expla, self.toend, self.elast = (
            st.sb(n, [P, NCH * SH]) for n in ("dt", "dta", "negla", "expla", "toend", "elast"))
        self.skip = st.sb("d_skip", [P, SH])


def load(nc, name, pairs):
    with Stage(nc, name) as st:
        loaded = st.sem("loaded")
        block = st.cs.enter_context(nc.Block())

        @block.sync
        def _(sp):
            for dst, src in pairs:
                sp.dma_start(dst, src).then_inc(loaded, 16)
            sp.wait_ge(loaded, 16 * len(pairs))


def tiles(buf, n, t0=0, t1=None):
    return [buf[:, k, t0:t1] for k in range(n)] if t1 else [buf[:, k, :] for k in range(n)]


def first_block(nc, a, x, c, tap):
    AT, QT = 12, 24

    def norm_of_x(name, xn, w):
        rms_norm(nc, name, KT, SEQ, lambda k: x[:, k, :], lambda k: (xn.hi[:, k, :], xn.lo[:, k, :]), c.one, c.eps,
                 gain=lambda k: w[:, k:k + 1])

    def add_to_x(e, m, b, banks, t):
        return e.tensor_tensor(x[:, m, :], x[:, m, :], banks[0][0][:], ALU.add)

    with Stage(nc, "mixer1") as mixer:
        attn_parts = Split(mixer, "attn", [P, HEADS * DH // P, SEQ])
        with Stage(nc, "att") as st:
            qk = st.sb("qk", [P, QT, SEQ])
            v = st.sb("v", [P, DIL, AT * P])
            with Stage(nc, "attin") as s2:
                xn = Split(s2, "xn", [P, KT, SEQ])
                norm_of_x("norm1", xn, c.norm1)
                project(nc, "qk", a["w_qk"], [xn.tiles(KT)], [(0, SEQ)],
                        [("vector", lambda e, m, b, banks, t: e.tensor_copy(
                            qk[:, m, :].rearrange("p (r i) -> p r i", r=DIL),
                            banks[0][0][:].rearrange("p (i r) -> p r i", r=DIL)))], unroll=4)
                token_major(nc, "v", a["w_v"], xn.tiles(KT), [slice(r, SEQ, DIL) for r in range(DIL)],
                            lambda e, n, r, bank: e.tensor_copy(v[:, r, n * 512:(n + 1) * 512], bank),
                            unroll=3, per_piece=2, engine="vector")
            tap("qk", qk)
            table = st.sb("table", [P, HEADS, TABLES, P])
            attn = st.sb("out", [P, HEADS * DH // P, SEQ])
            bias_tables(nc, "bias", a["rel_bias"], a["bias_onehot"], a["neg_row"], a["line_scratch"], c.flip, table)
            attention(nc, "attend", qk[:, 0:AT, :], qk[:, AT:QT, :], v, table, attn, c.ident)
            tap("attn", attn)
            split_up(nc, "attn_parts", attn, attn_parts, HEADS * DH // P)
        with Stage(nc, "ssm") as st:
            xn = Split(st, "xn", [P, KT, SEQ])
            norm_of_x("norm1b", xn, c.norm1)
            ssm = st.sb("ssm", [P, SH * SHD // P, SEQ])
            with Stage(nc, "ssmin") as s2:
                bc = s2.sb("bc", [P, 8, SEQ])
                z = s2.sb("z", [P, NCH, SH * SHD])
                dt_raw = s2.sb("dt_raw", [P, NCH, SH])
                d = Decays(s2)
                rows = [slice(i * P, (i + 1) * P) for i in range(NCH)]
                token_major(nc, "dt", a["w_dt"], xn.tiles(KT), rows,
                            lambda e, n, r, bank: e.tensor_copy(dt_raw[:, r, :], bank), unroll=1, per_piece=KT, engine="vector")
                ssd_decays(nc, "decays", d, dt_raw, a["dt_bias"], a["a_log"], a["d_skip"], c.one, c.upper)

                for part, w, buf, m0 in (("x", "w_x", ssm, 0), ("bc", "w_bc", bc, 16)):
                    def conv(e, m, b, banks, acc):
                        bank = banks[0][0]
                        e.tensor_scalar(acc[:], bank[:], c.conv_w[:, m + m0, 3:4], None, ALU.mult)
                        for j in range(1, 4):
                            e.drain()
                            ins = e.scalar_tensor_tensor(out=acc[:, j:SEQ], in0=bank[:, 0:SEQ - j],
                                                         scalar=c.conv_w[:, m + m0, 3 - j:4 - j], in1=acc[:, j:SEQ],
                                                         op0=ALU.mult, op1=ALU.add)
                        return ins

                    project(nc, part, a[w], [xn.tiles(KT)], [(0, SEQ)],
                            [("vector", conv),
                             ("scalar", lambda e, m, b, banks, acc: e.activation(buf[:, m, :], acc[:], ACT.Silu,
                                                                                bias=c.conv_b[:, m + m0, :]))],
                            unroll=4, temps=lambda s, n: [s.sb(f"acc{i}", [P, SEQ]) for i in range(n)])
                tap("xs", ssm)
                tap("bc", bc)
                token_major(nc, "z", a["w_z"], xn.tiles(KT), rows,
                            lambda e, n, r, bank: e.activation(z[:, r, n * 512:(n + 1) * 512], bank, ACT.Silu),
                            unroll=4, per_piece=2)
                ssd_scan(nc, "scan", d, ssm, bc, z, c.ssm_norm, c.ident, c.upper, c.neg_lower, c.eps)
            tap("ssm", ssm)
            merged = ssm[:, 0:KT, :]
            with Stage(nc, "merging") as s2:
                ssm_parts = Split(s2, "ssm", [P, SH * SHD // P, SEQ])
                split_up(nc, "ssm_parts", ssm, ssm_parts, SH * SHD // P)

                def gates(e, m, b, banks, t):
                    e.activation(t[0][:], banks[0][0][:], ACT.Sigmoid)
                    return e.activation(t[1][:], banks[1][0][:], ACT.Sigmoid)

                def merge(e, m, b, banks, t):
                    e.tensor_tensor(t[0][:], t[0][:], banks[2][0][:], ALU.mult)
                    e.tensor_tensor(t[1][:], t[1][:], banks[3][0][:], ALU.mult)
                    e.drain()
                    return e.tensor_tensor(merged[:, m, :], t[0][:], t[1][:], ALU.add)

                project(nc, "merge", a["w_merge"], [xn.tiles(KT), xn.tiles(KT), attn_parts.tiles(4), ssm_parts.tiles(16)],
                        [(0, SEQ)], [("scalar", gates), ("vector", merge)], unroll=2, per_piece=6,
                        temps=lambda s, n: [[s.sb(f"gate{i}_{j}", [P, SEQ]) for j in range(2)] for i in range(n)])
            with Stage(nc, "outs") as s2:
                merged_parts = Split(s2, "merged", [P, KT, SEQ])
                split_up(nc, "merged_parts", merged, merged_parts, KT)
                project(nc, "out", a["w_out"], [merged_parts.tiles(KT)], [(0, SEQ)], [("vector", add_to_x)], unroll=4)
    tap("h1", x)
    with Stage(nc, "ffn1") as st:
        hidden = Split(st, "hidden", [P, 22, SEQ])
        with Stage(nc, "ffn1in") as s2:
            xn = Split(s2, "xn", [P, KT, SEQ])
            norm_of_x("norm2", xn, c.norm2)
            project(nc, "up", a["w_ffn_in"], [xn.tiles(KT)] * 2, [(0, SEQ)],
                    [("scalar", lambda e, m, b, banks, t: e.activation(t[:], banks[0][0][:], ACT.Silu)),
                     ("vector", lambda e, m, b, banks, t: e.tensor_tensor(t[:], t[:], banks[1][0][:], ALU.mult)),
                     ("scalar", lambda e, m, b, banks, t: e.activation(hidden.hi[:, m, :], t[:], ACT.Copy)),
                     ("vector", lambda e, m, b, banks, t: e.tensor_tensor(
                         hidden.lo[:, m, :], t[:], hidden.hi[:, m, :].bitcast(F32), ALU.subtract))],
                    unroll=2, temps=lambda s, n: [s.sb(f"gate{i}", [P, SEQ]) for i in range(n)])
        project(nc, "down", a["w_ffn_out"], [hidden.tiles(22)], [(0, SEQ)], [("vector", add_to_x)], unroll=2, per_piece=11)
    tap("h2", x)


MOD = 6
SEQS = [(0, CTX), (CTX, SEQ)]
CHUNKS = ALLTOK // P
CTXCH = CTX // P
ORDER = [list(range(CHUNKS)), list(range(CTXCH))[::-1] + list(range(CTXCH, CHUNKS))[::-1]]
UNITS = [(d, ch) for d in range(2) for ch in ORDER[d]]


def modulations(nc, name, w, bias, cvec, ident, mods):
    N = w.shape[0]
    with Stage(nc, name) as st:
        rows = st.sb("rows", [2, N, 512])
        token_major(nc, name + "p", w, cvec.tiles(KT), [slice(0, 2)],
                    lambda e, n, r, bank: e.activation(rows[:, n, :], bank, ACT.Copy),
                    unroll=4, per_piece=2, raw_slots=8, lo_engine="vector", tall=2)
        with Stage(nc, name + "t") as s2:
            bank = s2.pb("bank")
            turned = s2.sem("turned")
            block = s2.cs.enter_context(nc.Block())

            @block.tensor
            def _(pe):
                for i in range(MOD * KT):
                    mm = pe.transpose(bank[:, 2 * i:2 * i + 2], rows[:, i // 4, i % 4 * P:(i % 4 + 1) * P], ident[0:2, 0:2])
                mm.then_inc(turned, 1)

            @block.vector
            def _(dve):
                dve.wait_ge(turned, 1)
                dve.tensor_tensor(mods[:], bank[:, 0:2 * MOD * KT].rearrange("p (i s) -> p i s", s=2), bias[:], ALU.add)


def modulation_gains(nc, name, layers):
    with Stage(nc, name) as st:
        block = st.cs.enter_context(nc.Block())

        @block.vector
        def _(dve):
            for L in layers:
                for i, pre, post in ((0, L.mix_pre, L.mix_post), (3, L.ffn_pre, L.ffn_post)):
                    scale, gate = (L.mods[:, (i + j) * KT:(i + j + 1) * KT, :] for j in (1, 2))
                    dve.scalar_tensor_tensor(out=scale, in0=scale, scalar=1.0, in1=last(pre[:], 2), op0=ALU.add, op1=ALU.mult)
                    dve.tensor_tensor(gate, gate, last(post[:], 2), ALU.mult)


def silu_columns(nc, name, buf):
    with Stage(nc, name) as st:
        block = st.cs.enter_context(nc.Block())

        @block.scalar
        def _(act):
            act.activation(buf, buf, ACT.Silu)


def conv3(e, out, x, w, n):
    e.tensor_scalar(out, x, w(1), None, ALU.mult)
    e.drain()
    e.scalar_tensor_tensor(out=out[:, 1:n], in0=x[:, 0:n - 1], scalar=w(0), in1=out[:, 1:n], op0=ALU.mult, op1=ALU.add)
    e.drain()
    return e.scalar_tensor_tensor(out=out[:, 0:n - 1], in0=x[:, 1:n], scalar=w(2), in1=out[:, 0:n - 1],
                                  op0=ALU.mult, op1=ALU.add)


def conv_grid(e, out, x, w):
    R, C = SEQ // 64, 64
    o3, x3 = (ap.rearrange("p (r c) -> p r c", c=C) for ap in (out, x))
    ins = e.tensor_scalar(out, x, w(1, 1), None, ALU.mult)
    for a in range(3):
        for b in range(3):
            if (a, b) == (1, 1):
                continue
            r0, r1 = max(0, 1 - a), min(R, R + 1 - a)
            c0, c1 = max(0, 1 - b), min(C, C + 1 - b)
            e.drain()
            o = o3[:, r0:r1, c0:c1]
            ins = e.scalar_tensor_tensor(out=o, in0=x3[:, r0 + a - 1:r1 + a - 1, c0 + b - 1:c1 + b - 1],
                                         scalar=w(a, b), in1=o, op0=ALU.mult, op1=ALU.add)
    return ins


def spatial_gate(nc, name, u, v, ws_t, bs, gv, out, eps):
    NG, NU = 4, 4 * CHUNKS
    with Stage(nc, name) as st:
        sq = st.sb("sq", [P, P])
        ss, rstd = st.sb("ss", [P, NU]), st.sb("rstd", [P, NU])
        banks = [[st.pb(f"z{i}_{j}") for j in range(2)] for i in range(2)]
        squared, normed, mixed, taken = (st.sem(n) for n in ("squared", "normed", "mixed", "taken"))
        block = st.cs.enter_context(nc.Block())

        @block.scalar
        def _(act):
            for n in range(NU):
                ch, g = n // NG, n % NG
                act.activation(sq[:], v[:, ch, g * P:(g + 1) * P], ACT.Square, accum_out=ss[:, n:n + 1])
                act.drain()
            act.activation(rstd[:], ss[:], ACT.Sqrt, bias=eps, scale=1.0 / P).then_inc(squared, 1)

        @block.vector
        def _(dve):
            dve.wait_ge(squared, 1)
            dve.reciprocal(rstd[:], rstd[:])
            dve.drain()
            for n in range(NU):
                ch, g = n // NG, n % NG
                vs = v[:, ch, g * P:(g + 1) * P]
                ins = dve.scalar_tensor_tensor(out=vs, in0=vs, scalar=rstd[:, n:n + 1], in1=gv[:, g * P:(g + 1) * P],
                                               op0=ALU.mult, op1=ALU.mult)
            ins.then_inc(normed, 1)
            for g in range(NG):
                dve.wait_ge(mixed, g + 1)
                for j, (c0, c1) in enumerate(((0, 4), (4, CHUNKS))):
                    o = out[:, g, c0 * P:c1 * P].rearrange("p (c q) -> p c q", q=P)
                    bank = banks[g % 2][j][:, 0:(c1 - c0) * P].rearrange("p (c q) -> p c q", q=P)
                    dve.tensor_tensor(o, bank, middle(bs[:, g * P:(g + 1) * P], c1 - c0), ALU.add)
                    dve.drain()
                    ins = dve.tensor_tensor(out[:, g, c0 * P:c1 * P], out[:, g, c0 * P:c1 * P], u[:, g, c0 * P:c1 * P], ALU.mult)
                ins.then_inc(taken, 1)

        @block.tensor
        def _(pe):
            pe.wait_ge(normed, 1)
            for g in range(NG):
                if g >= 2:
                    pe.wait_ge(taken, g - 1)
                for ch in range(CHUNKS):
                    mm = pe.matmul(banks[g % 2][ch // 4][:, (ch % 4) * P:(ch % 4 + 1) * P], v[:, ch, g * P:(g + 1) * P],
                                   ws_t[:, g, :], start=True, stop=True)
                mm.then_inc(mixed, 1)


DECAY_RATE = 0.6065306597126334


def rwkv_keys(nc, name, k, v, kk, vtok, b_kk, ident, blk, tiny):
    with Stage(nc, name) as st:
        sq = st.sb("sq", [P, 2, ALLTOK])
        norm = st.sb("norm", [P, 2, ALLTOK])
        sums = [[st.pb(f"sum{i}_{j}") for j in range(2)] for i in range(2)]
        turns = [st.pb(f"turn{i}") for i in range(2)]
        squared, summed, rooted, turned, copied = (st.sem(n) for n in ("squared", "summed", "rooted", "turned", "copied"))
        block = st.cs.enter_context(nc.Block())

        @block.vector
        def _(dve):
            for t in range(4):
                dve.tensor_scalar(kk[:, t, :], k[:, t, :], b_kk[:, t:t + 1], None, ALU.mult)
                dve.drain()
                dve.tensor_tensor(sq[:, t % 2, :], kk[:, t, :], kk[:, t, :], ALU.mult).then_inc(squared, 1)
                dve.wait_ge(summed, t + 1)
                for j, (t0, tw) in enumerate(SEQS):
                    ins = dve.tensor_scalar(norm[:, t % 2, t0:t0 + tw], sums[t % 2][j][:, 0:tw], 1e-12, None, ALU.max)
                ins.then_inc(rooted, 1)
                dve.wait_ge(copied, t + 1)
                dve.reciprocal(norm[:, t % 2, :], norm[:, t % 2, :])
                dve.drain()
                dve.tensor_tensor(kk[:, t, :], kk[:, t, :], norm[:, t % 2, :], ALU.mult)

        @block.tensor
        def _(pe):
            for t in range(4):
                pe.wait_ge(squared, t + 1)
                for j, (t0, tw) in enumerate(SEQS):
                    mm = pe.matmul(sums[t % 2][j][:, 0:tw], blk[:], sq[:, t % 2, t0:t0 + tw], start=True, stop=True)
                mm.then_inc(summed, 1)
            for ch in range(CHUNKS):
                if ch >= 2:
                    pe.wait_ge(copied, 4 + ch - 1)
                for t in range(4):
                    mm = pe.transpose(turns[ch % 2][:, t * P:(t + 1) * P], v[:, t, ch * P:(ch + 1) * P], ident[:])
                mm.then_inc(turned, 1)

        @block.scalar
        def _(act):
            for t in range(4):
                act.wait_ge(rooted, t + 1)
                act.activation(norm[:, t % 2, :], norm[:, t % 2, :], ACT.Sqrt).then_inc(copied, 1)
            for ch in range(CHUNKS):
                act.wait_ge(turned, ch + 1)
                act.activation(vtok[:, ch, :], turns[ch % 2][:], ACT.Copy).then_inc(copied, 1)


def rwkv_scan(nc, name, s):
    LEVELS = [2, 4, 8, 16, 32, 64]
    NL = len(LEVELS)
    NU = len(UNITS)
    with Stage(nc, name) as st:
        sig, aa, w0, w1, kd, qq, inv = (st.sb(n, [P, 4, P]) for n in ("sig", "aa", "w0", "w1", "kd", "qq", "inv"))
        pin, bb, bh, kh, stmp = sig, aa, aa, kd, inv
        half, hdec = st.sb("half", [P, 4, 1]), st.sb("hdec", [P, 4, 1])
        ar = st.sb("ar", [P, 4, 2, P])
        ktok, btok = st.sb("ktok", [P, 4, P]), st.sb("btok", [P, 4, P])
        kb = st.sb("kb", [P, 8, 4, P])
        X, XT, T = st.sb("X", [P, 8, P]), st.sb("XT", [P, 8, P]), st.sb("T", [P, 8, P])
        rhs, un = st.sb("rhs", [P, 512]), st.sb("un", [P, 512])
        state = st.sb("state", [P, 4, P])
        b = [st.pb(f"b{i}") for i in range(8)]
        names = ("lora", "gated", "centred", "exped", "prepared", "bonus_in", "bonus_out", "turned", "tokens", "scored",
                 "masked", "started", "t_ready", "t_copied", "x_ready", "x_taken", "rhs_ready", "rhs_copied",
                 "u_ready", "u_copied", "y_ready", "y_taken", "s_ready", "s_scaled", "s_taken", "keyed", "pooled", "kd_ready")
        S = {n: st.sem(n) for n in names}
        block = st.cs.enter_context(nc.Block())
        v4 = lambda bank: bank[:].rearrange("p (t n) -> p t n", t=4)

        @block.tensor
        def _(pe):
            for n, (d, ch) in enumerate(UNITS):
                cs, ds = slice(ch * P, (ch + 1) * P), slice(64 * d, 64 * d + 64)
                if n >= 1:
                    pe.wait_ge(S["x_taken"], 2 * NL * n)
                for t in range(4):
                    pe.matmul(b[0][:, t * P:(t + 1) * P], s.w_up[ds, t * P:(t + 1) * P], s.wd[ds, cs], start=True, stop=True)
                for t in range(4):
                    mm = pe.matmul(b[1][:, t * P:(t + 1) * P], s.a_up[ds, t * P:(t + 1) * P], s.ad[ds, cs], start=True, stop=True)
                mm.then_inc(S["lora"], 1)
                pe.wait_ge(S["bonus_in"], n + 1)
                if n >= 1:
                    pe.wait_ge(S["u_copied"], n)
                for t in range(4):
                    mm = pe.matmul(b[2][:, t * P:(t + 1) * P], s.blk_rk[:, t, :], qq[:, t, :], start=True, stop=True)
                mm.then_inc(S["bonus_out"], 1)
                pe.wait_ge(S["prepared"], n + 1)
                if n >= 1:
                    pe.wait_ge(S["y_taken"], n)
                    pe.wait_ge(S["s_taken"], n)
                for t in range(4):
                    pe.transpose(b[3][:, t * P:(t + 1) * P], kh[:, t, :], s.ident[:])
                for t in range(4):
                    mm = pe.transpose(b[4][:, t * P:(t + 1) * P], bh[:, t, :], s.ident[:])
                mm.then_inc(S["turned"], 1)
                for t in range(4):
                    if t == 0:
                        pe.wait_ge(S["keyed"], n + 1)
                    if t == 1:
                        pe.wait_ge(S["gated"], n + 1)
                    if t >= 2:
                        pe.wait_ge(S["masked"], 4 * n + t - 1)
                    for lhs, rhs_ap, bank, o in (
                            (kh, None, 0, 0), (bh, None, 0, 256), (None, bh, 1, t * P)):
                        for p in range(2):
                            ps = slice(64 * p, 64 * p + 64)
                            if bank == 0:
                                out, width = b[((5, 6), (0, 1))[t % 2][p]], 256
                                mm = pe.matmul(out[:, o:o + width], lhs[ps, t, :], ar[ps, t, :, :].rearrange("p a n -> p (a n)"),
                                               start=True, stop=True)
                            else:
                                mm = pe.matmul(b[(7, 2)[p]][:, o:o + P], ar[ps, t, 0, :], bh[ps, t, :], start=True, stop=True)
                    mm.then_inc(S["scored"], 1)
                for l in range(NL):
                    for g in range(2):
                        u = (n * NL + l) * 2 + g
                        if l == 0 and g == 0:
                            pe.wait_ge(S["tokens"], n + 1)
                            pe.wait_ge(S["masked"], 4 * n + 4)
                            pe.wait_ge(S["started"], n + 1)
                        if l >= 1:
                            pe.wait_ge(S["x_taken"], u - 1)
                        for h in range(4 * g, 4 * g + 4):
                            mm = pe.matmul(b[3 + g][:, (h % 4) * P:(h % 4 + 1) * P], kb[:, h, 2, :], X[:, h, :], start=True, stop=True)
                        mm.then_inc(S["t_ready"], 1)
                    for g in range(2):
                        u = (n * NL + l) * 2 + g
                        pe.wait_ge(S["t_copied"], u + 1)
                        xb, xtb = ((5, 6), (0, 1))[g]
                        if l < NL - 1:
                            for h in range(4 * g, 4 * g + 4):
                                pe.matmul(b[xb][:, (h % 4) * P:(h % 4 + 1) * P], XT[:, h, :], T[:, h, :], start=True, stop=True)
                        for h in range(4 * g, 4 * g + 4):
                            mm = pe.matmul(b[xtb][:, (h % 4) * P:(h % 4 + 1) * P], T[:, h, :], XT[:, h, :], start=True, stop=True)
                        mm.then_inc(S["x_ready"], 1)
                pe.wait_ge(S["s_scaled"], n + 1)
                for t in range(4):
                    pe.matmul(b[7][:, t * P:(t + 1) * P], ar[:, t, 0, :], state[:, t, :], start=True, stop=False, skip_group_check=True)
                    for h in (2 * t, 2 * t + 1):
                        mm = pe.matmul(b[7][:, h * 64:h * 64 + 64], kb[:, h, 0, :], s.vtok[:, ch, h * 64:h * 64 + 64],
                                       start=False, stop=True, skip_group_check=True)
                mm.then_inc(S["rhs_ready"], 1)
                pe.wait_ge(S["rhs_copied"], n + 1)
                pe.wait_ge(S["x_taken"], 2 * NL * (n + 1))
                for h in range(8):
                    mm = pe.matmul(b[2][:, h * 64:h * 64 + 64], XT[:, h, :], rhs[:, h * 64:h * 64 + 64], start=True, stop=True)
                mm.then_inc(S["u_ready"], 1)
                pe.wait_ge(S["u_copied"], n + 1)
                for t in range(4):
                    pe.matmul(b[3][:, t * P:(t + 1) * P], ar[:, t, 1, :], state[:, t, :], start=True, stop=False, skip_group_check=True)
                    for h in (2 * t, 2 * t + 1):
                        hs = slice(h * 64, h * 64 + 64)
                        pe.matmul(b[3][:, hs], kb[:, h, 1, :], s.vtok[:, ch, hs], start=False, stop=False, skip_group_check=True)
                        mm = pe.matmul(b[3][:, hs], kb[:, h, 3, :], un[:, hs], start=False, stop=True, skip_group_check=True)
                mm.then_inc(S["y_ready"], 1)
                for t in range(4):
                    ts = slice(t * P, (t + 1) * P)
                    pe.matmul(b[4][:, ts], ktok[:, t, :], s.vtok[:, ch, ts], start=True, stop=False)
                    mm = pe.matmul(b[4][:, ts], btok[:, t, :], un[:, ts], start=False, stop=True)
                mm.then_inc(S["s_ready"], 1)

        @block.scalar
        def _(act):
            for n, (d, ch) in enumerate(UNITS):
                act.wait_ge(S["lora"], n + 1)
                if n >= 1:
                    act.wait_ge(S["prepared"], n)
                for t in range(4):
                    act.activation(sig[:, t, :], b[0][:, t * P:(t + 1) * P], ACT.Sigmoid, bias=s.b_w0[:, d, t:t + 1])
                for t in range(4):
                    ins = act.activation(aa[:, t, :], b[1][:, t * P:(t + 1) * P], ACT.Sigmoid, bias=s.b_a0[:, d, t:t + 1])
                ins.then_inc(S["gated"], 1)
                act.wait_ge(S["centred"], n + 1)
                c = DECAY_RATE
                inc, exc, sgn = ((w0, w1, -c), (w1, w0, c))[d]
                act.activation(pin[:], inc[:], ACT.Exp, scale=sgn)
                act.activation(exc[:], exc[:], ACT.Exp, scale=sgn)
                act.activation(inv[:], inc[:], ACT.Exp, scale=-sgn)
                act.activation(hdec[:], half[:], ACT.Exp, scale=-c).then_inc(S["exped"], 1)
                act.wait_ge(S["turned"], n + 1)
                act.activation(ktok[:], v4(b[3]), ACT.Copy)
                act.activation(btok[:], v4(b[4]), ACT.Copy, scale=-1.0).then_inc(S["tokens"], 1)
                for l in range(NL):
                    for g in range(2):
                        u = (n * NL + l) * 2 + g
                        act.wait_ge(S["t_ready"], u + 1)
                        act.activation(T[:, 4 * g:4 * g + 4, :], v4(b[3 + g]), ACT.Copy).then_inc(S["t_copied"], 1)
                act.wait_ge(S["rhs_ready"], n + 1)
                act.activation(rhs[:], b[7][:], ACT.Copy).then_inc(S["rhs_copied"], 1)
                act.wait_ge(S["u_ready"], n + 1)
                act.activation(un[:], b[2][:], ACT.Copy).then_inc(S["u_copied"], 1)

        @block.gpsimd
        def _(pool):
            for n, (d, ch) in enumerate(UNITS):
                cs = slice(ch * P, (ch + 1) * P)
                pool.wait_ge(S["gated"], n + 1)
                if n >= 1:
                    pool.wait_ge(S["prepared"], n)
                pool.wait_ge(S["kd_ready"], n + 1)
                pool.tensor_tensor(bb[:], aa[:], s.kk[:, :, cs], ALU.mult)
                pool.tensor_tensor(kd[:], kd[:], s.k[:, :, cs], ALU.mult).then_inc(S["pooled"], 1)
                pool.wait_ge(S["pooled"], n + 1)
                if n >= 1:
                    pool.wait_ge(S["bonus_out"], n)
                pool.tensor_tensor(qq[:], kd[:], s.r[:, :, cs], ALU.mult).then_inc(S["bonus_in"], 1)

        @block.vector
        def _(dve):
            dve.memset(state[:], 0.0)
            for n, (d, ch) in enumerate(UNITS):
                cs = slice(ch * P, (ch + 1) * P)
                strict, X1, M = s.masks[d]
                dve.wait_ge(S["gated"], n + 1)
                for t in range(4):
                    ins = dve.tensor_scalar(kd[:, t, :], aa[:, t, :], s.b_ka[:, t:t + 1], s.one_ka[:, t:t + 1], ALU.mult, ALU.add)
                ins.then_inc(S["kd_ready"], 1)
                for t in range(4):
                    dve.tensor_tensor_scan(w0[:, t, :], s.one[:], sig[:, t, :], 0.0, ALU.mult, ALU.add)
                dve.drain()
                dve.tensor_scalar(half[:], w0[:, :, P - 1:P], 0.5, None, ALU.mult)
                dve.drain()
                dve.tensor_tensor(w0[:], w0[:], last(half[:, :, 0], P), ALU.subtract)
                dve.drain()
                dve.tensor_tensor(w1[:], w0[:], sig[:], ALU.subtract).then_inc(S["centred"], 1)
                dve.wait_ge(S["exped"], n + 1)
                if d == 0 and ch == 0:
                    pass
                elif ch == ORDER[d][0]:
                    dve.memset(state[:], 0.0)
                    dve.drain()
                dve.wait_ge(S["bonus_in"], n + 1)
                pex = (w1, w0)[d]
                dve.tensor_tensor(ar[:, :, 0, :], s.kk[:, :, cs], pex[:], ALU.mult)
                dve.tensor_tensor(ar[:, :, 1, :], s.r[:, :, cs], pin[:], ALU.mult)
                dve.tensor_tensor(kh[:], kd[:], inv[:], ALU.mult)
                dve.tensor_tensor(bh[:], bb[:], inv[:], ALU.mult).then_inc(S["prepared"], 1)
                dve.tensor_tensor(state[:], state[:], last(hdec[:, :, 0], P), ALU.mult).then_inc(S["s_scaled"], 1)
                dve.wait_ge(S["bonus_out"], n + 1)
                if d == 0:
                    dve.tensor_copy(s.bonus[:, :, cs], v4(b[2])).then_inc(S["keyed"], 1)
                else:
                    dve.tensor_tensor(s.bonus[:, :, cs], s.bonus[:, :, cs], v4(b[2]), ALU.add).then_inc(S["keyed"], 1)
                for t in range(4):
                    dve.wait_ge(S["scored"], 4 * n + t + 1)
                    for p in range(2):
                        ins = dve.tensor_tensor(kb[:, 2 * t + p, :, :].rearrange("p a n -> p (a n)"), b[((5, 6), (0, 1))[t % 2][p]][:],
                                                strict[:], ALU.mult)
                    ins.then_inc(S["masked"], 1)
                for p in range(2):
                    dve.tensor_tensor(X[:, p::2, :], v4(b[(7, 2)[p]]), middle(X1[:, 0, :], 4), ALU.mult)
                dve.drain()
                dve.tensor_tensor(X[:], X[:], middle(s.ident[:], 8), ALU.add)
                dve.tensor_tensor(XT[:], kb[:, :, 2, :], middle(X1[:, 1, :], 8), ALU.mult)
                dve.drain()
                dve.tensor_tensor(XT[:], XT[:], middle(s.ident[:], 8), ALU.add).then_inc(S["started"], 1)
                for l in range(NL):
                    for g in range(2):
                        u = (n * NL + l) * 2 + g
                        dve.wait_ge(S["x_ready"], u + 1)
                        xb, xtb = ((5, 6), (0, 1))[g]
                        hg = slice(4 * g, 4 * g + 4)
                        if l < NL - 1:
                            dve.copy_predicated(X[:, hg, :], middle(M[0][:, l, :], 4), v4(b[xb]))
                        dve.copy_predicated(XT[:, hg, :], middle(M[1][:, l, :], 4), v4(b[xtb])).then_inc(S["x_taken"], 1)
                dve.wait_ge(S["y_ready"], n + 1)
                y = s.y[:, ch, :]
                if d == 0:
                    dve.tensor_copy(y, b[3][:]).then_inc(S["y_taken"], 1)
                else:
                    dve.tensor_tensor(y, y, b[3][:], ALU.add).then_inc(S["y_taken"], 1)
                dve.wait_ge(S["s_ready"], n + 1)
                dve.tensor_tensor(stmp[:], state[:], v4(b[4]), ALU.add).then_inc(S["s_taken"], 1)
                dve.drain()
                dve.tensor_tensor(stmp[:], stmp[:], middle(s.blk[:], 4), ALU.mult)
                dve.drain()
                dve.tensor_tensor(state[:], stmp[:], last(hdec[:, :, 0], P), ALU.mult)
                dve.drain()


LN_EPS = 64e-5


def rwkv_out(nc, name, s, out):
    NH = CHUNKS * 8
    with Stage(nc, name) as st:
        sq = st.sb("sq", [P, CHUNKS * 512])
        mu, var = st.sb("mu", [P, NH]), st.sb("var", [P, NH])
        turned_y = [[st.pb(f"y{i}_{j}") for j in range(2)] for i in range(2)]
        gate = [[st.pb(f"g{i}_{j}") for j in range(2)] for i in range(2)]
        centred, squared, rooted, normed, ready, taken = (
            st.sem(n) for n in ("centred", "squared", "rooted", "normed", "ready", "taken"))
        block = st.cs.enter_context(nc.Block())
        y3 = s.y[:].rearrange("p c (h n) -> p (c h) n", n=64)
        sq3 = sq[:].rearrange("p (h n) -> p h n", n=64)

        @block.vector
        def _(dve):
            dve.tensor_reduce(mu[:], y3, AX.X, ALU.add)
            dve.drain()
            dve.tensor_scalar(mu[:], mu[:], 1.0 / 64, None, ALU.mult)
            dve.drain()
            dve.tensor_tensor(y3, y3, last(mu[:], 64), ALU.subtract).then_inc(centred, 1)
            dve.wait_ge(squared, 1)
            dve.tensor_reduce(var[:], sq3, AX.X, ALU.add).then_inc(rooted, 1)
            dve.wait_ge(squared, 2)
            dve.reciprocal(var[:], var[:])
            dve.drain()
            dve.tensor_tensor(y3, y3, last(var[:], 64), ALU.mult).then_inc(normed, 1)
            for t in range(4):
                for j, (t0, tw) in enumerate(SEQS):
                    n = 2 * t + j
                    o, v, bo = (z[:, t, t0:t0 + tw] for z in (out, s.v, s.bonus))
                    dve.tensor_tensor(v, v, bo, ALU.mult)
                    dve.wait_ge(ready, n + 1)
                    dve.drain()
                    dve.scalar_tensor_tensor(out=o, in0=turned_y[t % 2][j][:, 0:tw], scalar=s.ln_g[:, t:t + 1], in1=v,
                                             op0=ALU.mult, op1=ALU.add)
                    dve.drain()
                    dve.scalar_tensor_tensor(out=o, in0=o, scalar=s.ln_b[:, t:t + 1], in1=gate[t % 2][j][:, 0:tw],
                                             op0=ALU.add, op1=ALU.mult).then_inc(taken, 1)

        @block.scalar
        def _(act):
            act.wait_ge(centred, 1)
            act.activation(sq[:], s.y[:].rearrange("p c n -> p (c n)"), ACT.Square).then_inc(squared, 1)
            act.wait_ge(rooted, 1)
            act.activation(var[:], var[:], ACT.Sqrt, bias=s.ln_eps, scale=1.0 / 64).then_inc(squared, 1)

        @block.tensor
        def _(pe):
            pe.wait_ge(normed, 1)
            for t in range(4):
                for j, (t0, tw) in enumerate(SEQS):
                    n = 2 * t + j
                    if n >= 4:
                        pe.wait_ge(taken, n - 3)
                    for i in range(tw // P):
                        ch = t0 // P + i
                        pe.transpose(turned_y[t % 2][j][:, i * P:(i + 1) * P], s.y[:, ch, t * P:(t + 1) * P], s.ident[:])
                    pe.matmul(gate[t % 2][j][:, 0:tw], s.g_up[:, t * P:(t + 1) * P], s.gd[:, t0:t0 + tw],
                              start=True, stop=True).then_inc(ready, 1)


class Parts:
    pass


def ffn2(nc, name, a, c, L, x, seqs, w_up, w_down):
    t_min, t_max = seqs[0][0], seqs[-1][0] + seqs[-1][1]
    T = t_max - t_min
    split = T <= SEQ
    with Stage(nc, name) as st:
        hidden = Split(st, "hidden", [P, 22, T]) if split else st.sb("hidden", [P, 22, T])
        with Stage(nc, name + "_in") as s2:
            h = Split(s2, "h", [P, KT, T])
            cw, cb = s2.sb("cw", [P, 22, 9]), s2.sb("cb", [P, 22, 1])
            load(nc, name + "load", [(cw[:], a[f"ffn_conv{L.i}"]), (cb[:], a[f"ffn_conv_b{L.i}"])])
            pre_norm(nc, name, c, L, 3, x, h, seqs)

            def conv(e, m, b, banks, t):
                for j, (t0, tw) in enumerate(seqs):
                    acc = t[0][:, t0 - t_min:t0 - t_min + tw]
                    if tw == SEQ:
                        ins = conv_grid(e, acc, banks[0][j][:, 0:tw], lambda p, q: cw[:, m, 3 * p + q:3 * p + q + 1])
                    else:
                        ins = conv3(e, acc, banks[0][j][:, 0:tw], lambda q: cw[:, m, 3 + q:4 + q], tw)
                return ins

            def gelu(e, m, b, banks, t):
                return e.activation(t[1][:], t[0][:], ACT.Gelu_apprx_tanh, bias=cb[:, m, :])

            def mult(e, m, b, banks, t):
                for j, (t0, tw) in enumerate(seqs):
                    o = slice(t0 - t_min, t0 - t_min + tw)
                    ins = e.tensor_tensor(t[1][:, o] if split else hidden[:, m, o], t[1][:, o], banks[1][j][:, 0:tw], ALU.mult)
                return ins

            steps = [("vector", conv), ("scalar", gelu), ("vector", mult)]
            if split:
                steps += [("scalar", lambda e, m, b, banks, t: e.activation(hidden.hi[:, m, :], t[1][:], ACT.Copy)),
                          ("gpsimd", lambda e, m, b, banks, t: e.tensor_tensor(
                              hidden.lo[:, m, :], t[1][:], hidden.hi[:, m, :].bitcast(F32), ALU.subtract))]
            project(nc, name + "up", w_up, [h.tiles(KT)] * 2, [(t0 - t_min, tw) for t0, tw in seqs], steps,
                    unroll=2, extra=1, temps=lambda s, n: [[s.sb(f"t{i}_{j}", [P, T]) for j in range(2)] for i in range(n)])
        y = st.sb("y", [P, KT, ALLTOK if not split else SEQ])
        down(nc, name + "down", w_down, hidden.tiles(22) if split else [hidden[:, k, :] for k in range(22)], y, seqs, t_min,
             per_piece=11, split=split)
        post_norm(nc, name + "p", c, L, 5, x, y, seqs, t_min)


def down(nc, name, w, src, y, seqs, t_min, **kw):
    def keep(e, m, b, banks, t):
        for j, (t0, tw) in enumerate(seqs):
            ins = e.tensor_copy(y[:, m, t0 - t_min:t0 - t_min + tw], banks[0][j][:, 0:tw])
        return ins
    project(nc, name, w, [src], [(t0 - t_min, tw) for t0, tw in seqs], [("vector", keep)], unroll=2, **kw)


def pre_norm(nc, name, c, L, i, x, h, seqs):
    t_min = seqs[0][0]
    for t0, tw in seqs:
        s = 0 if t0 == 0 else 1
        mod = lambda j: lambda k: L.mods[:, (i + j) * KT + k, s:s + 1]
        o = slice(t0 - t_min, t0 - t_min + tw)
        rms_norm(nc, f"{name}pre{s}", KT, tw, lambda k: x[:, k, t0:t0 + tw], lambda k: (h.hi[:, k, o], h.lo[:, k, o]),
                 c.one, c.eps, gain=mod(1), shift=mod(0))


def post_norm(nc, name, c, L, i, x, y, seqs, t_min):
    for t0, tw in seqs:
        s = 0 if t0 == 0 else 1
        rms_norm(nc, f"{name}post{s}", KT, tw, lambda k: y[:, k, t0 - t_min:t0 - t_min + tw], None, c.one, c.eps,
                 gain=lambda k: L.mods[:, i * KT + k, s:s + 1], residual=lambda k: x[:, k, t0:t0 + tw])


def mixer_ab(nc, a, c, L, x, tap):
    with Stage(nc, "ab") as st:
        cat = st.sb("cat", [P, 8, ALLTOK])
        with Stage(nc, "ab2") as s1:
            s = Parts()
            rkv = s1.sb("rkv", [P, 12, ALLTOK])
            s.r, s.k, s.v = rkv[:, 0:4, :], rkv[:, 4:8, :], rkv[:, 8:12, :]
            s.bonus = cat[:, 4:8, :]
            lora = s1.sb("lora", [P, 3, ALLTOK])
            s.wd, s.ad, s.gd = lora[:, 0, :], lora[:, 1, :], lora[:, 2, :]
            with Stage(nc, "ab3") as s2:
                h = Split(s2, "h", [P, KT, ALLTOK])
                pre_norm(nc, "ab", c, L, 0, x, h, SEQS)
                u = s2.sb("u", [P, 4, ALLTOK])
                vg = s2.sb("vg", [P, CHUNKS, 512])
                shift = s2.sb("shift", [P, 12, 3])
                ws, bs, gv = s2.sb("ws", [P, 4, P]), s2.sb("bs", [P, 512]), s2.sb("gv", [P, 512])
                load(nc, "abload", [(shift[:], a["b_shift"]), (ws[:], a["a_ws"]), (bs[:], broadcast_rows(a["a_bs"], 512)),
                                    (gv[:], broadcast_rows(a["a_gv"], 512))])

                def each(f):
                    def g(e, m, b, banks, t):
                        for j, (t0, tw) in enumerate(SEQS):
                            ins = f(e, m, b, banks[0][j][:, 0:tw], t0, tw)
                        return ins
                    return g

                project(nc, "abu", a["w_ab_u"], [h.tiles(KT)], SEQS, [("scalar", each(
                    lambda e, m, b, bank, t0, tw: e.activation(u[:, m, t0:t0 + tw], bank, ACT.Gelu_apprx_tanh)))], unroll=4)
                project(nc, "abrkv", a["w_ab_rkv"], [h.tiles(KT)], SEQS, [("vector", each(
                    lambda e, m, b, bank, t0, tw: conv3(e, rkv[:, m, t0:t0 + tw], bank, lambda j: shift[:, m, j:j + 1], tw)))],
                    unroll=4)
                project(nc, "ablora", a["w_ab_lora"], [h.tiles(KT)], SEQS, [("scalar", each(
                    lambda e, m, b, bank, t0, tw: e.activation(lora[:, b, t0:t0 + tw], bank, (ACT.Tanh, ACT.Copy, ACT.Sigmoid)[b])))],
                    unroll=3)
                token_major(nc, "abv", a["w_ab_v"], h.tiles(KT), [slice(i * P, (i + 1) * P) for i in range(CHUNKS)],
                            lambda e, n, r, bank: e.activation(vg[:, r, :], bank, ACT.Gelu_apprx_tanh), unroll=1, per_piece=2)
                spatial_gate(nc, "gate", u, vg, ws, bs, gv, cat, c.eps)
            tap("rkv", rkv)
            tap("lora", lora)
            with Stage(nc, "rw") as s2:
                pairs = []

                def const(name, shape, dt=F32):
                    buf = s2.sb("c_" + name, shape, dt)
                    pairs.append((buf[:], a[name]))
                    return buf

                s.y = s2.sb("y", [P, CHUNKS, 512])
                s.kk = s2.sb("kk", [P, 4, ALLTOK])
                s.vtok = s2.sb("vtok", [P, CHUNKS, 512])
                s.ident, s.one = c.ident, c.one
                s.blk = const("blk64", [P, P])
                s.w_up, s.a_up = const("b_w_up", [P, 512]), const("b_a_up", [P, 512])
                s.b_w0, s.b_a0 = const("b_w0", [P, 2, 4]), const("b_a0", [P, 2, 4])
                s.b_ka, kkw, rk = const("b_ka", [P, 4]), const("b_kk", [P, 4]), const("b_rk", [P, 4])
                s.ln_g, s.ln_b = const("b_ln_g", [P, 4]), const("b_ln_b", [P, 4])
                lneps = const("ln_eps", [P, 1])
                s.ln_eps = lneps[:, 0:1]
                strict, x1 = const("strict", [P, 2, 4 * P]), const("x1", [P, 2, 2, P])
                lev = s2.sb("lev", [P, 2, 6, P], mybir.dt.uint8)
                s.masks = [(strict[:, d], x1[:, d], (lev[:, d], lev[:, 1 - d])) for d in range(2)]
                s.one_ka = s2.sb("one_ka", [P, 4])
                s.blk_rk = s2.sb("blk_rk", [P, 4, P])
                load(nc, "rwload", pairs)
                with Stage(nc, "rwprep") as s3:
                    levels, loaded = s3.sb("levels", [P, 2, 6, P]), s3.sem("loaded")
                    block = s3.cs.enter_context(nc.Block())

                    @block.sync
                    def _(sp):
                        sp.dma_start(levels[:], a["levels"]).then_inc(loaded, 16)

                    @block.vector
                    def _(dve):
                        dve.tensor_scalar(s.one_ka[:], s.b_ka[:], -1.0, 1.0, ALU.mult, ALU.add)
                        dve.tensor_tensor(s.blk_rk[:], middle(s.blk[:], 4), last(rk[:], P), ALU.mult)
                        dve.wait_ge(loaded, 16)
                        dve.tensor_copy(lev[:], levels[:])
                rwkv_keys(nc, "keys", s.k, s.v, s.kk, s.vtok, kkw, c.ident, s.blk, None)
                tap("kk", s.kk)
                tap("vtok", s.vtok)
                rwkv_scan(nc, "rwkv", s)
                tap("yrw", s.y)
                s.g_up = s2.sb("g_up", [P, 512])
                load(nc, "gload", [(s.g_up[:], a["b_g_up"])])
                rwkv_out(nc, "rwout", s, cat[:, 4:8, :])
        tap("cat", cat)
        y = st.sb("y", [P, KT, ALLTOK])
        cat_parts = Split(st, "cat", [P, 8, ALLTOK])
        split_up(nc, "cat_parts", cat, cat_parts, 8)
        down(nc, "about", a["w_ab_out"], cat_parts.tiles(8), y, SEQS, 0)
        tap("yab", y)
        post_norm(nc, "abp", c, L, 2, x, y, SEQS, 0)


def second_block(nc, a, c, x, tap):
    with Stage(nc, "mods") as st:
        layers = []
        for i in range(2):
            L = Parts()
            L.i = i
            L.mods = st.sb(f"mods{i}", [P, MOD * KT, 2])
            L.bias = st.sb(f"bias{i}", [P, MOD * KT, 2])
            L.mix_pre, L.mix_post, L.ffn_pre, L.ffn_post = (st.sb(f"{n}{i}", [P, KT]) for n in ("mix_pre", "mix_post", "ffn_pre", "ffn_post"))
            layers.append(L)
        cvec = st.sb("cvec", [P, KT, 2])
        load(nc, "modload", [(cvec[:], a["cvec"])] + [(b[:], a[f"{n}{L.i}"]) for L in layers for b, n in (
            (L.bias, "ada_b"), (L.mix_pre, "norm_mix_pre"), (L.mix_post, "norm_mix_post"),
            (L.ffn_pre, "norm_ffn_pre"), (L.ffn_post, "norm_ffn_post"))])
        silu_columns(nc, "silu", cvec[:])
        cvec_parts = Split(st, "cvec", [P, KT, 2])
        split_up(nc, "cvec_parts", cvec, cvec_parts, KT)
        for L in layers:
            modulations(nc, f"mod{L.i}", a[f"w_ada{L.i}"], L.bias, cvec_parts, c.ident, L.mods)
        modulation_gains(nc, "gains", layers)
        mixer_ab(nc, a, c, layers[0], x, tap)
        tap("x_ab", x)
        ffn2(nc, "f0", a, c, layers[0], x, SEQS, a["w_ffn_up0"], a["w_ffn_down0"])
        tap("x_l0", x)
        mixer_mlstm(nc, a, c, layers[1], x, tap)
        tap("x_ml", x)
        ffn2(nc, "f1", a, c, layers[1], x, SEQS[1:], a["w_ffn_up1"], a["w_ffn_down1"])
        tap("x_l1", x)


MH, MD = 4, 256


def expand_blocks(nc, name, compact, mask, out):
    with Stage(nc, name) as st:
        block = st.cs.enter_context(nc.Block())

        @block.vector
        def _(dve):
            for t in range(KT):
                dve.tensor_tensor(out[:, t, :].rearrange("p (g o) -> p g o", o=4), middle(compact[:, t, :], P // 4),
                                  mask[:].rearrange("p (g o) -> p g o", o=4), ALU.mult)


def mlstm_heads(nc, name, xm, xcv, wq, wk, wv, q, k, ktok, vtok, cb):
    with Stage(nc, name) as st:
        banks = [st.pb(f"bank{i}") for i in range(8)]
        made, taken_a, taken_v = st.sem("made"), st.sem("taken_a"), st.sem("taken_v")
        block = st.cs.enter_context(nc.Block())
        scale = MD ** -0.5
        jobs = [(w, t) for t in range(KT) for w in ("q", "k")]
        jobs += [(w, ch, half) for w in ("vt", "kt") for ch in range(CHUNKS) for half in range(2)]

        @block.tensor
        def _(pe):
            for n, job in enumerate(jobs):
                if n >= 8:
                    pe.wait_ge((taken_a, taken_v)[n % 2], (n - 8) // 2 + 1)
                bank = banks[n % 8]
                if job[0] in ("q", "k"):
                    mm = pe.matmul(bank[:], (wq if job[0] == "q" else wk)[:, job[1], :], xcv[:, job[1], CTX:ALLTOK], start=True, stop=True)
                else:
                    w, ch, half = job
                    for i in range(4):
                        t = 4 * half + i
                        mm = pe.matmul(bank[:, i * P:(i + 1) * P], (xcv if w == "kt" else xm)[:, t, ch * P:(ch + 1) * P],
                                       (wk if w == "kt" else wv)[:, t, :], start=True, stop=True)
                mm.then_inc(made, 1)

        def place(job):
            if job[0] in ("q", "k"):
                return (q if job[0] == "q" else k)[:, job[1], :], 1.0 if job[0] == "q" else scale
            if job[0] == "kt":
                return ktok[:, job[1], job[2] * 512:job[2] * 512 + 512].rearrange("p (h n) -> p h n", h=2), scale
            return vtok[:, job[1], 2 * job[2]:2 * job[2] + 2, 0:MD], 1.0

        def source(n):
            return banks[n % 8][:] if jobs[n][0] in ("q", "k") else banks[n % 8][:].rearrange("p (h n) -> p h n", h=2)

        @block.scalar
        def _(act):
            for n in range(0, len(jobs), 2):
                act.wait_ge(made, n + 1)
                dst, factor = place(jobs[n])
                act.activation(dst, source(n), ACT.Copy, scale=factor).then_inc(taken_a, 1)

        @block.vector
        def _(dve):
            dve.memset(vtok[:, :, :, MD:MD + 1], 1.0)
            for n in range(1, len(jobs), 2):
                dve.wait_ge(made, n + 1)
                dst, factor = place(jobs[n])
                dve.tensor_scalar(dst, source(n), factor, None, ALU.mult).then_inc(taken_v, 1)


def mlstm_gates(nc, name, raw, bias, tri, m, one):
    G = 2 * MH
    with Stage(nc, name) as st:
        x, ab, lf = st.sb("x", [P, CHUNKS, 2, G]), st.sb("ab", [P, CHUNKS, G]), st.sb("lf", [P, CHUNKS, G])
        ps = [st.pb(f"ps{i}") for i in range(2)]
        added, logged, forgot, summed = (st.sem(n) for n in ("added", "logged", "forgot", "summed"))
        block = st.cs.enter_context(nc.Block())
        W = CHUNKS * MH

        @block.vector
        def _(dve):
            dve.tensor_tensor(x[:].rearrange("p c a g -> p c (a g)"), raw[:], middle(bias[:], CHUNKS), ALU.add).then_inc(added, 1)
            dve.wait_ge(logged, 1)
            dve.scalar_tensor_tensor(out=lf[:], in0=x[:, :, 1, :], scalar=0.0, in1=ab[:], op0=ALU.min, op1=ALU.subtract).then_inc(forgot, 1)
            dve.wait_ge(summed, 1)
            for d in range(2):
                dve.tensor_copy(m.b[:, :, d, :], ps[d][:, 0:W].rearrange("p (c h) -> p c h", h=MH))
            dve.drain()
            dve.tensor_tensor(m.cc[:].rearrange("p c d h -> p c (d h)"), x[:, :, 0, :], m.b[:].rearrange("p c d h -> p c (d h)"), ALU.subtract)

        @block.scalar
        def _(act):
            act.wait_ge(added, 1)
            act.activation(ab[:], x[:, :, 1, :], ACT.Abs)
            act.drain()
            act.activation(ab[:], ab[:], ACT.Exp, scale=-1.0)
            act.drain()
            act.activation(ab[:], ab[:], ACT.Ln, bias=one[:, 0:1]).then_inc(logged, 1)

        @block.tensor
        def _(pe):
            pe.wait_ge(forgot, 1)
            for d in range(2):
                mm = pe.matmul(ps[d][:, 0:W], tri[d][:], lf[:, :, d * MH:(d + 1) * MH], start=True, stop=True)
            mm.then_inc(summed, 1)


def mlstm_scan(nc, name, m, q, k, ktok, vtok, hsum, ident, neg, edge):
    NU = len(UNITS)
    V = MD + 1
    with Stage(nc, name) as st:
        mm_b = st.sb("mm_b", [P, 2 * MH])
        nmm, rmax, mprev, win, floor, kco, carry, den = (
            st.sb(n, [P, MH]) for n in ("nmm", "rmax", "mprev", "win", "floor", "kco", "carry", "den"))
        args = st.sb("args", [P, 4, MH])
        edge_sb = st.sb("edge_sb", [P, 2 * MH])
        E, Sm, St = (st.sb(n, [P, MH, P]) for n in ("E", "Sm", "St"))
        num = st.sb("num", [P, MH, V])
        kw = st.sb("kw", [P, MH * MD])
        state = st.sb("state", [P, 2 * MH, V])
        cbank, sbank, ebank, tbank = (st.pb(n) for n in ("cbank", "sbank", "ebank", "tbank"))
        work = [st.pb(f"work{i}") for i in range(4)]
        names = ("spread", "maxed", "picked", "argued", "exped", "weighed", "scored", "masked", "turned", "copied",
                 "inner", "outer", "scaled", "summed", "updated", "taken", "keyed", "read")
        S = {n: st.sem(n) for n in names}
        block = st.cs.enter_context(nc.Block())
        xn = [n for n, (d, ch) in enumerate(UNITS) if ch >= CTXCH]
        before = lambda n: sum(1 for i in xn if i < n)

        @block.tensor
        def _(pe):
            for n, (d, ch) in enumerate(UNITS):
                i = before(n)
                js = slice((ch - CTXCH) * P, (ch - CTXCH + 1) * P)
                if n >= 1:
                    pe.wait_ge(S["exped"], n)
                for h in range(MH):
                    bank = cbank[:, h * P:(h + 1) * P]
                    pe.matmul(bank, m.cc[:, ch, d, h:h + 1].to_broadcast([P, P]), ident[:], start=True, stop=False)
                    mm = pe.matmul(bank, ident[:], neg[d][:], start=False, stop=True)
                mm.then_inc(S["spread"], 1)
                pe.wait_ge(S["maxed"], n + 1)
                if n >= 1:
                    pe.wait_ge(S["argued"], n)
                pe.matmul(ebank[:, 0:2 * MH], edge[d][:], mm_b[:], start=True, stop=True).then_inc(S["picked"], 1)
                if ch >= CTXCH:
                    if i >= 1:
                        pe.wait_ge(S["masked"], i)
                    for h in range(MH):
                        for kt in range(2):
                            mm = pe.matmul(sbank[:, h * P:(h + 1) * P], q[:, 2 * h + kt, js], k[:, 2 * h + kt, js],
                                           start=(kt == 0), stop=(kt == 1))
                    mm.then_inc(S["scored"], 1)
                    pe.wait_ge(S["masked"], i + 1)
                    for h in range(MH):
                        mm = pe.transpose(tbank[:, h * P:(h + 1) * P], Sm[:, h, :], ident[:])
                    mm.then_inc(S["turned"], 1)
                    pe.wait_ge(S["copied"], i + 1)
                    for h in range(MH):
                        inner, outer = work[2 * (h % 2)], work[2 * (h % 2) + 1]
                        if h >= 2:
                            pe.wait_ge(S["summed"], i * MH + h - 1)
                        pe.matmul(inner[:, 0:V], St[:, h, :], vtok[:, ch, h, :], start=True, stop=True).then_inc(S["inner"], 1)
                        for kt in range(2):
                            mm = pe.matmul(outer[:, 0:V], q[:, 2 * h + kt, js], state[:, 2 * h + kt, :], start=(kt == 0), stop=(kt == 1))
                        mm.then_inc(S["outer"], 1)
                    pe.wait_ge(S["summed"], i * MH + MH)
                pe.wait_ge(S["keyed"], n + 1)
                for u in range(2 * MH):
                    if u >= 4:
                        pe.wait_ge(S["taken"], n * 2 * MH + u - 3)
                    pe.matmul(work[u % 4][:, 0:V], kw[:, u * P:(u + 1) * P], vtok[:, ch, u // 2, :], start=True, stop=True).then_inc(S["updated"], 1)
                pe.wait_ge(S["taken"], (n + 1) * 2 * MH)

        @block.scalar
        def _(act):
            for n, (d, ch) in enumerate(UNITS):
                i = before(n)
                act.wait_ge(S["maxed"], n + 1)
                if ch >= CTXCH and i >= 1:
                    act.wait_ge(S["masked"], i)
                if n >= 1:
                    act.wait_ge(S["keyed"], n)
                    act.wait_ge(S["read"], n)
                for h in range(MH):
                    act.activation(E[:, h, :], cbank[:, h * P:(h + 1) * P], ACT.Exp, bias=nmm[:, h:h + 1])
                act.activation(win[:], args[:, 0, :], ACT.Exp)
                act.activation(floor[:], args[:, 1, :], ACT.Exp).then_inc(S["exped"], 1)
                act.wait_ge(S["argued"], n + 1)
                act.activation(kco[:], args[:, 2, :], ACT.Exp)
                act.activation(carry[:], args[:, 3, :], ACT.Exp).then_inc(S["weighed"], 1)
                if ch >= CTXCH:
                    act.wait_ge(S["turned"], i + 1)
                    act.activation(St[:], tbank[:].rearrange("p (h n) -> p h n", h=MH), ACT.Copy).then_inc(S["copied"], 1)
                    for h in range(MH):
                        act.wait_ge(S["outer"], i * MH + h + 1)
                        act.activation(num[:, h, :], work[2 * (h % 2) + 1][:, 0:V], ACT.Copy, scale=win[:, h:h + 1]).then_inc(S["scaled"], 1)

        @block.vector
        def _(dve):
            for n, (d, ch) in enumerate(UNITS):
                i = before(n)
                if n in (0, NU // 2):
                    dve.memset(state[:], 0.0)
                    dve.memset(mprev[:], 0.0)
                    dve.drain()
                dve.wait_ge(S["spread"], n + 1)
                dve.tensor_reduce(rmax[:], cbank[:].rearrange("p (h n) -> p h n", h=MH), AX.X, ALU.max)
                dve.tensor_copy(mm_b[:, MH:2 * MH], m.b[:, ch, d, :])
                dve.drain()
                dve.tensor_tensor(mm_b[:, 0:MH], rmax[:], mprev[:], ALU.max)
                dve.drain()
                dve.tensor_scalar(nmm[:], mm_b[:, 0:MH], -1.0, None, ALU.mult)
                dve.tensor_tensor(args[:, 0, :], mprev[:], mm_b[:, 0:MH], ALU.subtract)
                dve.drain()
                dve.tensor_tensor(args[:, 1, :], nmm[:], mm_b[:, MH:2 * MH], ALU.subtract).then_inc(S["maxed"], 1)
                dve.wait_ge(S["picked"], n + 1)
                dve.tensor_copy(edge_sb[:], ebank[:, 0:2 * MH])
                dve.drain()
                dve.tensor_tensor(args[:, 2, :], m.cc[:, ch, d, :], edge_sb[:, 0:MH], ALU.subtract)
                dve.tensor_tensor(args[:, 3, :], mprev[:], edge_sb[:, 0:MH], ALU.subtract).then_inc(S["argued"], 1)
                dve.drain()
                dve.tensor_tensor(mprev[:], edge_sb[:, 0:MH], edge_sb[:, MH:2 * MH], ALU.add)
                dve.wait_ge(S["exped"], n + 1)
                dve.wait_ge(S["weighed"], n + 1)
                dve.tensor_tensor(kw[:].rearrange("p (h n) -> p h n", h=MH), ktok[:, ch, :].rearrange("p (h n) -> p h n", h=MH),
                                  last(kco[:], MD), ALU.mult).then_inc(S["keyed"], 1)
                if ch >= CTXCH:
                    dve.wait_ge(S["scored"], i + 1)
                    dve.tensor_tensor(Sm[:], sbank[:].rearrange("p (h n) -> p h n", h=MH), E[:], ALU.mult).then_inc(S["masked"], 1)
                    for h in range(MH):
                        dve.wait_ge(S["scaled"], i * MH + h + 1)
                        dve.tensor_tensor(num[:, h, :], num[:, h, :], work[2 * (h % 2)][:, 0:V], ALU.add).then_inc(S["summed"], 1)
                    dve.drain()
                    dcol = num[:, :, MD]
                    dve.scalar_tensor_tensor(out=den[:], in0=dcol, scalar=-1.0, in1=dcol, op0=ALU.mult, op1=ALU.max)
                    dve.drain()
                    dve.tensor_tensor(den[:], den[:], floor[:], ALU.max)
                    dve.drain()
                    dve.reciprocal(den[:], den[:])
                    dve.drain()
                    h4 = hsum[:, ch - CTXCH, :].rearrange("p (h n) -> p h n", h=MH)
                    if d == 0:
                        dve.tensor_tensor(h4, num[:, :, 0:MD], last(den[:], MD), ALU.mult)
                    else:
                        dve.tensor_tensor(num[:, :, 0:MD], num[:, :, 0:MD], last(den[:], MD), ALU.mult)
                        dve.drain()
                        dve.tensor_tensor(h4, h4, num[:, :, 0:MD], ALU.add)
                dve.drain()
                for u in range(2 * MH):
                    dve.wait_ge(S["updated"], n * 2 * MH + u + 1)
                    ins = dve.scalar_tensor_tensor(out=state[:, u, :], in0=state[:, u, :], scalar=carry[:, u // 2:u // 2 + 1],
                                                   in1=work[u % 4][:, 0:V], op0=ALU.mult, op1=ALU.add)
                    ins.then_inc(S["taken"], 1)
                dve.drain()
                dve.nop().then_inc(S["read"], 1)


def mlstm_out(nc, name, hsum, xcv, z, c_norm, c_skip, out, ident, eps):
    NU = NCH * MH
    with Stage(nc, name) as st:
        sq = st.sb("sq", [P, MD])
        ss = st.sb("ss", [P, NU])
        tmp = st.sb("tmp", [P, 2, SEQ])
        banks = [st.pb(f"bank{i}") for i in range(2)]
        rooted, normed, turned, taken, scaled = (st.sem(n) for n in ("rooted", "normed", "turned", "taken", "scaled"))
        block = st.cs.enter_context(nc.Block())

        @block.scalar
        def _(act):
            for n in range(NU):
                act.activation(sq[:], hsum[:, n // MH, (n % MH) * MD:(n % MH + 1) * MD], ACT.Square, accum_out=ss[:, n:n + 1])
                act.drain()
            act.activation(ss[:], ss[:], ACT.Sqrt, bias=eps, scale=1.0 / MD).then_inc(rooted, 1)
            for t in range(KT):
                act.wait_ge(turned, t + 1)
                if t >= 2:
                    act.wait_ge(taken, t - 1)
                act.activation(tmp[:, t % 2, :], banks[t % 2][:], ACT.Copy, scale=c_norm[:, t:t + 1]).then_inc(scaled, 1)

        @block.vector
        def _(dve):
            dve.wait_ge(rooted, 1)
            dve.reciprocal(ss[:], ss[:])
            dve.drain()
            h3 = hsum[:].rearrange("p c (h n) -> p (c h) n", h=MH)
            dve.tensor_tensor(h3, h3, last(ss[:], MD), ALU.mult).then_inc(normed, 1)
            for t in range(KT):
                dve.wait_ge(scaled, t + 1)
                dve.scalar_tensor_tensor(out=out[:, t, :], in0=xcv[:, t, CTX:ALLTOK], scalar=c_skip[:, t:t + 1], in1=tmp[:, t % 2, :],
                                         op0=ALU.mult, op1=ALU.add).then_inc(taken, 1)
                dve.drain()
                dve.tensor_tensor(out[:, t, :], out[:, t, :], z[:, t, :], ALU.mult)

        @block.tensor
        def _(pe):
            pe.wait_ge(normed, 1)
            for t in range(KT):
                if t >= 2:
                    pe.wait_ge(scaled, t - 1)
                for i in range(NCH):
                    mm = pe.transpose(banks[t % 2][:, i * P:(i + 1) * P], hsum[:, i, t * P:(t + 1) * P], ident[:])
                mm.then_inc(turned, 1)


def mixer_mlstm(nc, a, c, L, x, tap):
    with Stage(nc, "ml") as st:
        xcv = st.sb("xcv", [P, KT, ALLTOK])
        z = st.sb("z", [P, KT, SEQ])
        q = st.sb("q", [P, KT, SEQ])
        hsum = st.sb("hsum", [P, NCH, D])
        with Stage(nc, "ml2") as s1:
            m = Parts()
            m.b, m.cc = s1.sb("b", [P, CHUNKS, 2, MH]), s1.sb("cc", [P, CHUNKS, 2, MH])
            lower = s1.sb("lower", [P, P])
            neg = [s1.sb(f"neg{d}", [P, P]) for d in range(2)]
            edge = [s1.sb(f"edge{d}", [P, P]) for d in range(2)]
            load(nc, "mlload", [(lower[:], a["lower"]), (neg[0][:], a["neg_later0"]), (neg[1][:], a["neg_later1"]),
                                (edge[0][:], a["edge0"]), (edge[1][:], a["edge1"])])
            xm = s1.sb("xm", [P, KT, ALLTOK])
            with Stage(nc, "ml3") as s2:
                h = Split(s2, "h", [P, KT, ALLTOK])
                raw, gbias = s2.sb("raw", [P, CHUNKS, 16]), s2.sb("gbias", [P, 16])
                cw, cb = s2.sb("cw", [P, KT, 3]), s2.sb("cb", [P, KT, 1])
                load(nc, "mlload2", [(cw[:], a["c_conv"]), (cb[:], a["c_conv_b"]), (gbias[:, 0:8], broadcast_rows(a["c_bi"], 8)),
                                     (gbias[:, 8:16], broadcast_rows(a["c_bf"], 8))])
                pre_norm(nc, "ml", c, L, 0, x, h, SEQS)

                def conv(e, m_, b, banks, t):
                    for j, (t0, tw) in enumerate(SEQS):
                        ins = conv3(e, t[:, t0:t0 + tw], banks[0][j][:, 0:tw], lambda i: cw[:, m_, i:i + 1], tw)
                    return ins

                def keep(e, m_, b, banks, t):
                    e.activation(xcv[:, m_, :], t[:], ACT.Silu, bias=cb[:, m_, :])
                    for j, (t0, tw) in enumerate(SEQS):
                        ins = e.activation(xm[:, m_, t0:t0 + tw], banks[0][j][:, 0:tw], ACT.Copy)
                    return ins

                project(nc, "xm", a["w_c_xm"], [h.tiles(KT)], SEQS, [("vector", conv), ("scalar", keep)], unroll=2,
                        temps=lambda s, n: [s.sb(f"acc{i}", [P, ALLTOK]) for i in range(n)])
                project(nc, "mz", a["w_c_z"], [h.tiles(KT)], SEQS[1:],
                        [("scalar", lambda e, m_, b, banks, t: e.activation(z[:, m_, :], banks[0][0][:], ACT.Sigmoid))], unroll=4)
                token_major(nc, "mg", a["w_c_gates"], h.tiles(KT), [slice(i * P, (i + 1) * P) for i in range(CHUNKS)],
                            lambda e, n, r, bank: e.tensor_copy(raw[:, r, :], bank), unroll=1, per_piece=KT, engine="vector")
                mlstm_gates(nc, "mgates", raw, gbias, (c.upper, lower), m, c.one)
            tap("xcv", xcv)
            tap("m_cc", m.cc)
            k = s1.sb("k", [P, KT, SEQ])
            ktok = xm[:].rearrange("p k t -> p (k t)").rearrange("p (c n) -> p c n", c=CHUNKS)
            vtok = s1.sb("vtok", [P, CHUNKS, MH, MD + 1])
            with Stage(nc, "ml4") as s2:
                mask = s2.sb("mask", [P, P])
                ws = []
                compact = [s2.sb(f"compact{i}", [P, KT, 4]) for i in range(3)]
                load(nc, "mlload3", [(mask[:], a["block4"])] + [(compact[i][:], a[n]) for i, n in enumerate(("c_wq", "c_wk", "c_wv"))])
                for i in range(3):
                    ws.append(s2.sb(f"w{i}", [P, KT, P]))
                    expand_blocks(nc, f"expand{i}", compact[i], mask, ws[i])
                mlstm_heads(nc, "mheads", xm, xcv, *ws, q, k, ktok, vtok, None)
            mlstm_scan(nc, "mscan", m, q, k, ktok, vtok, hsum, c.ident, neg, edge)
        tap("hsum", hsum)
        cn, ck = st.sb("cn", [P, KT]), st.sb("ck", [P, KT])
        load(nc, "mlload4", [(cn[:], a["c_norm"]), (ck[:], a["c_skip"])])
        mlstm_out(nc, "mout", hsum, xcv, z, cn, ck, q, c.ident, c.eps)
        y = st.sb("y", [P, KT, SEQ])
        out_parts = Split(st, "out", [P, KT, SEQ])
        split_up(nc, "out_parts", q, out_parts, KT)
        down(nc, "mlout", a["w_c_out"], out_parts.tiles(KT), y, SEQS[1:], CTX)
        post_norm(nc, "mlp", c, L, 2, x, y, SEQS[1:], CTX)


class Constants:
    pass


def build(nc, a, out, tap=lambda name, buf: None, start=0):
    Stage.number[0] = 0
    with Stage(nc, "whole") as st:
        c = Constants()
        pairs = []

        def const(name, shape):
            buf = st.sb(name, shape)
            pairs.append((buf[:], a[name]))
            return buf

        c.ident, c.flip, c.one, c.upper, c.neg_lower = (
            const(n, [P, P]) for n in ("ident", "flip", "one", "upper", "neg_lower"))
        c.eps_buf = const("eps", [P, 1])
        c.eps = c.eps_buf[:, 0:1]
        c.norm1, c.norm2 = const("norm1_w", [P, KT]), const("norm2_w", [P, KT])
        c.final = const("final_norm_w", [P, KT])
        c.ssm_norm = const("ssm_norm_w", [P, 16])
        c.conv_w, c.conv_b = const("conv_w", [P, 24, 4]), const("conv_b", [P, 24, 1])
        streams = st.sb("streams", [P, KT, ALLTOK])
        x = streams[:, :, CTX:ALLTOK]
        pairs += [(x, a["x"]), (streams[:, :, 0:CTX], a["ctx"])]
        load(nc, "load", pairs)
        if start == 0:
            first_block(nc, a, x, c, tap)
        rms_norm(nc, "final", KT, SEQ, lambda k: x[:, k, :], lambda k: x[:, k, :], c.one, c.eps,
                 gain=lambda k: c.final[:, k:k + 1])
        second_block(nc, a, c, streams, tap)
        with Stage(nc, "store") as last_stage:
            stored = last_stage.sem("stored")
            block = last_stage.cs.enter_context(nc.Block())

            @block.sync
            def _(sp):
                sp.dma_start(out, x).then_inc(stored, 16)
                sp.wait_ge(stored, 16)


def chan(v, extra=()):
    import numpy as np
    return np.ascontiguousarray(np.moveaxis(v.reshape(-1, P, *v.shape[1:]), 1, 0))


def by_tile(w, width=P):
    import numpy as np
    K, M = w.shape
    return np.ascontiguousarray(w.reshape(K // P, P, M // width, width).transpose(2, 1, 0, 3)).reshape(M // width, P, -1)


def shape_constants():
    import numpy as np
    i = np.arange(P)
    c = {"ident": np.eye(P), "flip": np.eye(P)[::-1], "one": np.ones((P, P)), "upper": i[:, None] <= i[None, :],
         "neg_lower": np.where(i[:, None] > i[None, :], NEG, 0.0), "eps": np.full((P, 1), EPS),
         "neg_row": np.ones((1, 3 * HEADS))}

    def bucket(dist):
        f = np.maximum(dist, 1).astype(np.float32)
        large = 16 + (np.log(f / np.float32(16)) / np.float32(np.log(128.0)) * np.float32(16)).astype(np.int32)
        return np.where(dist < 16, dist, np.minimum(large, 31))

    u = P - 1 - np.arange(2 * P)
    hot = np.zeros((33, TABLES, 2 * P))
    for t in range(TABLES):
        if t < 2 * DIL - 1:
            s, ok, dil = DIL * u + DIL - 1 - t, True, 1
        elif t == 2 * DIL - 1:
            s, ok, dil = u, True, DIL
        else:
            s, ok, dil = u // 4, u % 4 == 0, 16
        ok = ok & (s >= 0) & (s <= P)
        b = bucket(np.where(ok, s, 0) * dil)
        for w in range(2 * P):
            hot[b[w] if ok[w] else 32, t, w] = 1.0 if ok[w] else NEG
    c["bias_onehot"] = hot
    before, same = i[:, None] < i[None, :], i[:, None] == i[None, :]
    c["lower"] = i[:, None] >= i[None, :]
    c["blk64"] = i[:, None] // 64 == i[None, :] // 64
    c["block4"] = i[:, None] // 4 == i[None, :] // 4
    c["ln_eps"] = np.full((P, 1), LN_EPS)
    c["neg_later0"] = np.where(before, NEG, 0.0)
    c["neg_later1"] = np.where(before.T, NEG, 0.0)
    c["edge0"], c["edge1"] = (np.broadcast_to((i == e)[:, None], (P, P)) for e in (P - 1, 0))
    strict = np.zeros((P, 2, 2, 2 * P))
    for d, bf in enumerate((before, before.T)):
        for s, sign in enumerate((1.0, -1.0)):
            strict[:, d, s] = sign * np.concatenate([bf, bf | same], axis=1)
    c["strict"] = strict.reshape(P, 2, 4 * P)

    def level(m):
        return (i[:, None] // (2 * m) == i[None, :] // (2 * m)) & (i[:, None] // m % 2 == 1) & (i[None, :] // m % 2 == 0)

    c["x1"] = np.stack([np.stack([-1.0 * level(1), 1.0 * level(1).T]), np.stack([-1.0 * level(1).T, 1.0 * level(1)])]).transpose(2, 0, 1, 3)
    levels = np.stack([np.stack([level(m), level(m).T]) for m in (2, 4, 8, 16, 32, 64)], axis=1).transpose(2, 0, 1, 3)
    c["levels"] = levels
    return {n: np.ascontiguousarray(v, np.float32) for n, v in c.items()}


def lay_out(i):
    import numpy as np
    f = {n: np.asarray(v) for n, v in i.items()}
    w = f["w_in"][0]
    cut = np.cumsum([1536, 1536, 1536, 2048, 3072, 32])
    a = {
        "x": chan(np.ascontiguousarray(f["x"][0].T)),
        "norm1_w": chan(f["norm1_w"][0]), "norm2_w": chan(f["norm2_w"][0]), "final_norm_w": chan(f["final_norm_w"]),
        "ssm_norm_w": chan(f["ssm_norm_w"][0]),
        "conv_w": chan(np.ascontiguousarray(f["conv_w"][0].T)), "conv_b": chan(f["conv_b"][0][:, None]),
        "dt_bias": f["dt_bias"][0], "a_log": f["a_log"][0], "d_skip": f["d_skip"][0], "rel_bias": f["rel_bias"],
        "w_qk": by_tile(w[:, :cut[1]]), "w_v": by_tile(w[:, cut[1]:cut[2]], 512), "w_z": by_tile(w[:, cut[2]:cut[3]], 512),
        "w_x": by_tile(w[:, cut[3]:cut[3] + 2048]), "w_bc": by_tile(w[:, cut[3] + 2048:cut[4]]), "w_dt": by_tile(w[:, cut[4]:cut[5]], 32),
        "w_merge": np.concatenate([by_tile(w[:, cut[5]:cut[5] + D]), by_tile(w[:, cut[5] + D:]),
                                   by_tile(f["w_attn_branch"][0]), by_tile(f["w_ssm_branch"][0])], axis=2),
        "w_out": by_tile(f["w_out"][0]),
        "w_ffn_in": np.concatenate([by_tile(f["w_ffn_in"][0][:, :2816]), by_tile(f["w_ffn_in"][0][:, 2816:])], axis=2),
        "w_ffn_out": by_tile(f["w_ffn_out"][0]),
    }
    a["ctx"] = chan(np.ascontiguousarray(f["ctx_2"][0].T))
    a["cvec"] = np.ascontiguousarray(np.stack([chan(f["c_ctx_2"]), chan(f["c_2"][0])], axis=2))
    for i in range(2):
        a[f"w_ada{i}"] = by_tile(f["ada_w_2"][i], 512)
        a[f"ada_b{i}"] = np.repeat(chan(f["ada_b_2"][i])[:, :, None], 2, axis=2)
        for n in ("norm_mix_pre", "norm_mix_post", "norm_ffn_pre", "norm_ffn_post"):
            a[f"{n}{i}"] = chan(f[n + "_2"][i])
        up = f["ffn_up_2"][i]
        a[f"w_ffn_up{i}"] = np.concatenate([by_tile(up[:, :2816]), by_tile(up[:, 2816:])], axis=2)
        a[f"w_ffn_down{i}"] = by_tile(f["ffn_down_2"][i])
        a[f"ffn_conv{i}"] = chan(np.ascontiguousarray(f["ffn_conv_2"][i].reshape(9, -1).T))
        a[f"ffn_conv_b{i}"] = chan(f["ffn_conv_b_2"][i][:, None])
    w = f["ab_w_in_2"][0]
    a["w_ab_u"], a["w_ab_v"] = by_tile(w[:, :512]), by_tile(w[:, 512:1024], 512)
    a["w_ab_rkv"], a["w_ab_lora"], a["w_ab_out"] = by_tile(w[:, 1024:2560]), by_tile(w[:, 2560:]), by_tile(f["ab_w_out_2"][0])
    a["b_shift"] = chan(np.ascontiguousarray(f["b_shift_2"][0].T))
    a["a_ws"] = np.ascontiguousarray(f["a_ws_2"][0].transpose(2, 0, 1))
    a["a_bs"], a["a_gv"] = f["a_bs_2"][0].reshape(-1), f["a_gv_2"][0].reshape(-1)
    a["b_w_up"], a["b_a_up"] = f["b_w_up_2"][0].reshape(P, 512), f["b_a_up_2"][0].reshape(P, 512)
    a["b_g_up"] = f["b_g_up_2"][0]
    for n in ("b_w0", "b_a0"):
        a[n] = np.ascontiguousarray(f[n + "_2"][0].reshape(2, 4, P).transpose(2, 0, 1))
    for n in ("b_ka", "b_kk", "b_rk", "b_ln_g", "b_ln_b", "c_norm", "c_skip"):
        a[n] = chan(f[n + "_2"][0].reshape(-1))
    w = f["c_w_in_2"][0]
    a["w_c_xm"], a["w_c_z"], a["w_c_gates"] = by_tile(w[:, :D]), by_tile(w[:, D:2 * D]), by_tile(w[:, 2 * D:], 16)
    a["w_c_out"] = by_tile(f["c_w_out_2"][0])
    a["c_conv"], a["c_conv_b"] = chan(np.ascontiguousarray(f["c_conv_2"][0].T)), chan(f["c_conv_b_2"][0][:, None])
    a["c_bi"], a["c_bf"] = f["c_bi_2"][0].reshape(-1), f["c_bf_2"][0].reshape(-1)
    for n in ("c_wq", "c_wk", "c_wv"):
        a[n] = chan(f[n + "_2"][0].reshape(D, 4))
    return {n: np.ascontiguousarray(v) for n, v in a.items()}


SCRATCH = {"line_scratch": (HEADS, TABLES, 2 * P)}
OUT = (P, KT, SEQ)


def kernel(**inputs):
    import numpy as np
    import concourse.bacc as bacc
    from concourse.bass_utils import run_bass_kernel_spmd

    nc = bacc.Bacc("TRN2", target_bir_lowering=False, num_devices=1)
    arrays = {**lay_out(inputs), **shape_constants()}
    aps = {n: nc.dram_tensor(f"in_{n}", v.shape, mybir.dt.from_np(v.dtype), kind="ExternalInput").ap() for n, v in arrays.items()}
    aps.update({n: nc.dram_tensor(n, s, F32, kind="Internal").ap() for n, s in SCRATCH.items()})
    out = nc.dram_tensor("out", OUT, F32, kind="ExternalOutput").ap()
    build(nc, aps, out)
    r = run_bass_kernel_spmd(nc, [{f"in_{n}": v for n, v in arrays.items()}], core_ids=[0])
    y = r.results[0]["out"]
    return np.ascontiguousarray(np.moveaxis(y, 1, 0).reshape(D, SEQ).T)[None]
```

```python
from contextlib import ExitStack

import concourse.bass as bass
from concourse import mybir

P = 128
F32 = mybir.dt.float32
F32R = mybir.dt.float32r
ALU = mybir.AluOpType
ACT = mybir.ActivationFunctionType
AX = mybir.AxisListType
NEG = -1e30

D, SEQ, CTX = 1024, 512, 256
KT = D // P
ALLTOK = CTX + SEQ
NCH = SEQ // P
EPS = 1e-6


def broadcast_rows(row, n):
    return bass.AP(tensor=row.tensor, offset=row.offset, ap=[[0, P], [1, n]])


def middle(ap, n):
    return bass.AP(tensor=ap.tensor, offset=ap.offset, ap=[ap.ap[0], [0, n], ap.ap[1]])


def last(ap, n):
    return bass.AP(tensor=ap.tensor, offset=ap.offset, ap=[ap.ap[0], ap.ap[1], [0, n]])


class Stage:

    number = [0]

    def __init__(self, nc, name):
        self.nc, self.name, self.cs, self.sems = nc, name, ExitStack(), []

    def __enter__(self):
        self.cs.__enter__()
        return self

    def __exit__(self, *e):
        self.cs.__exit__(*e)
        if self.sems:
            self.nc.clear_and_free_semaphores(self.sems)

    def sb(self, name, shape, dt=F32):
        return self.cs.enter_context(self.nc.sbuf_tensor(f"{self.name}_{name}", shape, dt))

    def pb(self, name, width=512):
        return self.cs.enter_context(self.nc.psum_tensor(f"{self.name}_{name}", [P, width], F32))

    def sem(self, name):
        free = list(self.nc.free_semaphores)
        later = [n for n in free if n > Stage.number[0]]
        Stage.number[0] = min(later or free)
        self.sems.append(self.nc.alloc_semaphore(f"{self.name}_{name}", num=Stage.number[0]))
        return self.sems[-1]


class Split:

    def __init__(self, st, name, shape):
        self.hi, self.lo = st.sb(name + "_hi", shape, F32R), st.sb(name + "_lo", shape, F32R)

    def tiles(self, n):
        return [(self.hi[:, k, :], self.lo[:, k, :]) for k in range(n)]


class Ring:

    def __init__(self, st, name, w, pieces, slots):
        self.w, self.NP, self.width = w, pieces, w.shape[2] // pieces
        self.raw = st.sb(name, [P, slots, self.width])
        self.loaded = [st.sem(f"{name}_loaded{r}") for r in range(slots)]

    def fetch_first(self, sp):
        for j in range(len(self.loaded)):
            o = j % self.NP * self.width
            sp.dma_start(self.raw[:, j, :], self.w[j // self.NP][:, o:o + self.width]).then_inc(self.loaded[j], 16)


def products(nc, name, w, pieces, banks, steps, unroll, temps=None, raw_slots=4, split=True, lo_engine="gpsimd", tall=P, extra=1,
             split_slots=2, max_sets=8, bank_step=None, ring=None):
    M, NP = w.shape[0], len(pieces)
    pw = w.shape[2] // NP
    sets = max(s for s in range(1, unroll + 1) if s * banks <= 8 and s <= max_sets and (unroll % s == 0 or unroll == M))
    assert M % unroll == 0 and pw * NP == w.shape[2], (name, M, unroll)
    groups, C = M // unroll, unroll * NP
    raw_slots = len(ring.loaded) if ring else raw_slots
    R = next(r for r in range(min(raw_slots, C), 0, -1) if C % r == 0)
    HS = split_slots
    AHEAD = NP + extra
    assert groups == 1 or (C % R == 0 and (C % HS == 0 or not split)), name
    with Stage(nc, name) as st:
        mine = ring or Ring(st, "weights", w, NP, R)
        raw, raw_loaded = mine.raw, mine.loaded
        if split:
            hi, lo = st.sb("hi", [P, HS, pw], F32R), st.sb("lo", [P, HS, pw], F32R)
        bank = [[st.pb(f"bank{s}_{i}") for i in range(banks)] for s in range(sets)]
        tmp = temps(st, sets) if temps else None
        hi_made, lo_made = st.sem("hi_made"), st.sem("lo_made")
        piece_used = st.sem("piece_used")
        psum_free = st.sem("psum_free")
        done = [st.sem(f"step_done{s}") for s in range(len(steps))]
        final = len(steps) - 1
        last_bank = final if bank_step is None else bank_step
        temps_free = done[final]
        block = st.cs.enter_context(nc.Block())
        raw_used, credit = (lo_made, 0) if split else (piece_used, HS)

        def over_groups(e, body):
            if groups > 1:
                with e.Fori(0, groups - 1) as i:
                    body(i, False)
            body(groups - 1, True)

        def make_hi(act, i, j):
            act.wait_ge(raw_loaded[j % R], i * (16 * (C // R)) + 16 * (j // R + 1))
            act.wait_ge(piece_used, i * C + (j + 1))
            act.activation(hi[:, j % HS, :], raw[:, j % R, :], ACT.Copy).then_inc(hi_made, 1)

        def make_lo(e, i, j):
            e.wait_ge(hi_made, i * C + (j + 1))
            e.tensor_tensor(lo[:, j % HS, :], raw[:, j % R, :], hi[:, j % HS, :].bitcast(F32), ALU.subtract).then_inc(lo_made, 1)

        @block.sync
        def _(sp):
            def fetch(i, j):
                m = i * unroll + j // NP
                sp.dma_start(raw[:, j % R, :], w[m][:, (j % NP) * pw:(j % NP + 1) * pw]).then_inc(raw_loaded[j % R], 16)

            if not ring:
                mine.fetch_first(sp)

            def body(i, end):
                for j in range(C - R if end else C):
                    sp.wait_ge(raw_used, i * C + (j + 1 + credit))
                    fetch(i, j + R)
            over_groups(sp, body)

        @block.tensor
        def _(pe):
            pe.nop().then_inc(piece_used, HS)

            def body(i, end):
                for b in range(unroll):
                    pe.wait_ge(psum_free, i * unroll + (b + 1))
                    for p, items in enumerate(pieces):
                        j = b * NP + p
                        if split:
                            pe.wait_ge(lo_made, i * C + (j + 1))
                        else:
                            pe.wait_ge(raw_loaded[j % R], i * (16 * (C // R)) + 16 * (j // R + 1))
                        for to, width, c0, c1, x, weights_move, start, stop in items:
                            out = bank[b % sets][to][0:tall, 0:width]
                            if split:
                                wh, wl, (xh, xl) = hi[:, j % HS, c0:c1], lo[:, j % HS, c0:c1], x
                                terms = [(wh, xh), (wh, xl), (wl, xh)]
                            else:
                                terms = [(raw[:, j % R, c0:c1], x)]
                            if weights_move:
                                terms = [(xx, ww) for ww, xx in terms]
                            for n, (stationary, moving) in enumerate(terms):
                                mm = pe.matmul(out, stationary, moving, start=start and n == 0, stop=stop and n == len(terms) - 1)
                        mm.then_inc(piece_used, 1)
            over_groups(pe, body)

        def engine_program(which):
            def program(e):
                if steps[last_bank][0] == which:
                    e.nop().then_inc(psum_free, sets)
                if last_bank < final and steps[final][0] == which:
                    e.nop().then_inc(temps_free, sets)
                make = {"scalar": make_hi, lo_engine: make_lo}.get(which) if split else None
                helped = split and lo_engine == "gpsimd"
                if helped and which == "vector":
                    make_lo(e, 0, 0)
                if make:
                    if helped and which == "gpsimd":
                        e.wait_ge(lo_made, 1)
                    for j in range(1 if helped and which == "gpsimd" else 0, min(AHEAD, C)):
                        make(e, 0, j)

                def body(i, end):
                    for b in range(unroll):
                        for j in range(b * NP + AHEAD, (b + 1) * NP + AHEAD):
                            if make and not (end and j >= C):
                                make(e, i, j)
                        for s, (who, f) in enumerate(steps):
                            if who == which:
                                if s == 0:
                                    e.wait_ge(piece_used, i * C + ((b + 1) * NP + HS))
                                elif s - 1 == last_bank:
                                    e.wait_ge(psum_free, i * unroll + (b + 1 + sets))
                                else:
                                    e.wait_ge(done[s - 1], i * unroll + (b + 1))
                                if s == 0 and last_bank < final:
                                    e.wait_ge(temps_free, i * unroll + (b + 1))
                                ins = f(e, i * unroll + b, b, bank[b % sets], tmp and tmp[b % sets])
                                ins.then_inc(psum_free if s == last_bank else done[s], 1)
                over_groups(e, body)
            return program

        working = {s[0] for s in steps} | ({"scalar", "vector", lo_engine} if split else set())
        for which, register in (("scalar", block.scalar), ("vector", block.vector), ("gpsimd", block.gpsimd)):
            if which in working:
                register(engine_program(which))


def project(nc, name, w, parts, cols, steps, unroll, per_piece=None, tall=P, **kw):
    ks = [(q, k, x) for q, moving in enumerate(parts) for k, x in enumerate(moving)]
    per_piece = per_piece or len(parts[0])
    split = kw.get("split", True)
    pieces = []
    for n, (q, k, x) in enumerate(ks):
        if n % per_piece == 0:
            pieces.append([])
        o = (n % per_piece) * tall
        for c, (t0, tw) in enumerate(cols):
            xs = tuple(z[:, t0:t0 + tw] for z in x) if split else x[:, t0:t0 + tw]
            pieces[-1].append((q * len(cols) + c, tw, o, o + tall, xs, 0, k == 0, k == len(parts[q]) - 1))
    nested = lambda banks: [banks[q * len(cols):(q + 1) * len(cols)] for q in range(len(parts))]
    wrap = lambda f: lambda e, m, b, banks, t: f(e, m, b, nested(banks), t)
    products(nc, name, w, pieces, len(parts) * len(cols), [(who, wrap(f)) for who, f in steps], unroll, tall=tall, **kw)


def token_major(nc, name, w, src, rows, step, unroll, per_piece, engine="scalar", **kw):
    width = w.shape[2] // len(src)
    pieces = []
    for k, x in enumerate(src):
        if k % per_piece == 0:
            pieces.append([])
        o = (k % per_piece) * width
        for r, row in enumerate(rows):
            pieces[-1].append((r, width, o, o + width, tuple(z[:, row] for z in x), 1, k == 0, k == len(src) - 1))

    def all_rows(e, n, b, banks, t):
        for r in range(len(rows)):
            ins = step(e, n, r, banks[r][0:kw.get("tall", P), 0:width])
        return ins
    products(nc, name, w, pieces, len(rows), [(engine, all_rows)], unroll, **kw)


def narrow(nc, name, w, src, cols, out, ident):
    width = out.shape[-1]
    T = cols[-1][0] + cols[-1][1]
    with Stage(nc, name) as st:
        channels = st.sb("channels", [width, T])

        def keep(e, m, b, banks, t):
            for c, (t0, tw) in enumerate(cols):
                ins = e.tensor_copy(channels[:, t0:t0 + tw], banks[0][c][0:width, 0:tw])
            return ins

        project(nc, name + "p", w, [src], cols, [("vector", keep)], unroll=1, tall=width)
        with Stage(nc, name + "t") as s2:
            bank, turned = s2.pb("bank"), s2.sem("turned")
            block = s2.cs.enter_context(nc.Block())

            @block.tensor
            def _(pe):
                for i in range(T // P):
                    mm = pe.transpose(bank[:, i * width:(i + 1) * width], channels[:, i * P:(i + 1) * P], ident[0:width, 0:width])
                mm.then_inc(turned, 1)

            @block.vector
            def _(dve):
                dve.wait_ge(turned, 1)
                dve.tensor_copy(out[:], bank[:, 0:T // P * width].rearrange("p (i w) -> p i w", w=width))


def split_up(nc, name, src, dst, n):
    with Stage(nc, name) as st:
        rounded = st.sem("rounded")
        block = st.cs.enter_context(nc.Block())

        @block.scalar
        def _(act):
            for k in range(n):
                act.activation(dst.hi[:, k, :], src[:, k, :], ACT.Copy).then_inc(rounded, 1)

        @block.vector
        def _(dve):
            for k in range(n):
                dve.wait_ge(rounded, k + 1)
                dve.tensor_tensor(dst.lo[:, k, :], src[:, k, :], dst.hi[:, k, :].bitcast(F32), ALU.subtract)


def sum_squares(nc, name, K, x, sums):
    with Stage(nc, name) as st:
        sq = st.sb("squares", [P, 2, sums.shape[-1]])
        squared, added = st.sem("squared"), st.sem("added")
        block = st.cs.enter_context(nc.Block())

        @block.scalar
        def _(act):
            for k in range(K):
                if k >= 2:
                    act.wait_ge(added, k - 1)
                act.activation(sq[:, k % 2, :], x[:, k, :], ACT.Square).then_inc(squared, 1)

        @block.vector
        def _(dve):
            dve.memset(sums, 0.0)
            for k in range(K):
                dve.drain()
                dve.wait_ge(squared, k + 1)
                dve.tensor_tensor(sums, sums, sq[:, k % 2, :], ALU.add).then_inc(added, 1)


def square_steps(source, sums, square_of):
    def square(e, m, b, banks, t):
        return e.activation(square_of(t), source(m), ACT.Square)

    def add(e, m, b, banks, t):
        return e.tensor_tensor(sums, sums, square_of(t), ALU.add)
    return [("scalar", square), ("vector", add)]


def rms_norm(nc, name, K, T, x, y, c, sums, gain, shift=None, residual=None, next_sums=None, clear=True,
             ahead=None):
    pair = y is not None and isinstance(y(0), tuple)
    NT = T // P
    SLOTS = 4
    result = residual or y
    on_pool = lambda k: k % 2 == 1
    with Stage(nc, name) as st:
        root = st.sb("root", [P, NT])
        tmp = st.sb("scaled", [P, SLOTS, T])
        sq = st.sb("squares", [P, 2, T]) if next_sums is not None else None
        total, rstd = st.pb("total"), st.pb("rstd")
        totaled, rooted, inverted, spread, scaled, rounded, rest_a, rest_b, finished, squared, added = (
            st.sem(n) for n in ("totaled", "rooted", "inverted", "spread", "scaled", "rounded", "rest_vector",
                                "rest_gpsimd", "finished", "squared", "added"))
        block = st.cs.enter_context(nc.Block())

        if ahead:
            block.sync(ahead.fetch_first)

        @block.tensor
        def _(pe):
            for i in range(NT):
                mm = pe.matmul(total[:, i:i + 1], sums[:, i * P:(i + 1) * P], c.one[:, 0:1], start=True, stop=True)
            mm.then_inc(totaled, 1)
            pe.wait_ge(inverted, 1)
            for i in range(NT):
                mm = pe.matmul(rstd[:, i * P:(i + 1) * P], root[:, i:i + 1].to_broadcast([P, P]), c.ident[:], start=True, stop=True)
            mm.then_inc(spread, 1)

        @block.scalar
        def _(act):
            act.wait_ge(totaled, 1)
            act.activation(root[:], total[:, 0:NT], ACT.Sqrt, bias=c.eps, scale=1.0 / (K * P)).then_inc(rooted, 1)
            for k in range(K):
                t = tmp[:, k % SLOTS, :]
                if pair:
                    act.wait_ge(scaled, k + 1)
                    if shift is not None:
                        act.activation(t, t, ACT.Identity, bias=shift(k))
                        act.drain()
                    act.activation(y(k)[0], t, ACT.Copy).then_inc(rounded, 1)
                elif next_sums is not None:
                    act.wait_ge(finished, k + 1)
                    if k >= 2:
                        act.wait_ge(added, k - 1)
                    act.activation(sq[:, k % 2, :], result(k), ACT.Square).then_inc(squared, 1)

        def rest(e, k):
            e.wait_ge(rounded, k + 1)
            e.tensor_tensor(y(k)[1], tmp[:, k % SLOTS, :], y(k)[0].bitcast(F32), ALU.subtract).then_inc(
                rest_b if on_pool(k) else rest_a, 1)

        @block.vector
        def _(dve):
            def scale(k):
                if pair and k >= SLOTS:
                    if on_pool(k - SLOTS):
                        dve.wait_ge(rest_b, (k - SLOTS) // 2 + 1)
                    else:
                        dve.wait_ge(rest_a, (k - SLOTS) // 2 + 1)
                to = tmp[:, k % SLOTS, :] if pair or residual else y(k)
                ins = dve.scalar_tensor_tensor(out=to, in0=x(k), scalar=gain(k), in1=rstd[:, 0:T], op0=ALU.mult, op1=ALU.mult)
                ins.then_inc(scaled if pair or residual else finished, 1)

            dve.wait_ge(rooted, 1)
            dve.reciprocal(root[:], root[:]).then_inc(inverted, 1)
            dve.wait_ge(spread, 1)
            for k in range(K + 1):
                if k < K:
                    scale(k)
                if k >= 1 and pair and not on_pool(k - 1):
                    rest(dve, k - 1)
                if k >= 1 and residual:
                    dve.wait_ge(scaled, k)
                    dve.tensor_tensor(residual(k - 1), residual(k - 1), tmp[:, (k - 1) % SLOTS, :], ALU.add).then_inc(finished, 1)

        @block.gpsimd
        def _(pool):
            if clear:
                pool.wait_ge(totaled, 1)
                pool.memset(sums, 0.0)
            for k in range(K):
                if pair and on_pool(k):
                    rest(pool, k)
                if next_sums is not None:
                    pool.wait_ge(squared, k + 1)
                    pool.drain()
                    pool.tensor_tensor(next_sums, next_sums, sq[:, k % 2, :], ALU.add).then_inc(added, 1)


HEADS, DH = 8, 64
DIL = 4
TABLES = 2 * DIL - 1 + 2


def bias_tables(nc, name, rel, onehot, neg_row, scratch, flip, table):
    with Stage(nc, name) as st:
        rel_sb = st.sb("rel", [33, 3 * HEADS])
        hot = st.sb("hot", [33, TABLES, 2 * P])
        line = st.sb("line", [HEADS, TABLES, 2 * P])
        shifted = st.sb("shifted", [P, 2, TABLES * P])
        banks = [st.pb(f"bank{i}") for i in range(TABLES // 2 + 1)]
        turned = [st.pb(f"turned{i}") for i in range(3)]
        loaded, made, copied, kept, flipped, taken = (
            st.sem(n) for n in ("loaded", "made", "copied", "kept", "flipped", "taken"))
        spread = [st.sem(f"spread{i}") for i in range(2)]
        block = st.cs.enter_context(nc.Block())
        W = TABLES * P // 3
        assert W <= 512

        @block.sync
        def _(sp):
            sp.dma_start(rel_sb[0:32, :], rel).then_inc(loaded, 16)
            sp.dma_start(rel_sb[32:33, :], neg_row).then_inc(loaded, 16)
            sp.dma_start(hot[:], onehot).then_inc(loaded, 16)
            sp.wait_ge(copied, TABLES)
            sp.dma_start(scratch, line[:]).then_inc(kept, 16)
            sp.wait_ge(kept, 16)
            for h in range(HEADS):
                if h >= 2:
                    sp.wait_ge(flipped, 3 * (h - 1))
                src = bass.AP(tensor=scratch.tensor, offset=scratch.offset + h * TABLES * 2 * P,
                              ap=[[1, P], [2 * P, TABLES], [1, P]])
                sp.dma_start(shifted[:, h % 2, :].rearrange("p (t n) -> p t n", t=TABLES), src).then_inc(spread[h % 2], 16)

        @block.tensor
        def _(pe):
            pe.wait_ge(loaded, 48)
            for t in range(TABLES):
                g = max(0, t - (TABLES - 3))
                pe.matmul(banks[t // 2][0:HEADS, (t % 2) * 2 * P:(t % 2 + 1) * 2 * P],
                          rel_sb[:, g * HEADS:(g + 1) * HEADS], hot[:, t, :], start=True, stop=True).then_inc(made, 1)
            for h in range(HEADS):
                pe.wait_ge(spread[h % 2], 16 * (h // 2 + 1))
                for i in range(3):
                    if h >= 1:
                        pe.wait_ge(taken, 3 * (h - 1) + i + 1)
                    pe.matmul(turned[i][:, 0:W], flip[:], shifted[:, h % 2, i * W:(i + 1) * W], start=True, stop=True).then_inc(flipped, 1)

        @block.vector
        def _(dve):
            for t in range(TABLES):
                dve.wait_ge(made, min(TABLES, t // 2 * 2 + 2))
                dve.tensor_copy(line[:, t, :], banks[t // 2][0:HEADS, (t % 2) * 2 * P:(t % 2 + 1) * 2 * P]).then_inc(copied, 1)
            for h in range(HEADS):
                for i in range(3):
                    dve.wait_ge(flipped, 3 * h + i + 1)
                    dve.tensor_copy(table[:, h, :, :].rearrange("p t n -> p (t n)")[:, i * W:(i + 1) * W], turned[i][:, 0:W]).then_inc(taken, 1)


def attention(nc, name, q, k, v, table, out, ident):
    units = [(h, r) for h in range(HEADS) for r in range(DIL)]
    NU, NK = len(units), SEQ + 2 * P
    with Stage(nc, name) as st:
        logits = st.sb("logits", [P, 2, NK])
        probs = st.sb("probs", [P, 2, NK])
        probs_t = st.sb("probs_t", [P, 2, NK])
        negmax = st.sb("negmax", [P, NU])
        den = st.sb("den", [P, NU])
        rden = st.sb("rden", [P, NU])
        score = [st.pb(f"score{i}", 1024) for i in range(2)]
        turned = st.pb("turned", 1024)
        outs = [st.pb(f"outs{i}") for i in range(2)]
        scored, biased, maxed, exped, normed, transposed, copied, mixed, stored = (
            st.sem(n) for n in ("scored", "biased", "maxed", "exped", "normed", "transposed", "copied", "mixed", "stored"))
        block = st.cs.enter_context(nc.Block())

        @block.tensor
        def _(pe):
            def scores(n):
                h, r = units[n]
                p0, t = DH * (h % 2), h // 2
                if n >= 2:
                    pe.wait_ge(biased, n - 1)
                for g in range(3):
                    qg = q[p0:p0 + DH, 4 * g + t, r * P:(r + 1) * P]
                    kg = k[p0:p0 + DH, 4 * g + t, :] if g == 0 else k[p0:p0 + DH, 4 * g + t, r * P:(r + 1) * P]
                    o = 0 if g == 0 else SEQ + (g - 1) * P
                    mm = pe.matmul(score[n % 2][:, o:o + (SEQ if g == 0 else P)], qg, kg, start=True, stop=True)
                mm.then_inc(scored, 1)

            def turn(n):
                pe.wait_ge(normed, n + 1)
                if n >= 1:
                    pe.wait_ge(copied, n)
                for t in range(NK // P):
                    mm = pe.transpose(turned[:, t * P:(t + 1) * P], probs[:, n % 2, t * P:(t + 1) * P], ident[:])
                mm.then_inc(transposed, 1)

            def mix(n):
                h, r = units[n]
                pe.wait_ge(copied, n + 1)
                pair = h // 2
                if h % 2 == 0 and r == 0 and pair >= 2:
                    pe.wait_ge(stored, pair - 1)
                for t in range(NK // P):
                    g = max(0, t - 3)
                    row = t if g == 0 else r
                    mm = pe.matmul(outs[pair % 2][DH * (h % 2):DH * (h % 2) + DH, r * P:(r + 1) * P],
                                   v[:, row, (g * HEADS + h) * DH:(g * HEADS + h + 1) * DH],
                                   probs_t[:, n % 2, t * P:(t + 1) * P], start=(t == 0), stop=(t == NK // P - 1))
                mm.then_inc(mixed, 1)

            scores(0)
            scores(1)
            for n in range(NU):
                if n + 2 < NU:
                    scores(n + 2)
                turn(n)
                if n >= 1:
                    mix(n - 1)
            mix(NU - 1)

        @block.vector
        def _(dve):
            def bias(n):
                h, r = units[n]
                dve.wait_ge(scored, n + 1)
                if n >= 2:
                    dve.wait_ge(exped, n - 1)
                dve.scalar_tensor_tensor(out=logits[:, n % 2, 0:SEQ], in0=score[n % 2][:, 0:SEQ], scalar=DH ** -0.5,
                                         in1=table[:, h, DIL - 1 - r:2 * DIL - 1 - r, :].rearrange("p a b -> p (a b)"),
                                         op0=ALU.mult, op1=ALU.add)
                dve.scalar_tensor_tensor(out=logits[:, n % 2, SEQ:NK], in0=score[n % 2][:, SEQ:NK], scalar=DH ** -0.5,
                                         in1=table[:, h, 2 * DIL - 1:TABLES, :].rearrange("p a b -> p (a b)"),
                                         op0=ALU.mult, op1=ALU.add).then_inc(biased, 1)
                dve.drain()
                dve.tensor_reduce(negmax[:, n:n + 1], logits[:, n % 2, :], AX.X, ALU.max, negate=True).then_inc(maxed, 1)

            def normalise(n):
                dve.wait_ge(exped, n + 1)
                dve.reciprocal(rden[:, n:n + 1], den[:, n:n + 1])
                dve.drain()
                dve.tensor_scalar(probs[:, n % 2, :], probs[:, n % 2, :], rden[:, n:n + 1], None, ALU.mult).then_inc(normed, 1)

            for n in range(NU + 1):
                if n < NU:
                    bias(n)
                if n >= 1:
                    normalise(n - 1)

        @block.scalar
        def _(act):
            def exp(n):
                act.wait_ge(maxed, n + 1)
                if n >= 2:
                    act.wait_ge(transposed, n - 1)
                act.activation(probs[:, n % 2, :], logits[:, n % 2, :], ACT.Exp, bias=negmax[:, n:n + 1],
                               accum_out=den[:, n:n + 1]).then_inc(exped, 1)

            def copy(n):
                act.wait_ge(transposed, n + 1)
                if n >= 2:
                    act.wait_ge(mixed, n - 1)
                act.activation(probs_t[:, n % 2, 0:SEQ], turned[:, 0:SEQ], ACT.Copy)
                act.activation(probs_t[:, n % 2, SEQ:NK], turned[:, SEQ:NK], ACT.Copy).then_inc(copied, 1)
                if n % (2 * DIL) == 2 * DIL - 1:
                    pair = n // (2 * DIL)
                    act.wait_ge(mixed, n + 1)
                    act.activation(out[:, pair, :].rearrange("p (i r) -> p r i", r=DIL),
                                   outs[pair % 2][:].rearrange("p (r i) -> p r i", r=DIL), ACT.Copy).then_inc(stored, 1)

            for n in range(NU + 1):
                if n < NU:
                    exp(n)
                if n >= 1:
                    copy(n - 1)


GROUPS, GH, SHD, NSTATE = 4, 8, 64, 128
GW = GH * SHD
SH = GROUPS * GH


def ssd_decays(nc, name, d, dt_raw, dt_bias, a_log, d_skip, one, upper):
    CH = NCH * SH
    with Stage(nc, name) as st:
        bias_sb, alog_sb = (st.sb(n, [P, SH]) for n in ("dt_bias", "a_log"))
        raw, soft = (st.sb(n, [P, CH]) for n in ("raw", "soft"))
        la_ps, last_ps = st.pb("la"), st.pb("last")
        loaded, absd, softened, raised, cumd, prepared = (
            st.sem(n) for n in ("loaded", "absd", "softened", "raised", "cumd", "prepared"))
        block = st.cs.enter_context(nc.Block())

        @block.sync
        def _(sp):
            for dst, src in ((bias_sb, dt_bias), (alog_sb, a_log), (d.skip, d_skip)):
                sp.dma_start(dst[:], broadcast_rows(src, SH)).then_inc(loaded, 16)

        @block.vector
        def _(dve):
            dve.wait_ge(loaded, 48)
            dve.tensor_tensor(raw[:].rearrange("p (c h) -> p c h", c=NCH), dt_raw[:],
                              middle(bias_sb[:], NCH), ALU.add).then_inc(absd, 1)
            dve.wait_ge(softened, 1)
            dve.scalar_tensor_tensor(out=d.dt[:], in0=raw[:], scalar=0.0, in1=soft[:], op0=ALU.max, op1=ALU.add)
            dve.drain()
            dve.scalar_tensor_tensor(out=d.dta[:].rearrange("p (c h) -> p c h", c=NCH),
                                     in0=d.dt[:].rearrange("p (c h) -> p c h", c=NCH), scalar=-1.0,
                                     in1=middle(alog_sb[:], NCH), op0=ALU.mult, op1=ALU.mult).then_inc(raised, 1)
            dve.wait_ge(cumd, 1)
            dve.tensor_scalar(d.negla[:], la_ps[:, 0:CH], -1.0, None, ALU.mult)
            dve.drain()
            dve.tensor_tensor(raw[:], last_ps[:, 0:CH], d.negla[:], ALU.add).then_inc(prepared, 1)
            dve.wait_ge(softened, 2)
            dve.tensor_tensor(d.toend[:], d.toend[:], d.dt[:], ALU.mult)

        @block.scalar
        def _(act):
            act.wait_ge(loaded, 48)
            act.activation(alog_sb[:], alog_sb[:], ACT.Exp)
            act.wait_ge(absd, 1)
            act.activation(soft[:], raw[:], ACT.Abs)
            act.drain()
            act.activation(soft[:], soft[:], ACT.Exp, scale=-1.0)
            act.drain()
            act.activation(soft[:], soft[:], ACT.Ln, bias=one[:, 0:1]).then_inc(softened, 1)
            act.wait_ge(prepared, 1)
            act.activation(d.expla[:], la_ps[:, 0:CH], ACT.Exp)
            act.activation(d.elast[:], last_ps[:, 0:CH], ACT.Exp)
            act.activation(d.toend[:], raw[:], ACT.Exp).then_inc(softened, 1)

        @block.tensor
        def _(pe):
            pe.wait_ge(raised, 1)
            pe.matmul(la_ps[:, 0:CH], upper[:], d.dta[:], start=True, stop=True)
            pe.matmul(last_ps[:, 0:CH], one[:], d.dta[:], start=True, stop=True).then_inc(cumd, 1)


def ssd_scan(nc, name, d, x, bc, z, norm_w, ident, upper, neg_lower, eps):
    units = [(c, g) for c in range(NCH) for g in range(GROUPS)]
    NU = len(units)
    BM, CM = 0, GROUPS
    TPG = GW // P
    with Stage(nc, name) as st:
        state = st.sb("state", [P, GROUPS, GW])
        xtok = st.sb("xtok", [P, 3, GW])
        xend = st.sb("xend", [P, 2, GW])
        btok = st.sb("btok", [P, 2, P])
        decay = st.sb("decay", [P, GH, P])
        mix = st.sb("mix", [P, 2, GH, P])
        y, t1 = st.sb("y", [P, 2, GW]), st.sb("t1", [P, GW])
        sq = st.sb("sq", [P, GW])
        ss, rstd = st.sb("ss", [P, NU]), st.sb("rstd", [P, NU])
        xturn, bturn, la0, la1, yin, yst, upd, yturn = (
            st.pb(n) for n in ("xturn", "bturn", "la0", "la1", "yin", "yst", "upd", "yturn"))
        las = (la0, la1)
        names = ("turned", "tokens", "spread", "decayed", "mixed", "ended", "produced", "gated",
                 "rooted", "normed", "turned_back", "stored", "stated")
        (turned, tokens, spread, decayed, mixed, ended, produced, gated,
         rooted, normed, turned_back, stored, stated) = (st.sem(n) for n in names)
        block = st.cs.enter_context(nc.Block())

        def where(n):
            c, g = units[n]
            return c, g, slice(c * P, (c + 1) * P), c * SH + g * GH

        @block.tensor
        def _(pe):
            def front(n):
                c, g, ts, h0 = where(n)
                if n >= 1:
                    pe.wait_ge(tokens, n)
                    pe.wait_ge(mixed, n)
                    pe.wait_ge(decayed, n)
                for t in range(TPG):
                    pe.transpose(xturn[:, t * P:(t + 1) * P], x[:, TPG * g + t, ts], ident[:])
                pe.transpose(bturn[:, 0:P], bc[:, BM + g, ts], ident[:])
                pe.matmul(bturn[:, P:2 * P], bc[:, BM + g, ts], bc[:, CM + g, ts], start=True, stop=True).then_inc(turned, 1)
                for h in range(GH):
                    bank = las[h // 4][:, (h % 4) * P:(h % 4 + 1) * P]
                    pe.matmul(bank, d.dta[:, h0 + h:h0 + h + 1].to_broadcast([P, P]), upper[:], start=True, stop=False)
                    mm = pe.matmul(bank, ident[:], neg_lower[:], start=False, stop=True)
                mm.then_inc(spread, 1)

            def outputs(n):
                c, g, ts, h0 = where(n)
                if n >= 1:
                    pe.wait_ge(stated, n)
                pe.wait_ge(mixed, n + 1)
                for h in range(GH):
                    pe.matmul(yin[:, h * SHD:(h + 1) * SHD], mix[:, n % 2, h, :], xtok[:, n % 3, h * SHD:(h + 1) * SHD],
                              start=True, stop=True)
                if c >= 1:
                    pe.matmul(yst[:], bc[:, CM + g, ts], state[:, g, :], start=True, stop=True)
                pe.wait_ge(ended, n + 1)
                pe.matmul(upd[:], btok[:, n % 2, :], xend[:, n % 2, :], start=True, stop=True).then_inc(produced, 1)

            def turn_back(n):
                pe.wait_ge(normed, n + 1)
                if n >= 1:
                    pe.wait_ge(stored, n)
                for t in range(TPG):
                    mm = pe.transpose(yturn[:, t * P:(t + 1) * P], y[:, n % 2, t * P:(t + 1) * P], ident[:])
                mm.then_inc(turned_back, 1)

            front(0)
            front(1)
            for n in range(NU):
                outputs(n)
                if n + 2 < NU:
                    front(n + 2)
                if n >= 1:
                    turn_back(n - 1)
            turn_back(NU - 1)

        @block.scalar
        def _(act):
            def front(n):
                c, g, ts, h0 = where(n)
                act.wait_ge(turned, n + 1)
                if n >= 2:
                    act.wait_ge(produced, n - 1)
                if n >= 3:
                    act.wait_ge(gated, n - 2)
                act.activation(xtok[:, n % 3, :], xturn[:], ACT.Copy)
                act.activation(btok[:, n % 2, :], bturn[:, 0:P], ACT.Copy).then_inc(tokens, 1)
                act.wait_ge(spread, n + 1)
                if n >= 1:
                    act.wait_ge(mixed, n)
                for h in range(GH):
                    ins = act.activation(decay[:, h, :], las[h // 4][:, (h % 4) * P:(h % 4 + 1) * P], ACT.Exp,
                                         bias=d.negla[:, h0 + h:h0 + h + 1])
                ins.then_inc(decayed, 1)

            def root(n):
                act.wait_ge(gated, n + 1)
                act.activation(sq[:], t1[:], ACT.Square, accum_out=ss[:, n:n + 1])
                act.drain()
                act.activation(rstd[:, n:n + 1], ss[:, n:n + 1], ACT.Sqrt, bias=eps, scale=1.0 / GW).then_inc(rooted, 1)

            def store(n):
                c, g, ts, h0 = where(n)
                act.wait_ge(turned_back, n + 1)
                for t in range(TPG):
                    ins = act.activation(x[:, TPG * g + t, ts], yturn[:, t * P:(t + 1) * P], ACT.Copy,
                                         scale=norm_w[:, TPG * g + t:TPG * g + t + 1])
                ins.then_inc(stored, 1)

            front(0)
            front(1)
            for n in range(NU):
                if n + 2 < NU:
                    front(n + 2)
                root(n)
                if n >= 1:
                    store(n - 1)
            store(NU - 1)

        @block.vector
        def _(dve):
            by_head = lambda ap: ap.rearrange("p (h d) -> p h d", h=GH)

            def weigh(n):
                c, g, ts, h0 = where(n)
                dve.wait_ge(tokens, n + 1)
                dve.wait_ge(decayed, n + 1)
                if n >= 2:
                    dve.wait_ge(produced, n - 1)
                for h in range(GH):
                    ins = dve.scalar_tensor_tensor(out=mix[:, n % 2, h, :], in0=decay[:, h, :], scalar=d.dt[:, h0 + h:h0 + h + 1],
                                                   in1=bturn[:, P:2 * P], op0=ALU.mult, op1=ALU.mult)
                ins.then_inc(mixed, 1)
                dve.tensor_tensor(by_head(xend[:, n % 2, :]), by_head(xtok[:, n % 3, :]), last(d.toend[:, h0:h0 + GH], SHD),
                                  ALU.mult).then_inc(ended, 1)

            def combine(n):
                c, g, ts, h0 = where(n)
                if n >= 2:
                    dve.wait_ge(turned_back, n - 1)
                dve.tensor_tensor(by_head(y[:, n % 2, :]), by_head(xtok[:, n % 3, :]), last(d.skip[:, g * GH:(g + 1) * GH], SHD), ALU.mult)
                dve.wait_ge(produced, n + 1)
                if n >= 1:
                    dve.wait_ge(normed, n)
                sg = by_head(state[:, g, :])
                if c >= 1:
                    dve.tensor_tensor(by_head(t1[:]), by_head(yst[:]), last(d.expla[:, h0:h0 + GH], SHD), ALU.mult)
                    dve.tensor_tensor(sg, sg, last(d.elast[:, h0:h0 + GH], SHD), ALU.mult)
                    dve.drain()
                    dve.tensor_tensor(t1[:], t1[:], yin[:], ALU.add)
                else:
                    dve.tensor_copy(t1[:], yin[:])
                dve.tensor_tensor(state[:, g, :], state[:, g, :], upd[:], ALU.add).then_inc(stated, 1)
                dve.drain()
                dve.tensor_tensor(t1[:], t1[:], y[:, n % 2, :], ALU.add)
                dve.drain()
                dve.tensor_tensor(t1[:], t1[:], z[:, c, g * GW:(g + 1) * GW], ALU.mult).then_inc(gated, 1)

            def normalise(n):
                dve.wait_ge(rooted, n + 1)
                dve.reciprocal(rstd[:, n:n + 1], rstd[:, n:n + 1])
                dve.drain()
                dve.tensor_scalar(y[:, n % 2, :], t1[:], rstd[:, n:n + 1], None, ALU.mult).then_inc(normed, 1)

            dve.memset(state[:], 0.0)
            dve.drain()
            weigh(0)
            weigh(1)
            for n in range(NU):
                combine(n)
                if n + 2 < NU:
                    weigh(n + 2)
                normalise(n)


class Decays:
    def __init__(self, st):
        self.dt, self.dta, self.negla, self.expla, self.toend, self.elast = (
            st.sb(n, [P, NCH * SH]) for n in ("dt", "dta", "negla", "expla", "toend", "elast"))
        self.skip = st.sb("d_skip", [P, SH])


def load(nc, name, pairs):
    with Stage(nc, name) as st:
        loaded = st.sem("loaded")
        block = st.cs.enter_context(nc.Block())

        @block.sync
        def _(sp):
            for dst, src in pairs:
                sp.dma_start(dst, src).then_inc(loaded, 16)
            sp.wait_ge(loaded, 16 * len(pairs))


def first_block(nc, a, x, c, tap):
    AT, QT = 12, 24

    def norm_of_x(name, xn, w, clear=True, ahead=None):
        rms_norm(nc, name, KT, SEQ, lambda k: x[:, k, :], lambda k: (xn.hi[:, k, :], xn.lo[:, k, :]), c, sums,
                 gain=lambda k: w[:, k:k + 1], clear=clear, ahead=ahead)

    sums = c.sums[:, CTX:ALLTOK]

    def add(e, m, b, banks, t):
        ins = e.tensor_tensor(x[:, m, :], x[:, m, :], banks[0][0][:], ALU.add)
        e.drain()
        return ins

    add_to_x = [("vector", add)] + square_steps(lambda m: x[:, m, :], sums, lambda t: t[:])
    squares = lambda s, n: [s.sb(f"square{i}", [P, SEQ]) for i in range(n)]

    with Stage(nc, "mixer1") as mixer:
        attn_parts = Split(mixer, "attn", [P, HEADS * DH // P, SEQ])
        with Stage(nc, "att") as st:
            qk = st.sb("qk", [P, QT, SEQ])
            v = st.sb("v", [P, DIL, AT * P])
            with Stage(nc, "attin") as s2:
                xn = Split(s2, "xn", [P, KT, SEQ])
                ring = Ring(s2, "weights", a["w_qk"], 1, 4)
                norm_of_x("norm1", xn, c.norm1, clear=False, ahead=ring)
                project(nc, "qk", a["w_qk"], [xn.tiles(KT)], [(0, SEQ)],
                        [("vector", lambda e, m, b, banks, t: e.tensor_copy(
                            qk[:, m, :].rearrange("p (r i) -> p r i", r=DIL),
                            banks[0][0][:].rearrange("p (i r) -> p r i", r=DIL)))], unroll=4, ring=ring)
                token_major(nc, "v", a["w_v"], xn.tiles(KT), [slice(r, SEQ, DIL) for r in range(DIL)],
                            lambda e, n, r, bank: e.tensor_copy(v[:, r, n * 512:(n + 1) * 512], bank),
                            unroll=3, per_piece=2, engine="vector")
            tap("qk", qk)
            table = st.sb("table", [P, HEADS, TABLES, P])
            attn = st.sb("out", [P, HEADS * DH // P, SEQ])
            bias_tables(nc, "bias", a["rel_bias"], a["bias_onehot"], a["neg_row"], a["line_scratch"], c.flip, table)
            attention(nc, "attend", qk[:, 0:AT, :], qk[:, AT:QT, :], v, table, attn, c.ident)
            tap("attn", attn)
            split_up(nc, "attn_parts", attn, attn_parts, HEADS * DH // P)
        with Stage(nc, "ssm") as st:
            xn = Split(st, "xn", [P, KT, SEQ])
            norm_of_x("norm1b", xn, c.norm1)
            ssm = st.sb("ssm", [P, SH * SHD // P, SEQ])
            with Stage(nc, "ssmin") as s2:
                bc = s2.sb("bc", [P, 8, SEQ])
                z = s2.sb("z", [P, NCH, SH * SHD])
                dt_raw = s2.sb("dt_raw", [P, NCH, SH])
                d = Decays(s2)
                rows = [slice(i * P, (i + 1) * P) for i in range(NCH)]
                narrow(nc, "dt", a["w_dt"], xn.tiles(KT), [(0, SEQ)], dt_raw, c.ident)
                ssd_decays(nc, "decays", d, dt_raw, a["dt_bias"], a["a_log"], a["d_skip"], c.one, c.upper)

                for part, w, buf, m0 in (("x", "w_x", ssm, 0), ("bc", "w_bc", bc, 16)):
                    def conv(e, m, b, banks, acc):
                        bank = banks[0][0]
                        e.tensor_scalar(acc[:], bank[:], c.conv_w[:, m + m0, 3:4], None, ALU.mult)
                        for j in range(1, 4):
                            e.drain()
                            ins = e.scalar_tensor_tensor(out=acc[:, j:SEQ], in0=bank[:, 0:SEQ - j],
                                                         scalar=c.conv_w[:, m + m0, 3 - j:4 - j], in1=acc[:, j:SEQ],
                                                         op0=ALU.mult, op1=ALU.add)
                        return ins

                    project(nc, part, a[w], [xn.tiles(KT)], [(0, SEQ)],
                            [("vector", conv),
                             ("scalar", lambda e, m, b, banks, acc: e.activation(buf[:, m, :], acc[:], ACT.Silu,
                                                                                bias=c.conv_b[:, m + m0, :]))],
                            unroll=4, temps=lambda s, n: [s.sb(f"acc{i}", [P, SEQ]) for i in range(n)])
                tap("xs", ssm)
                tap("bc", bc)
                token_major(nc, "z", a["w_z"], xn.tiles(KT), rows,
                            lambda e, n, r, bank: e.activation(z[:, r, n * 512:(n + 1) * 512], bank, ACT.Silu),
                            unroll=4, per_piece=2)
                ssd_scan(nc, "scan", d, ssm, bc, z, c.ssm_norm, c.ident, c.upper, c.neg_lower, c.eps)
            tap("ssm", ssm)
            merged = ssm[:, 0:KT, :]
            with Stage(nc, "merging") as s2:
                ssm_parts = Split(s2, "ssm", [P, SH * SHD // P, SEQ])
                split_up(nc, "ssm_parts", ssm, ssm_parts, SH * SHD // P)

                def gates(e, m, b, banks, t):
                    e.activation(t[0][:], banks[0][0][:], ACT.Sigmoid)
                    return e.activation(t[1][:], banks[1][0][:], ACT.Sigmoid)

                def merge(e, m, b, banks, t):
                    e.tensor_tensor(t[0][:], t[0][:], banks[2][0][:], ALU.mult)
                    e.tensor_tensor(t[1][:], t[1][:], banks[3][0][:], ALU.mult)
                    e.drain()
                    return e.tensor_tensor(merged[:, m, :], t[0][:], t[1][:], ALU.add)

                project(nc, "merge", a["w_merge"], [xn.tiles(KT), xn.tiles(KT), attn_parts.tiles(4), ssm_parts.tiles(16)],
                        [(0, SEQ)], [("scalar", gates), ("vector", merge)], unroll=2, per_piece=6, extra=0,
                        temps=lambda s, n: [[s.sb(f"gate{i}_{j}", [P, SEQ]) for j in range(2)] for i in range(n)])
            with Stage(nc, "outs") as s2:
                merged_parts = Split(s2, "merged", [P, KT, SEQ])
                split_up(nc, "merged_parts", merged, merged_parts, KT)
                project(nc, "out", a["w_out"], [merged_parts.tiles(KT)], [(0, SEQ)], add_to_x, unroll=4, temps=squares)
    tap("h1", x)
    with Stage(nc, "ffn1") as st:
        hidden = Split(st, "hidden", [P, 22, SEQ])
        with Stage(nc, "ffn1in") as s2:
            xn = Split(s2, "xn", [P, KT, SEQ])
            ring = Ring(s2, "weights", a["w_ffn_in"], 2, 4)
            norm_of_x("norm2", xn, c.norm2, ahead=ring)
            project(nc, "up", a["w_ffn_in"], [xn.tiles(KT)] * 2, [(0, SEQ)],
                    [("scalar", lambda e, m, b, banks, t: e.activation(t[:], banks[0][0][:], ACT.Silu)),
                     ("vector", lambda e, m, b, banks, t: e.tensor_tensor(t[:], t[:], banks[1][0][:], ALU.mult)),
                     ("scalar", lambda e, m, b, banks, t: e.activation(hidden.hi[:, m, :], t[:], ACT.Copy)),
                     ("vector", lambda e, m, b, banks, t: e.tensor_tensor(
                         hidden.lo[:, m, :], t[:], hidden.hi[:, m, :].bitcast(F32), ALU.subtract))],
                    unroll=2, ring=ring, temps=lambda s, n: [s.sb(f"gate{i}", [P, SEQ]) for i in range(n)])
        project(nc, "down", a["w_ffn_out"], [hidden.tiles(22)], [(0, SEQ)], add_to_x, unroll=2, per_piece=11, temps=squares)
    tap("h2", x)


MOD = 6
SEQS = [(0, CTX), (CTX, SEQ)]
CHUNKS = ALLTOK // P
CTXCH = CTX // P
ORDER = [list(range(CHUNKS)), list(range(CTXCH))[::-1] + list(range(CTXCH, CHUNKS))[::-1]]
UNITS = [(d, ch) for d in range(2) for ch in ORDER[d]]


def modulations(nc, name, w, bias, cvec, ident, mods):
    N = w.shape[0]
    with Stage(nc, name) as st:
        rows = st.sb("rows", [2, N, 512])
        token_major(nc, name + "p", w, cvec.tiles(KT), [slice(0, 2)],
                    lambda e, n, r, bank: e.activation(rows[:, n, :], bank, ACT.Copy),
                    unroll=4, per_piece=2, raw_slots=8, split_slots=4, lo_engine="vector", tall=2)
        with Stage(nc, name + "t") as s2:
            bank = s2.pb("bank")
            turned = s2.sem("turned")
            block = s2.cs.enter_context(nc.Block())

            @block.tensor
            def _(pe):
                for i in range(4 * N):
                    mm = pe.transpose(bank[:, 2 * i:2 * i + 2], rows[:, i // 4, i % 4 * P:(i % 4 + 1) * P], ident[0:2, 0:2])
                mm.then_inc(turned, 1)

            @block.vector
            def _(dve):
                dve.wait_ge(turned, 1)
                dve.tensor_tensor(mods[:], bank[:, 0:8 * N].rearrange("p (i s) -> p i s", s=2), bias[:], ALU.add)


def modulation_gains(nc, name, layers):
    with Stage(nc, name) as st:
        block = st.cs.enter_context(nc.Block())

        @block.vector
        def _(dve):
            for L in layers:
                for i, pre, post in ((0, L.mix_pre, L.mix_post), (3, L.ffn_pre, L.ffn_post)):
                    scale, gate = (L.mods[:, (i + j) * KT:(i + j + 1) * KT, :] for j in (1, 2))
                    dve.scalar_tensor_tensor(out=scale, in0=scale, scalar=1.0, in1=last(pre[:], 2), op0=ALU.add, op1=ALU.mult)
                    dve.tensor_tensor(gate, gate, last(post[:], 2), ALU.mult)


def silu_columns(nc, name, buf):
    with Stage(nc, name) as st:
        block = st.cs.enter_context(nc.Block())

        @block.scalar
        def _(act):
            act.activation(buf, buf, ACT.Silu)


def conv3(e, out, x, w, n):
    e.tensor_scalar(out, x, w(1), None, ALU.mult)
    e.drain()
    e.scalar_tensor_tensor(out=out[:, 1:n], in0=x[:, 0:n - 1], scalar=w(0), in1=out[:, 1:n], op0=ALU.mult, op1=ALU.add)
    e.drain()
    return e.scalar_tensor_tensor(out=out[:, 0:n - 1], in0=x[:, 1:n], scalar=w(2), in1=out[:, 0:n - 1],
                                  op0=ALU.mult, op1=ALU.add)


def conv_grid(e, out, x, w):
    R, C = SEQ // 64, 64
    o3, x3 = (ap.rearrange("p (r c) -> p r c", c=C) for ap in (out, x))
    ins = e.tensor_scalar(out, x, w(1, 1), None, ALU.mult)
    for a in range(3):
        for b in range(3):
            if (a, b) == (1, 1):
                continue
            r0, r1 = max(0, 1 - a), min(R, R + 1 - a)
            c0, c1 = max(0, 1 - b), min(C, C + 1 - b)
            e.drain()
            o = o3[:, r0:r1, c0:c1]
            ins = e.scalar_tensor_tensor(out=o, in0=x3[:, r0 + a - 1:r1 + a - 1, c0 + b - 1:c1 + b - 1],
                                         scalar=w(a, b), in1=o, op0=ALU.mult, op1=ALU.add)
    return ins


def spatial_gate(nc, name, u, v, ws_t, bs, gv, out, eps):
    NG, NU = 4, 4 * CHUNKS
    with Stage(nc, name) as st:
        sq = st.sb("sq", [P, P])
        ss, rstd = st.sb("ss", [P, NU]), st.sb("rstd", [P, NU])
        banks = [[st.pb(f"z{i}_{j}") for j in range(2)] for i in range(2)]
        squared, normed, mixed, taken = (st.sem(n) for n in ("squared", "normed", "mixed", "taken"))
        block = st.cs.enter_context(nc.Block())

        @block.scalar
        def _(act):
            for n in range(NU):
                ch, g = n // NG, n % NG
                act.activation(sq[:], v[:, ch, g * P:(g + 1) * P], ACT.Square, accum_out=ss[:, n:n + 1])
                act.drain()
            act.activation(rstd[:], ss[:], ACT.Sqrt, bias=eps, scale=1.0 / P).then_inc(squared, 1)

        @block.vector
        def _(dve):
            dve.wait_ge(squared, 1)
            dve.reciprocal(rstd[:], rstd[:])
            dve.drain()
            for n in range(NU):
                ch, g = n // NG, n % NG
                vs = v[:, ch, g * P:(g + 1) * P]
                ins = dve.scalar_tensor_tensor(out=vs, in0=vs, scalar=rstd[:, n:n + 1], in1=gv[:, g * P:(g + 1) * P],
                                               op0=ALU.mult, op1=ALU.mult)
            ins.then_inc(normed, 1)
            for g in range(NG):
                dve.wait_ge(mixed, g + 1)
                for j, (c0, c1) in enumerate(((0, 4), (4, CHUNKS))):
                    o = out[:, g, c0 * P:c1 * P].rearrange("p (c q) -> p c q", q=P)
                    bank = banks[g % 2][j][:, 0:(c1 - c0) * P].rearrange("p (c q) -> p c q", q=P)
                    dve.tensor_tensor(o, bank, middle(bs[:, g * P:(g + 1) * P], c1 - c0), ALU.add)
                    dve.drain()
                    ins = dve.tensor_tensor(out[:, g, c0 * P:c1 * P], out[:, g, c0 * P:c1 * P], u[:, g, c0 * P:c1 * P], ALU.mult)
                ins.then_inc(taken, 1)

        @block.tensor
        def _(pe):
            pe.wait_ge(normed, 1)
            for g in range(NG):
                if g >= 2:
                    pe.wait_ge(taken, g - 1)
                for ch in range(CHUNKS):
                    mm = pe.matmul(banks[g % 2][ch // 4][:, (ch % 4) * P:(ch % 4 + 1) * P], v[:, ch, g * P:(g + 1) * P],
                                   ws_t[:, g, :], start=True, stop=True)
                mm.then_inc(mixed, 1)


DECAY_RATE = 0.6065306597126334


def rwkv_keys(nc, name, k, v, kk, vtok, b_kk, ident, blk):
    NT = 4 * CHUNKS
    with Stage(nc, name) as st:
        sq = st.sb("sq", [P, 2, ALLTOK])
        length = st.sb("length", [P, 2 * NT])
        sums = st.pb("sums")
        spread = [[st.pb(f"spread{i}_{j}") for j in range(2)] for i in range(2)]
        turns = [st.pb(f"turn{i}") for i in range(2)]
        weighed, squared, summed, clipped, rooted, inverted, spreaded, scaled, turned, copied = (
            st.sem(n) for n in ("weighed", "squared", "summed", "clipped", "rooted", "inverted", "spread", "scaled",
                                "turned", "copied"))
        block = st.cs.enter_context(nc.Block())
        columns = lambda t, ch: slice(2 * (t * CHUNKS + ch), 2 * (t * CHUNKS + ch) + 2)

        @block.vector
        def _(dve):
            for t in range(4):
                dve.tensor_scalar(kk[:, t, :], k[:, t, :], b_kk[:, t:t + 1], None, ALU.mult).then_inc(weighed, 1)
            dve.wait_ge(summed, 4)
            dve.tensor_scalar(length[:], sums[:, 0:2 * NT], 1e-12, None, ALU.max).then_inc(clipped, 1)
            dve.wait_ge(rooted, 1)
            dve.reciprocal(length[:], length[:]).then_inc(inverted, 1)
            for t in range(4):
                dve.wait_ge(spreaded, t + 1)
                for j, (c0, c1) in enumerate(((0, 4), (4, CHUNKS))):
                    o = kk[:, t, c0 * P:c1 * P]
                    ins = dve.tensor_tensor(o, o, spread[t % 2][j][:, 0:(c1 - c0) * P], ALU.mult)
                ins.then_inc(scaled, 1)

        @block.tensor
        def _(pe):
            for ch in range(CHUNKS):
                if ch >= 2:
                    pe.wait_ge(copied, ch - 1)
                for t in range(4):
                    mm = pe.transpose(turns[ch % 2][:, t * P:(t + 1) * P], v[:, t, ch * P:(ch + 1) * P], ident[:])
                mm.then_inc(turned, 1)
            for t in range(4):
                pe.wait_ge(squared, t + 1)
                for ch in range(CHUNKS):
                    mm = pe.matmul(sums[:, columns(t, ch)], sq[:, t % 2, ch * P:(ch + 1) * P], blk[:, ::64], start=True, stop=True)
                mm.then_inc(summed, 1)
            pe.wait_ge(inverted, 1)
            for t in range(4):
                if t >= 2:
                    pe.wait_ge(scaled, t - 1)
                for ch in range(CHUNKS):
                    for p in range(2):
                        o = columns(t, ch).start + p
                        mm = pe.matmul(spread[t % 2][ch // 4][64 * p:64 * p + 64, ch % 4 * P:(ch % 4 + 1) * P],
                                       length[:, o:o + 1].to_broadcast([P, 64]), ident[:], start=True, stop=True)
                mm.then_inc(spreaded, 1)

        @block.scalar
        def _(act):
            for ch in range(CHUNKS):
                act.wait_ge(turned, ch + 1)
                act.activation(vtok[:, ch, :], turns[ch % 2][:], ACT.Copy).then_inc(copied, 1)
            for t in range(4):
                act.wait_ge(weighed, t + 1)
                if t >= 2:
                    act.wait_ge(summed, t - 1)
                act.activation(sq[:, t % 2, :], kk[:, t, :], ACT.Square).then_inc(squared, 1)
            act.wait_ge(clipped, 1)
            act.activation(length[:], length[:], ACT.Sqrt).then_inc(rooted, 1)


def rwkv_scan(nc, name, s):
    LEVELS = [2, 4, 8, 16, 32, 64]
    NL = len(LEVELS)
    NU = len(UNITS)
    with Stage(nc, name) as st:
        sig, aa, w0, w1, kd, qq, inv = (st.sb(n, [P, 4, P]) for n in ("sig", "aa", "w0", "w1", "kd", "qq", "inv"))
        pin, bb, bh, kh = sig, aa, aa, kd
        half = st.sb("half", [P, 4, 1])
        carry = st.sb("carry", [P, 4, 1])
        hdecs = [st.sb(f"hdec{i}", [P, 4, 1]) for i in range(2)]
        ars = [st.sb(f"ar{i}", [P, 4, 2, P]) for i in range(2)]
        ktok, btok = st.sb("ktok", [P, 4, P]), st.sb("btok", [P, 4, P])
        kb = st.sb("kb", [P, 8, 4, P])
        X, XT, T = st.sb("X", [P, 8, P]), st.sb("XT", [P, 8, P]), st.sb("T", [P, 8, P])
        rhs, un = (buf[:, 0:4, :].rearrange("p h n -> p (h n)") for buf in (T, X))
        stmp = XT[:, 0:4, :]
        state = st.sb("state", [P, 4, P])
        b = [st.pb(f"b{i}") for i in range(8)]
        names = ("lora", "gated", "centred", "exped", "prepared", "bonus_in", "bonus_out", "turned", "tokens", "scored",
                 "masked", "started", "t_ready", "t_copied", "x_ready", "x_taken", "rhs_ready", "rhs_copied",
                 "u_ready", "u_copied", "y_ready", "y_taken", "s_ready", "s_scaled", "s_taken", "keyed", "pooled", "kd_ready", "xt_unit", "x_first")
        S = {n: st.sem(n) for n in names}
        block = st.cs.enter_context(nc.Block())
        v4 = lambda bank: bank[:].rearrange("p (t n) -> p t n", t=4)

        @block.tensor
        def _(pe):
            def lora(n):
                d, ch = UNITS[n]
                cs, ds = slice(ch * P, (ch + 1) * P), slice(64 * d, 64 * d + 64)
                for t in range(4):
                    pe.matmul(b[7][:, t * P:(t + 1) * P], s.w_up[ds, t * P:(t + 1) * P], s.wd[ds, cs], start=True, stop=True)
                for t in range(4):
                    mm = pe.matmul(b[2][:, t * P:(t + 1) * P], s.a_up[ds, t * P:(t + 1) * P], s.ad[ds, cs], start=True, stop=True)
                mm.then_inc(S["lora"], 1)

            def bonus(n):
                pe.wait_ge(S["bonus_in"], n + 1)
                for t in range(4):
                    mm = pe.matmul(b[2][:, t * P:(t + 1) * P], s.blk_rk[:, t, :], qq[:, t, :], start=True, stop=True)
                mm.then_inc(S["bonus_out"], 1)

            lora(0)
            bonus(0)
            for n, (d, ch) in enumerate(UNITS):
                ar = ars[n % 2]
                pe.wait_ge(S["prepared"], n + 1)
                for t in range(4):
                    if t == 0:
                        pe.wait_ge(S["keyed"], n + 1)
                    if t >= 2:
                        pe.wait_ge(S["masked"], 4 * n + t - 1)
                    for lhs, rhs_ap, bank, o in (
                            (kh, None, 0, 0), (bh, None, 0, 256), (None, bh, 1, t * P)):
                        for p in range(2):
                            ps = slice(64 * p, 64 * p + 64)
                            if bank == 0:
                                out, width = b[((5, 6), (0, 1))[t % 2][p]], 256
                                mm = pe.matmul(out[:, o:o + width], lhs[ps, t, :], ar[ps, t, :, :].rearrange("p a n -> p (a n)"),
                                               start=True, stop=True)
                            else:
                                mm = pe.matmul(b[(7, 2)[p]][:, o:o + P], ar[ps, t, 0, :], bh[ps, t, :], start=True, stop=True)
                    mm.then_inc(S["scored"], 1)
                if n >= 1:
                    pe.wait_ge(S["y_taken"], n)
                    pe.wait_ge(S["s_taken"], n)
                for t in range(4):
                    pe.transpose(b[3][:, t * P:(t + 1) * P], kh[:, t, :], s.ident[:])
                for t in range(4):
                    mm = pe.transpose(b[4][:, t * P:(t + 1) * P], bh[:, t, :], s.ident[:])
                mm.then_inc(S["turned"], 1)
                for l in range(NL):
                    if l == 1 and n + 1 < NU:
                        lora(n + 1)
                    if l == NL - 1 and n + 1 < NU:
                        bonus(n + 1)
                    for g in range(2):
                        u = (n * NL + l) * 2 + g
                        if l == 0 and g == 0:
                            pe.wait_ge(S["tokens"], n + 1)
                            pe.wait_ge(S["masked"], 4 * n + 4)
                        if l == 0:
                            pe.wait_ge(S["started"], 2 * n + g + 1)
                        if l >= 1:
                            pe.wait_ge(S["x_first"], (n * (NL - 1) + l - 1) * 2 + g + 1)
                        for h in range(4 * g, 4 * g + 4):
                            mm = pe.matmul(b[3 + g][:, (h % 4) * P:(h % 4 + 1) * P], kb[:, h, 2, :], X[:, h, :], start=True, stop=True)
                        mm.then_inc(S["t_ready"], 1)
                    for g in range(2):
                        u = (n * NL + l) * 2 + g
                        pe.wait_ge(S["t_copied"], u + 1)
                        if l >= 1:
                            pe.wait_ge(S["x_taken"], u - 1)
                        xb, xtb = ((5, 6), (0, 1))[g]
                        if l < NL - 1:
                            for h in range(4 * g, 4 * g + 4):
                                pe.matmul(b[xb][:, (h % 4) * P:(h % 4 + 1) * P], XT[:, h, :], T[:, h, :], start=True, stop=True)
                        for h in range(4 * g, 4 * g + 4):
                            mm = pe.matmul(b[xtb][:, (h % 4) * P:(h % 4 + 1) * P], T[:, h, :], XT[:, h, :], start=True, stop=True)
                        mm.then_inc(S["x_ready"], 1)
                pe.wait_ge(S["s_scaled"], n + 1)
                if n + 1 < NU:
                    pe.wait_ge(S["gated"], n + 2)
                for t in range(4):
                    pe.matmul(b[7][:, t * P:(t + 1) * P], ar[:, t, 0, :], state[:, t, :], start=True, stop=False, skip_group_check=True)
                    for h in (2 * t, 2 * t + 1):
                        mm = pe.matmul(b[7][:, h * 64:h * 64 + 64], kb[:, h, 0, :], s.vtok[:, ch, h * 64:h * 64 + 64],
                                       start=False, stop=True, skip_group_check=True)
                mm.then_inc(S["rhs_ready"], 1)
                for t in range(4):
                    pe.matmul(b[3][:, t * P:(t + 1) * P], ar[:, t, 1, :], state[:, t, :], start=(t == 0), stop=False, skip_group_check=True)
                    for h in (2 * t, 2 * t + 1):
                        pe.matmul(b[3][:, h * 64:h * 64 + 64], kb[:, h, 1, :], s.vtok[:, ch, h * 64:h * 64 + 64],
                                  start=False, stop=False, skip_group_check=True)
                pe.wait_ge(S["rhs_copied"], n + 1)
                pe.wait_ge(S["x_taken"], 2 * NL * (n + 1))
                if n + 1 < NU:
                    pe.wait_ge(S["keyed"], n + 2)
                for h in range(8):
                    mm = pe.matmul(b[2][:, h * 64:h * 64 + 64], XT[:, h, :], rhs[:, h * 64:h * 64 + 64], start=True, stop=True)
                mm.then_inc(S["u_ready"], 1)
                for t in range(4):
                    ts = slice(t * P, (t + 1) * P)
                    pe.matmul(b[4][:, ts], ktok[:, t, :], s.vtok[:, ch, ts], start=(t == 0), stop=False, skip_group_check=True)
                pe.wait_ge(S["u_copied"], n + 1)
                for t in range(4):
                    ts = slice(t * P, (t + 1) * P)
                    mm = pe.matmul(b[4][:, ts], btok[:, t, :], un[:, ts], start=False, stop=True, skip_group_check=True)
                mm.then_inc(S["s_ready"], 1)
                for h in range(8):
                    hs = slice(h * 64, h * 64 + 64)
                    mm = pe.matmul(b[3][:, hs], kb[:, h, 3, :], un[:, hs], start=False, stop=True, skip_group_check=True)
                mm.then_inc(S["y_ready"], 1)

        @block.scalar
        def _(act):
            def gates(n):
                d = UNITS[n][0]
                act.wait_ge(S["lora"], n + 1)
                if n >= 1:
                    act.wait_ge(S["prepared"], n)
                    act.wait_ge(S["scored"], 4 * n)
                for t in range(4):
                    act.activation(sig[:, t, :], b[7][:, t * P:(t + 1) * P], ACT.Sigmoid, bias=s.b_w0[:, d, t:t + 1])
                for t in range(4):
                    ins = act.activation(aa[:, t, :], b[2][:, t * P:(t + 1) * P], ACT.Sigmoid, bias=s.b_a0[:, d, t:t + 1])
                ins.then_inc(S["gated"], 1)

            def decays(n):
                act.wait_ge(S["centred"], n + 1)
                c = DECAY_RATE
                inc, exc, sgn = ((w0, w1, -c), (w1, w0, c))[UNITS[n][0]]
                act.activation(pin[:], inc[:], ACT.Exp, scale=sgn)
                act.activation(exc[:], exc[:], ACT.Exp, scale=sgn)
                act.activation(inv[:], inc[:], ACT.Exp, scale=-sgn)
                act.activation(hdecs[n % 2][:], half[:], ACT.Exp, scale=-c).then_inc(S["exped"], 1)

            gates(0)
            decays(0)
            for n, (d, ch) in enumerate(UNITS):
                act.wait_ge(S["s_scaled"], n + 1)
                act.activation(XT[:], middle(s.ident[:], 8), ACT.Copy).then_inc(S["xt_unit"], 1)
                act.wait_ge(S["turned"], n + 1)
                act.activation(ktok[:], v4(b[3]), ACT.Copy)
                act.activation(btok[:], v4(b[4]), ACT.Copy, scale=-1.0).then_inc(S["tokens"], 1)
                for l in range(NL):
                    for g in range(2):
                        u = (n * NL + l) * 2 + g
                        act.wait_ge(S["t_ready"], u + 1)
                        act.activation(T[:, 4 * g:4 * g + 4, :], v4(b[3 + g]), ACT.Copy).then_inc(S["t_copied"], 1)
                    if l == 1 and n + 1 < NU:
                        gates(n + 1)
                    if l == 3 and n + 1 < NU:
                        decays(n + 1)
                act.wait_ge(S["rhs_ready"], n + 1)
                act.activation(rhs, b[7][:], ACT.Copy).then_inc(S["rhs_copied"], 1)
                act.wait_ge(S["u_ready"], n + 1)
                act.activation(un, b[2][:], ACT.Copy).then_inc(S["u_copied"], 1)

        @block.gpsimd
        def _(pool):
            for n, (d, ch) in enumerate(UNITS):
                cs = slice(ch * P, (ch + 1) * P)
                pool.wait_ge(S["gated"], n + 1)
                if n >= 1:
                    pool.wait_ge(S["prepared"], n)
                pool.wait_ge(S["kd_ready"], n + 1)
                pool.tensor_tensor(bb[:], aa[:], s.kk[:, :, cs], ALU.mult)
                pool.tensor_tensor(kd[:], kd[:], s.k[:, :, cs], ALU.mult).then_inc(S["pooled"], 1)
                pool.wait_ge(S["pooled"], n + 1)
                if n >= 1:
                    pool.wait_ge(S["bonus_out"], n)
                pool.tensor_tensor(qq[:], kd[:], s.r[:, :, cs], ALU.mult).then_inc(S["bonus_in"], 1)

        @block.vector
        def _(dve):
            def gates(n):
                dve.wait_ge(S["gated"], n + 1)
                for t in range(4):
                    ins = dve.tensor_scalar(kd[:, t, :], aa[:, t, :], s.b_ka[:, t:t + 1], s.one_ka[:, t:t + 1], ALU.mult, ALU.add)
                ins.then_inc(S["kd_ready"], 1)
                for t in range(4):
                    dve.tensor_tensor_scan(w0[:, t, :], s.one[:], sig[:, t, :], 0.0, ALU.mult, ALU.add)

            def centre(n):
                dve.drain()
                dve.tensor_scalar(half[:], w0[:, :, P - 1:P], 0.5, None, ALU.mult)
                dve.drain()
                dve.tensor_tensor(w0[:], w0[:], last(half[:, :, 0], P), ALU.subtract)
                dve.drain()
                dve.tensor_tensor(w1[:], w0[:], sig[:], ALU.subtract).then_inc(S["centred"], 1)

            def operands(n):
                d, ch = UNITS[n]
                cs, ar = slice(ch * P, (ch + 1) * P), ars[n % 2]
                dve.wait_ge(S["exped"], n + 1)
                dve.wait_ge(S["bonus_in"], n + 1)
                pex = (w1, w0)[d]
                dve.tensor_tensor(ar[:, :, 0, :], s.kk[:, :, cs], pex[:], ALU.mult)
                dve.tensor_tensor(ar[:, :, 1, :], s.r[:, :, cs], pin[:], ALU.mult)
                dve.tensor_tensor(kh[:], kd[:], inv[:], ALU.mult)
                dve.tensor_tensor(bh[:], bb[:], inv[:], ALU.mult).then_inc(S["prepared"], 1)
                if n >= 1:
                    dve.tensor_tensor(carry[:], hdecs[0][:], hdecs[1][:], ALU.mult)

            def keep_bonus(n):
                d, ch = UNITS[n]
                cs = slice(ch * P, (ch + 1) * P)
                dve.wait_ge(S["bonus_out"], n + 1)
                if d == 0:
                    dve.tensor_copy(s.bonus[:, :, cs], v4(b[2])).then_inc(S["keyed"], 1)
                else:
                    dve.tensor_tensor(s.bonus[:, :, cs], s.bonus[:, :, cs], v4(b[2]), ALU.add).then_inc(S["keyed"], 1)

            gates(0)
            centre(0)
            operands(0)
            keep_bonus(0)
            dve.memset(state[:], 0.0).then_inc(S["s_scaled"], 1)
            for n, (d, ch) in enumerate(UNITS):
                strict, X1, M = s.masks[d]
                for t in range(4):
                    dve.wait_ge(S["scored"], 4 * n + t + 1)
                    for p in range(2):
                        ins = dve.tensor_tensor(kb[:, 2 * t + p, :, :].rearrange("p a n -> p (a n)"), b[((5, 6), (0, 1))[t % 2][p]][:],
                                                strict[:], ALU.mult)
                    ins.then_inc(S["masked"], 1)
                    if t == 0:
                        dve.wait_ge(S["xt_unit"], n + 1)
                    dve.drain()
                    hs = slice(2 * t, 2 * t + 2)
                    dve.copy_predicated(XT[:, hs, :], middle(M[1][:, 0, :], 2), kb[:, hs, 2, :])
                for p in range(2):
                    dve.tensor_tensor(X[:, p::2, :], v4(b[(7, 2)[p]]), middle(X1, 4), ALU.mult)
                dve.drain()
                for g in range(2):
                    hg = slice(4 * g, 4 * g + 4)
                    dve.tensor_tensor(X[:, hg, :], X[:, hg, :], middle(s.ident[:], 4), ALU.add).then_inc(S["started"], 1)
                for l in range(NL):
                    for g in range(2):
                        u = (n * NL + l) * 2 + g
                        dve.wait_ge(S["x_ready"], u + 1)
                        xb, xtb = ((5, 6), (0, 1))[g]
                        hg = slice(4 * g, 4 * g + 4)
                        if l < NL - 1:
                            dve.copy_predicated(X[:, hg, :], middle(M[0][:, l + 1, :], 4), v4(b[xb])).then_inc(S["x_first"], 1)
                        dve.copy_predicated(XT[:, hg, :], middle(M[1][:, l + 1, :], 4), v4(b[xtb])).then_inc(S["x_taken"], 1)
                    if n + 1 < NU:
                        if l == 1:
                            gates(n + 1)
                        if l == 2:
                            centre(n + 1)
                        if l == 4:
                            operands(n + 1)
                if n + 1 < NU:
                    keep_bonus(n + 1)
                dve.wait_ge(S["s_ready"], n + 1)
                dve.tensor_tensor(stmp, state[:], v4(b[4]), ALU.add).then_inc(S["s_taken"], 1)
                dve.drain()
                dve.wait_ge(S["y_ready"], n + 1)
                if n + 1 < NU and UNITS[n + 1][1] == ORDER[UNITS[n + 1][0]][0]:
                    dve.memset(state[:], 0.0).then_inc(S["s_scaled"], 1)
                else:
                    for t in range(4):
                        ins = dve.scalar_tensor_tensor(out=state[:, t, :], in0=stmp[:, t, :], scalar=carry[:, t, :], in1=s.blk[:],
                                                       op0=ALU.mult, op1=ALU.mult)
                    ins.then_inc(S["s_scaled"], 1)
                y = s.y[:, ch, :]
                if d == 0:
                    dve.tensor_copy(y, b[3][:]).then_inc(S["y_taken"], 1)
                else:
                    dve.tensor_tensor(y, y, b[3][:], ALU.add).then_inc(S["y_taken"], 1)


LN_EPS = 64e-5


def rwkv_out(nc, name, s, out):
    NH = CHUNKS * 8
    with Stage(nc, name) as st:
        sq = st.sb("sq", [P, CHUNKS * 512])
        mu, var = st.sb("mu", [P, NH]), st.sb("var", [P, NH])
        turned_y = [[st.pb(f"y{i}_{j}") for j in range(2)] for i in range(2)]
        gate = [[st.pb(f"g{i}_{j}") for j in range(2)] for i in range(2)]
        centred, squared, rooted, normed, ready, taken = (
            st.sem(n) for n in ("centred", "squared", "rooted", "normed", "ready", "taken"))
        block = st.cs.enter_context(nc.Block())
        y3 = s.y[:].rearrange("p c (h n) -> p (c h) n", n=64)
        sq3 = sq[:].rearrange("p (h n) -> p h n", n=64)

        @block.vector
        def _(dve):
            dve.tensor_reduce(mu[:], y3, AX.X, ALU.add)
            dve.drain()
            dve.tensor_scalar(mu[:], mu[:], 1.0 / 64, None, ALU.mult)
            dve.drain()
            dve.tensor_tensor(y3, y3, last(mu[:], 64), ALU.subtract).then_inc(centred, 1)
            dve.wait_ge(squared, 1)
            dve.tensor_reduce(var[:], sq3, AX.X, ALU.add).then_inc(rooted, 1)
            dve.wait_ge(squared, 2)
            dve.reciprocal(var[:], var[:])
            dve.drain()
            dve.tensor_tensor(y3, y3, last(var[:], 64), ALU.mult).then_inc(normed, 1)
            for t in range(4):
                for j, (t0, tw) in enumerate(SEQS):
                    n = 2 * t + j
                    o, v, bo = (z[:, t, t0:t0 + tw] for z in (out, s.v, s.bonus))
                    dve.tensor_tensor(v, v, bo, ALU.mult)
                    dve.wait_ge(ready, n + 1)
                    dve.drain()
                    dve.scalar_tensor_tensor(out=o, in0=turned_y[t % 2][j][:, 0:tw], scalar=s.ln_g[:, t:t + 1], in1=v,
                                             op0=ALU.mult, op1=ALU.add)
                    dve.drain()
                    dve.scalar_tensor_tensor(out=o, in0=o, scalar=s.ln_b[:, t:t + 1], in1=gate[t % 2][j][:, 0:tw],
                                             op0=ALU.add, op1=ALU.mult).then_inc(taken, 1)

        @block.scalar
        def _(act):
            act.wait_ge(centred, 1)
            act.activation(sq[:], s.y[:].rearrange("p c n -> p (c n)"), ACT.Square).then_inc(squared, 1)
            act.wait_ge(rooted, 1)
            act.activation(var[:], var[:], ACT.Sqrt, bias=s.ln_eps, scale=1.0 / 64).then_inc(squared, 1)

        @block.tensor
        def _(pe):
            pe.wait_ge(normed, 1)
            for t in range(4):
                for j, (t0, tw) in enumerate(SEQS):
                    n = 2 * t + j
                    if n >= 4:
                        pe.wait_ge(taken, n - 3)
                    for i in range(tw // P):
                        ch = t0 // P + i
                        pe.transpose(turned_y[t % 2][j][:, i * P:(i + 1) * P], s.y[:, ch, t * P:(t + 1) * P], s.ident[:])
                    pe.matmul(gate[t % 2][j][:, 0:tw], s.g_up[:, t * P:(t + 1) * P], s.gd[:, t0:t0 + tw],
                              start=True, stop=True).then_inc(ready, 1)


class Parts:
    pass


def ffn2(nc, name, a, c, L, x, seqs, w_up, w_down):
    t_min, t_max = seqs[0][0], seqs[-1][0] + seqs[-1][1]
    T = t_max - t_min
    split = T <= SEQ
    with Stage(nc, name) as st:
        hidden = Split(st, "hidden", [P, 22, T]) if split else st.sb("hidden", [P, 22, T])
        with Stage(nc, name + "_in") as s2:
            h = Split(s2, "h", [P, KT, T])
            cw, cb = s2.sb("cw", [P, 22, 9]), s2.sb("cb", [P, 22, 1])
            load(nc, name + "load", [(cw[:], a[f"ffn_conv{L.i}"]), (cb[:], a[f"ffn_conv_b{L.i}"])])
            ring = Ring(s2, "weights", w_up, 2, 4)
            pre_norm(nc, name, c, L, 3, x, h, seqs, ahead=ring)

            def conv(e, m, b, banks, t):
                for j, (t0, tw) in enumerate(seqs):
                    acc = t[0][:, t0 - t_min:t0 - t_min + tw]
                    if tw == SEQ:
                        ins = conv_grid(e, acc, banks[0][j][:, 0:tw], lambda p, q: cw[:, m, 3 * p + q:3 * p + q + 1])
                    else:
                        ins = conv3(e, acc, banks[0][j][:, 0:tw], lambda q: cw[:, m, 3 + q:4 + q], tw)
                return ins

            def gelu(e, m, b, banks, t):
                return e.activation(t[1][:], t[0][:], ACT.Gelu_apprx_tanh, bias=cb[:, m, :])

            def mult(e, m, b, banks, t):
                for j, (t0, tw) in enumerate(seqs):
                    o = slice(t0 - t_min, t0 - t_min + tw)
                    ins = e.tensor_tensor(t[1][:, o] if split else hidden[:, m, o], t[1][:, o], banks[1][j][:, 0:tw], ALU.mult)
                return ins

            steps = [("vector", conv), ("scalar", gelu), ("vector", mult)]
            if split:
                steps += [("scalar", lambda e, m, b, banks, t: e.activation(hidden.hi[:, m, :], t[1][:], ACT.Copy)),
                          ("gpsimd", lambda e, m, b, banks, t: e.tensor_tensor(
                              hidden.lo[:, m, :], t[1][:], hidden.hi[:, m, :].bitcast(F32), ALU.subtract))]
            project(nc, name + "up", w_up, [h.tiles(KT)] * 2, [(t0 - t_min, tw) for t0, tw in seqs], steps,
                    unroll=2, bank_step=2, ring=ring, temps=lambda s, n: [[s.sb(f"t{i}_{j}", [P, T]) for j in range(2)] for i in range(n)])
        y, sums = st.sb("y", [P, KT, T]), st.sb("sums", [P, T])
        down(nc, name + "down", w_down, hidden.tiles(22) if split else [hidden[:, k, :] for k in range(22)], y, sums,
             seqs, t_min, per_piece=11, split=split)
        post_norm(nc, name + "p", c, L, 5, x, y, sums, seqs, t_min)


def down(nc, name, w, src, y, sums, seqs, t_min, **kw):
    def keep(e, m, b, banks, t):
        for j, (t0, tw) in enumerate(seqs):
            ins = e.tensor_copy(y[:, m, t0 - t_min:t0 - t_min + tw], banks[0][j][:, 0:tw])
        e.drain()
        return ins
    with Stage(nc, name + "clear") as st:
        block = st.cs.enter_context(nc.Block())

        @block.vector
        def _(dve):
            dve.memset(sums[:], 0.0)
    project(nc, name, w, [src], [(t0 - t_min, tw) for t0, tw in seqs],
            [("vector", keep)] + square_steps(lambda m: y[:, m, :], sums[:], lambda t: t[:]), unroll=2,
            temps=lambda s, n: [s.sb(f"square{i}", [P, y.shape[-1]]) for i in range(n)], **kw)


def pre_norm(nc, name, c, L, i, x, h, seqs, ahead=None):
    t_min = seqs[0][0]
    for t0, tw in seqs:
        s = 0 if t0 == 0 else 1
        mod = lambda j: lambda k: L.mods[:, (i + j) * KT + k, s:s + 1]
        o = slice(t0 - t_min, t0 - t_min + tw)
        rms_norm(nc, f"{name}pre{s}", KT, tw, lambda k: x[:, k, t0:t0 + tw], lambda k: (h.hi[:, k, o], h.lo[:, k, o]),
                 c, c.sums[:, t0:t0 + tw], gain=mod(1), shift=mod(0), ahead=ahead if t0 == t_min else None)


def post_norm(nc, name, c, L, i, x, y, sums, seqs, t_min):
    for t0, tw in seqs:
        s = 0 if t0 == 0 else 1
        o = slice(t0 - t_min, t0 - t_min + tw)
        rms_norm(nc, f"{name}post{s}", KT, tw, lambda k: y[:, k, o], None, c, sums[:, o],
                 gain=lambda k: L.mods[:, i * KT + k, s:s + 1], residual=lambda k: x[:, k, t0:t0 + tw],
                 next_sums=c.sums[:, t0:t0 + tw], clear=False)


def mixer_ab(nc, a, c, L, x, tap):
    with Stage(nc, "ab") as st:
        cat = st.sb("cat", [P, 8, ALLTOK])
        with Stage(nc, "ab2") as s1:
            s = Parts()
            rkv = s1.sb("rkv", [P, 12, ALLTOK])
            s.r, s.k, s.v = rkv[:, 0:4, :], rkv[:, 4:8, :], rkv[:, 8:12, :]
            s.bonus = cat[:, 4:8, :]
            lora = s1.sb("lora", [P, 3, ALLTOK])
            s.wd, s.ad, s.gd = lora[:, 0, :], lora[:, 1, :], lora[:, 2, :]
            with Stage(nc, "ab3") as s2:
                h = Split(s2, "h", [P, KT, ALLTOK])
                pre_norm(nc, "ab", c, L, 0, x, h, SEQS)
                u = s2.sb("u", [P, 4, ALLTOK])
                vg = s2.sb("vg", [P, CHUNKS, 512])
                shift = s2.sb("shift", [P, 12, 3])
                ws, bs, gv = s2.sb("ws", [P, 4, P]), s2.sb("bs", [P, 512]), s2.sb("gv", [P, 512])
                load(nc, "abload", [(shift[:], a["b_shift"]), (ws[:], a["a_ws"]), (bs[:], broadcast_rows(a["a_bs"], 512)),
                                    (gv[:], broadcast_rows(a["a_gv"], 512))])

                def each(f):
                    def g(e, m, b, banks, t):
                        for j, (t0, tw) in enumerate(SEQS):
                            ins = f(e, m, b, banks[0][j][:, 0:tw], t0, tw)
                        return ins
                    return g

                project(nc, "abu", a["w_ab_u"], [h.tiles(KT)], SEQS, [("scalar", each(
                    lambda e, m, b, bank, t0, tw: e.activation(u[:, m, t0:t0 + tw], bank, ACT.Gelu_apprx_tanh)))], unroll=4, raw_slots=2)
                project(nc, "abrkv", a["w_ab_rkv"], [h.tiles(KT)], SEQS, [("vector", each(
                    lambda e, m, b, bank, t0, tw: conv3(e, rkv[:, m, t0:t0 + tw], bank, lambda j: shift[:, m, j:j + 1], tw)))],
                    unroll=4, raw_slots=2)
                project(nc, "ablora", a["w_ab_lora"], [h.tiles(KT)], SEQS, [("scalar", each(
                    lambda e, m, b, bank, t0, tw: e.activation(lora[:, b, t0:t0 + tw], bank, (ACT.Tanh, ACT.Copy, ACT.Sigmoid)[b])))],
                    unroll=3, raw_slots=3)
                token_major(nc, "abv", a["w_ab_v"], h.tiles(KT), [slice(i * P, (i + 1) * P) for i in range(CHUNKS)],
                            lambda e, n, r, bank: e.activation(vg[:, r, :], bank, ACT.Gelu_apprx_tanh), unroll=1, per_piece=2, raw_slots=2)
                spatial_gate(nc, "gate", u, vg, ws, bs, gv, cat, c.eps)
            tap("rkv", rkv)
            tap("lora", lora)
            with Stage(nc, "rw") as s2:
                pairs = []

                def const(name, shape, dt=F32):
                    buf = s2.sb("c_" + name, shape, dt)
                    pairs.append((buf[:], a[name]))
                    return buf

                s.y = s2.sb("y", [P, CHUNKS, 512])
                s.kk = s2.sb("kk", [P, 4, ALLTOK])
                s.vtok = s2.sb("vtok", [P, CHUNKS, 512])
                s.ident, s.one = c.ident, c.one
                s.blk = const("blk64", [P, P])
                s.w_up, s.a_up = const("b_w_up", [P, 512]), const("b_a_up", [P, 512])
                s.b_w0, s.b_a0 = const("b_w0", [P, 2, 4]), const("b_a0", [P, 2, 4])
                s.b_ka, kkw, rk = const("b_ka", [P, 4]), const("b_kk", [P, 4]), const("b_rk", [P, 4])
                s.ln_g, s.ln_b = const("b_ln_g", [P, 4]), const("b_ln_b", [P, 4])
                lneps = const("ln_eps", [P, 1])
                s.ln_eps = lneps[:, 0:1]
                strict, x1 = const("strict", [P, 2, 4 * P]), const("x1", [P, 2, P])
                lev = s2.sb("lev", [P, 2, 7, P], mybir.dt.uint8)
                s.masks = [(strict[:, d], x1[:, d], (lev[:, d], lev[:, 1 - d])) for d in range(2)]
                s.one_ka = s2.sb("one_ka", [P, 4])
                s.blk_rk = s2.sb("blk_rk", [P, 4, P])
                load(nc, "rwload", pairs)
                with Stage(nc, "rwprep") as s3:
                    levels, loaded = s3.sb("levels", [P, 2, 7, P]), s3.sem("loaded")
                    block = s3.cs.enter_context(nc.Block())

                    @block.sync
                    def _(sp):
                        sp.dma_start(levels[:], a["levels"]).then_inc(loaded, 16)

                    @block.vector
                    def _(dve):
                        dve.tensor_scalar(s.one_ka[:], s.b_ka[:], -1.0, 1.0, ALU.mult, ALU.add)
                        dve.tensor_tensor(s.blk_rk[:], middle(s.blk[:], 4), last(rk[:], P), ALU.mult)
                        dve.wait_ge(loaded, 16)
                        dve.tensor_copy(lev[:], levels[:])
                rwkv_keys(nc, "keys", s.k, s.v, s.kk, s.vtok, kkw, c.ident, s.blk)
                tap("kk", s.kk)
                tap("vtok", s.vtok)
                rwkv_scan(nc, "rwkv", s)
                tap("yrw", s.y)
                s.g_up = s2.sb("g_up", [P, 512])
                load(nc, "gload", [(s.g_up[:], a["b_g_up"])])
                rwkv_out(nc, "rwout", s, cat[:, 4:8, :])
        tap("cat", cat)
        y, sums = st.sb("y", [P, KT, ALLTOK]), st.sb("sums", [P, ALLTOK])
        cat_parts = Split(st, "cat", [P, 8, ALLTOK])
        split_up(nc, "cat_parts", cat, cat_parts, 8)
        down(nc, "about", a["w_ab_out"], cat_parts.tiles(8), y, sums, SEQS, 0)
        tap("yab", y)
        post_norm(nc, "abp", c, L, 2, x, y, sums, SEQS, 0)


def second_block(nc, a, c, x, tap):
    with Stage(nc, "mods") as st:
        layers = []
        mods, bias = st.sb("mods", [P, 2 * MOD * KT, 2]), st.sb("bias", [P, 2 * MOD * KT, 2])
        for i in range(2):
            L = Parts()
            L.i = i
            L.mods = mods[:, i * MOD * KT:(i + 1) * MOD * KT, :]
            L.mix_pre, L.mix_post, L.ffn_pre, L.ffn_post = (st.sb(f"{n}{i}", [P, KT]) for n in ("mix_pre", "mix_post", "ffn_pre", "ffn_post"))
            layers.append(L)
        cvec = st.sb("cvec", [P, KT, 2])
        load(nc, "modload", [(cvec[:], a["cvec"]), (bias[:], a["ada_b"])] + [(b[:], a[f"{n}{L.i}"]) for L in layers for b, n in (
            (L.mix_pre, "norm_mix_pre"), (L.mix_post, "norm_mix_post"),
            (L.ffn_pre, "norm_ffn_pre"), (L.ffn_post, "norm_ffn_post"))])
        silu_columns(nc, "silu", cvec[:])
        cvec_parts = Split(st, "cvec", [P, KT, 2])
        split_up(nc, "cvec_parts", cvec, cvec_parts, KT)
        modulations(nc, "mod", a["w_ada"], bias, cvec_parts, c.ident, mods)
        modulation_gains(nc, "gains", layers)
        mixer_ab(nc, a, c, layers[0], x, tap)
        tap("x_ab", x)
        ffn2(nc, "f0", a, c, layers[0], x, SEQS, a["w_ffn_up0"], a["w_ffn_down0"])
        tap("x_l0", x)
        mixer_mlstm(nc, a, c, layers[1], x, tap)
        tap("x_ml", x)
        ffn2(nc, "f1", a, c, layers[1], x, SEQS[1:], a["w_ffn_up1"], a["w_ffn_down1"])
        tap("x_l1", x)


MH, MD = 4, 256


def expand_blocks(nc, name, compact, mask, out):
    with Stage(nc, name) as st:
        block = st.cs.enter_context(nc.Block())

        @block.vector
        def _(dve):
            for t in range(KT):
                dve.tensor_tensor(out[:, t, :].rearrange("p (g o) -> p g o", o=4), middle(compact[:, t, :], P // 4),
                                  mask[:].rearrange("p (g o) -> p g o", o=4), ALU.mult)


def mlstm_heads(nc, name, xm, xcv, wq, wk, wv, q, k, ktok, vtok):
    with Stage(nc, name) as st:
        banks = [st.pb(f"bank{i}") for i in range(8)]
        made, taken_a, taken_v = st.sem("made"), st.sem("taken_a"), st.sem("taken_v")
        block = st.cs.enter_context(nc.Block())
        scale = MD ** -0.5
        jobs = [(w, t) for t in range(KT) for w in ("q", "k")]
        jobs += [(w, ch, half) for w in ("vt", "kt") for ch in range(CHUNKS) for half in range(2)]

        @block.tensor
        def _(pe):
            for n, job in enumerate(jobs):
                if n >= 8:
                    pe.wait_ge((taken_a, taken_v)[n % 2], (n - 8) // 2 + 1)
                bank = banks[n % 8]
                if job[0] in ("q", "k"):
                    mm = pe.matmul(bank[:], (wq if job[0] == "q" else wk)[:, job[1], :], xcv[:, job[1], CTX:ALLTOK], start=True, stop=True)
                else:
                    w, ch, half = job
                    for i in range(4):
                        t = 4 * half + i
                        mm = pe.matmul(bank[:, i * P:(i + 1) * P], (xcv if w == "kt" else xm)[:, t, ch * P:(ch + 1) * P],
                                       (wk if w == "kt" else wv)[:, t, :], start=True, stop=True)
                mm.then_inc(made, 1)

        def place(job):
            if job[0] in ("q", "k"):
                return (q if job[0] == "q" else k)[:, job[1], :], 1.0 if job[0] == "q" else scale
            if job[0] == "kt":
                return ktok[:, job[1], job[2] * 512:job[2] * 512 + 512].rearrange("p (h n) -> p h n", h=2), scale
            return vtok[:, job[1], 2 * job[2]:2 * job[2] + 2, 0:MD], 1.0

        def source(n):
            return banks[n % 8][:] if jobs[n][0] in ("q", "k") else banks[n % 8][:].rearrange("p (h n) -> p h n", h=2)

        @block.scalar
        def _(act):
            for n in range(0, len(jobs), 2):
                act.wait_ge(made, n + 1)
                dst, factor = place(jobs[n])
                act.activation(dst, source(n), ACT.Copy, scale=factor).then_inc(taken_a, 1)

        @block.vector
        def _(dve):
            dve.memset(vtok[:, :, :, MD:MD + 1], 1.0)
            for n in range(1, len(jobs), 2):
                dve.wait_ge(made, n + 1)
                dst, factor = place(jobs[n])
                dve.tensor_scalar(dst, source(n), factor, None, ALU.mult).then_inc(taken_v, 1)


def mlstm_gates(nc, name, raw, bias, tri, m, one):
    G = 2 * MH
    with Stage(nc, name) as st:
        x, ab, lf = st.sb("x", [P, CHUNKS, 2, G]), st.sb("ab", [P, CHUNKS, G]), st.sb("lf", [P, CHUNKS, G])
        ps = [st.pb(f"ps{i}") for i in range(2)]
        added, logged, forgot, summed = (st.sem(n) for n in ("added", "logged", "forgot", "summed"))
        block = st.cs.enter_context(nc.Block())
        W = CHUNKS * MH

        @block.vector
        def _(dve):
            dve.tensor_tensor(x[:].rearrange("p c a g -> p c (a g)"), raw[:], middle(bias[:], CHUNKS), ALU.add).then_inc(added, 1)
            dve.wait_ge(logged, 1)
            dve.scalar_tensor_tensor(out=lf[:], in0=x[:, :, 1, :], scalar=0.0, in1=ab[:], op0=ALU.min, op1=ALU.subtract).then_inc(forgot, 1)
            dve.wait_ge(summed, 1)
            for d in range(2):
                dve.tensor_copy(m.b[:, :, d, :], ps[d][:, 0:W].rearrange("p (c h) -> p c h", h=MH))
            dve.drain()
            dve.tensor_tensor(m.cc[:].rearrange("p c d h -> p c (d h)"), x[:, :, 0, :], m.b[:].rearrange("p c d h -> p c (d h)"), ALU.subtract)

        @block.scalar
        def _(act):
            act.wait_ge(added, 1)
            act.activation(ab[:], x[:, :, 1, :], ACT.Abs)
            act.drain()
            act.activation(ab[:], ab[:], ACT.Exp, scale=-1.0)
            act.drain()
            act.activation(ab[:], ab[:], ACT.Ln, bias=one[:, 0:1]).then_inc(logged, 1)

        @block.tensor
        def _(pe):
            pe.wait_ge(forgot, 1)
            for d in range(2):
                mm = pe.matmul(ps[d][:, 0:W], tri[d][:], lf[:, :, d * MH:(d + 1) * MH], start=True, stop=True)
            mm.then_inc(summed, 1)


def mlstm_scan(nc, name, m, q, k, ktok, vtok, hsum, ident, neg, edge):
    NU = len(UNITS)
    V = MD + 1
    with Stage(nc, name) as st:
        mm_b = st.sb("mm_b", [P, 2 * MH])
        nmm, rmax, mprev, den = (st.sb(n, [P, MH]) for n in ("nmm", "rmax", "mprev", "den"))
        win, floor, kco, carry = (st.sb(n, [P, 2, MH]) for n in ("win", "floor", "kco", "carry"))
        args = st.sb("args", [P, 4, MH])
        edge_sb = st.sb("edge_sb", [P, 2 * MH])
        E, Sm, St = (st.sb(n, [P, MH, P]) for n in ("E", "Sm", "St"))
        num = st.sb("num", [P, MH, V])
        kw = st.sb("kw", [P, MH * MD])
        state = st.sb("state", [P, 2 * MH, V])
        cbank, sbank, ebank, tbank = (st.pb(n) for n in ("cbank", "sbank", "ebank", "tbank"))
        work = [st.pb(f"work{i}") for i in range(4)]
        names = ("spread", "maxed", "picked", "argued", "exped", "weighed", "scored", "masked", "turned", "copied",
                 "outer", "scaled", "summed", "updated", "taken", "keyed", "kept")
        S = {n: st.sem(n) for n in names}
        block = st.cs.enter_context(nc.Block())
        before = lambda n: sum(1 for d, ch in UNITS[:n] if ch >= CTXCH)

        latent = lambda n: UNITS[n][1] >= CTXCH

        @block.tensor
        def _(pe):
            def spread(n):
                d, ch = UNITS[n]
                if n >= 1:
                    pe.wait_ge(S["exped"], n)
                for h in range(MH):
                    bank = cbank[:, h * P:(h + 1) * P]
                    pe.matmul(bank, m.cc[:, ch, d, h:h + 1].to_broadcast([P, P]), ident[:], start=True, stop=False)
                    mm = pe.matmul(bank, ident[:], neg[d][:], start=False, stop=True)
                mm.then_inc(S["spread"], 1)

            def pick(n):
                pe.wait_ge(S["maxed"], n + 1)
                if n >= 1:
                    pe.wait_ge(S["argued"], n)
                pe.matmul(ebank[:, 0:2 * MH], edge[UNITS[n][0]][:], mm_b[:], start=True, stop=True).then_inc(S["picked"], 1)

            def scores(n):
                i, ch = before(n), UNITS[n][1]
                js = slice((ch - CTXCH) * P, (ch - CTXCH + 1) * P)
                if i >= 1:
                    pe.wait_ge(S["masked"], i)
                for h in range(MH):
                    for kt in range(2):
                        mm = pe.matmul(sbank[:, h * P:(h + 1) * P], q[:, 2 * h + kt, js], k[:, 2 * h + kt, js],
                                       start=(kt == 0), stop=(kt == 1))
                mm.then_inc(S["scored"], 1)

            def turn(n):
                i = before(n)
                pe.wait_ge(S["masked"], i + 1)
                if i >= 1:
                    pe.wait_ge(S["copied"], i)
                for h in range(MH):
                    mm = pe.transpose(tbank[:, h * P:(h + 1) * P], Sm[:, h, :], ident[:])
                mm.then_inc(S["turned"], 1)

            def outputs(n):
                i, ch = before(n), UNITS[n][1]
                js = slice((ch - CTXCH) * P, (ch - CTXCH + 1) * P)
                pe.wait_ge(S["copied"], i + 1)
                pe.wait_ge(S["taken"], n * 2 * MH)
                for h in range(MH):
                    inner, outer = work[2 * (h % 2)], work[2 * (h % 2) + 1]
                    if h >= 2:
                        pe.wait_ge(S["summed"], i * MH + h - 1)
                    pe.matmul(inner[:, 0:V], St[:, h, :], vtok[:, ch, h, :], start=True, stop=True)
                    for kt in range(2):
                        mm = pe.matmul(outer[:, 0:V], q[:, 2 * h + kt, js], state[:, 2 * h + kt, :], start=(kt == 0), stop=(kt == 1))
                    mm.then_inc(S["outer"], 1)

            def updates(n):
                ch = UNITS[n][1]
                pe.wait_ge(S["keyed"], n + 1)
                if latent(n):
                    pe.wait_ge(S["summed"], (before(n) + 1) * MH)
                for u in range(2 * MH):
                    if n * 2 * MH + u >= 4:
                        pe.wait_ge(S["taken"], n * 2 * MH + u - 3)
                    pe.matmul(work[u % 4][:, 0:V], kw[:, u * P:(u + 1) * P], vtok[:, ch, u // 2, :], start=True, stop=True).then_inc(S["updated"], 1)

            spread(0)
            pick(0)
            for n in range(NU):
                more = n + 1 < NU
                if more:
                    spread(n + 1)
                if latent(n):
                    outputs(n)
                if more:
                    pick(n + 1)
                if more and latent(n + 1):
                    scores(n + 1)
                updates(n)
                if more and latent(n + 1):
                    turn(n + 1)

        @block.scalar
        def _(act):
            def weights(n):
                i = before(n)
                act.wait_ge(S["maxed"], n + 1)
                if n >= 2:
                    act.wait_ge(S["kept"], n - 1)
                if latent(n):
                    if i >= 1:
                        act.wait_ge(S["masked"], i)
                    for h in range(MH):
                        act.activation(E[:, h, :], cbank[:, h * P:(h + 1) * P], ACT.Exp, bias=nmm[:, h:h + 1])
                act.activation(win[:, n % 2, :], args[:, 0, :], ACT.Exp)
                act.activation(floor[:, n % 2, :], args[:, 1, :], ACT.Exp).then_inc(S["exped"], 1)

            def factors(n):
                act.wait_ge(S["argued"], n + 1)
                act.activation(kco[:, n % 2, :], args[:, 2, :], ACT.Exp)
                act.activation(carry[:, n % 2, :], args[:, 3, :], ACT.Exp).then_inc(S["weighed"], 1)

            def copy(n):
                act.wait_ge(S["turned"], before(n) + 1)
                act.activation(St[:], tbank[:].rearrange("p (h n) -> p h n", h=MH), ACT.Copy).then_inc(S["copied"], 1)

            def scale(n):
                act.wait_ge(S["kept"], n)
                for h in range(MH):
                    act.wait_ge(S["outer"], before(n) * MH + h + 1)
                    act.activation(num[:, h, :], work[2 * (h % 2) + 1][:, 0:V], ACT.Copy, scale=win[:, n % 2, h:h + 1]).then_inc(S["scaled"], 1)

            weights(0)
            factors(0)
            for n in range(NU):
                more = n + 1 < NU
                if more:
                    weights(n + 1)
                if latent(n):
                    scale(n)
                if more:
                    factors(n + 1)
                if more and latent(n + 1):
                    copy(n + 1)

        @block.vector
        def _(dve):
            starts = (0, NU // 2)

            def largest(n):
                d, ch = UNITS[n]
                if n in starts:
                    dve.memset(mprev[:], 0.0)
                    dve.drain()
                dve.wait_ge(S["spread"], n + 1)
                if n >= 1:
                    dve.wait_ge(S["exped"], n)
                dve.tensor_reduce(rmax[:], cbank[:].rearrange("p (h n) -> p h n", h=MH), AX.X, ALU.max)
                dve.tensor_copy(mm_b[:, MH:2 * MH], m.b[:, ch, d, :])
                dve.drain()
                dve.tensor_tensor(mm_b[:, 0:MH], rmax[:], mprev[:], ALU.max)
                dve.drain()
                dve.tensor_scalar(nmm[:], mm_b[:, 0:MH], -1.0, None, ALU.mult)
                dve.tensor_tensor(args[:, 0, :], mprev[:], mm_b[:, 0:MH], ALU.subtract)
                dve.drain()
                dve.tensor_tensor(args[:, 1, :], nmm[:], mm_b[:, MH:2 * MH], ALU.subtract).then_inc(S["maxed"], 1)

            def last_step(n):
                d, ch = UNITS[n]
                dve.wait_ge(S["picked"], n + 1)
                if n >= 1:
                    dve.wait_ge(S["weighed"], n)
                dve.tensor_copy(edge_sb[:], ebank[:, 0:2 * MH])
                dve.drain()
                dve.tensor_tensor(args[:, 2, :], m.cc[:, ch, d, :], edge_sb[:, 0:MH], ALU.subtract)
                dve.tensor_tensor(args[:, 3, :], mprev[:], edge_sb[:, 0:MH], ALU.subtract).then_inc(S["argued"], 1)
                dve.drain()
                dve.tensor_tensor(mprev[:], edge_sb[:, 0:MH], edge_sb[:, MH:2 * MH], ALU.add)
                dve.drain()

            def weigh(n):
                ch, i = UNITS[n][1], before(n)
                dve.wait_ge(S["weighed"], n + 1)
                dve.tensor_tensor(kw[:].rearrange("p (h n) -> p h n", h=MH), ktok[:, ch, :].rearrange("p (h n) -> p h n", h=MH),
                                  last(kco[:, n % 2, :], MD), ALU.mult).then_inc(S["keyed"], 1)
                if latent(n):
                    dve.wait_ge(S["exped"], n + 1)
                    dve.wait_ge(S["scored"], i + 1)
                    if i >= 1:
                        dve.wait_ge(S["turned"], i)
                    dve.tensor_tensor(Sm[:], sbank[:].rearrange("p (h n) -> p h n", h=MH), E[:], ALU.mult).then_inc(S["masked"], 1)

            def numerators(n):
                for h in range(MH):
                    dve.wait_ge(S["scaled"], before(n) * MH + h + 1)
                    dve.tensor_tensor(num[:, h, :], num[:, h, :], work[2 * (h % 2)][:, 0:V], ALU.add).then_inc(S["summed"], 1)

            def update(n):
                for u in range(2 * MH):
                    dve.wait_ge(S["updated"], n * 2 * MH + u + 1)
                    if n + 1 in starts:
                        ins = dve.memset(state[:, u, :], 0.0)
                    else:
                        ins = dve.scalar_tensor_tensor(out=state[:, u, :], in0=state[:, u, :], scalar=carry[:, n % 2, u // 2:u // 2 + 1],
                                                       in1=work[u % 4][:, 0:V], op0=ALU.mult, op1=ALU.add)
                    ins.then_inc(S["taken"], 1)

            def divide(n):
                d, ch = UNITS[n]
                dcol = num[:, :, MD]
                dve.scalar_tensor_tensor(out=den[:], in0=dcol, scalar=-1.0, in1=dcol, op0=ALU.mult, op1=ALU.max)
                dve.drain()
                dve.tensor_tensor(den[:], den[:], floor[:, n % 2, :], ALU.max)
                dve.drain()
                dve.reciprocal(den[:], den[:])
                dve.drain()
                h4 = hsum[:, ch - CTXCH, :].rearrange("p (h n) -> p h n", h=MH)
                if d == 0:
                    dve.tensor_tensor(h4, num[:, :, 0:MD], last(den[:], MD), ALU.mult)
                else:
                    dve.tensor_tensor(num[:, :, 0:MD], num[:, :, 0:MD], last(den[:], MD), ALU.mult)
                    dve.drain()
                    dve.tensor_tensor(h4, h4, num[:, :, 0:MD], ALU.add)

            dve.memset(state[:], 0.0)
            largest(0)
            last_step(0)
            weigh(0)
            for n in range(NU):
                more = n + 1 < NU
                if more:
                    largest(n + 1)
                if latent(n):
                    numerators(n)
                if more:
                    last_step(n + 1)
                update(n)
                if more:
                    weigh(n + 1)
                dve.drain()
                if latent(n):
                    divide(n)
                dve.drain()
                dve.nop().then_inc(S["kept"], 1)


def mlstm_out(nc, name, hsum, xcv, z, c_norm, c_skip, out, ident, eps):
    NU = NCH * MH
    with Stage(nc, name) as st:
        sq = st.sb("sq", [P, MD])
        ss = st.sb("ss", [P, NU])
        tmp = st.sb("tmp", [P, 2, SEQ])
        banks = [st.pb(f"bank{i}") for i in range(2)]
        rooted, normed, turned, taken, scaled = (st.sem(n) for n in ("rooted", "normed", "turned", "taken", "scaled"))
        block = st.cs.enter_context(nc.Block())

        @block.scalar
        def _(act):
            for n in range(NU):
                act.activation(sq[:], hsum[:, n // MH, (n % MH) * MD:(n % MH + 1) * MD], ACT.Square, accum_out=ss[:, n:n + 1])
                act.drain()
            act.activation(ss[:], ss[:], ACT.Sqrt, bias=eps, scale=1.0 / MD).then_inc(rooted, 1)
            for t in range(KT):
                act.wait_ge(turned, t + 1)
                if t >= 2:
                    act.wait_ge(taken, t - 1)
                act.activation(tmp[:, t % 2, :], banks[t % 2][:], ACT.Copy, scale=c_norm[:, t:t + 1]).then_inc(scaled, 1)

        @block.vector
        def _(dve):
            dve.wait_ge(rooted, 1)
            dve.reciprocal(ss[:], ss[:])
            dve.drain()
            h3 = hsum[:].rearrange("p c (h n) -> p (c h) n", h=MH)
            dve.tensor_tensor(h3, h3, last(ss[:], MD), ALU.mult).then_inc(normed, 1)
            for t in range(KT):
                dve.wait_ge(scaled, t + 1)
                dve.scalar_tensor_tensor(out=out[:, t, :], in0=xcv[:, t, CTX:ALLTOK], scalar=c_skip[:, t:t + 1], in1=tmp[:, t % 2, :],
                                         op0=ALU.mult, op1=ALU.add).then_inc(taken, 1)
                dve.drain()
                dve.tensor_tensor(out[:, t, :], out[:, t, :], z[:, t, :], ALU.mult)

        @block.tensor
        def _(pe):
            pe.wait_ge(normed, 1)
            for t in range(KT):
                if t >= 2:
                    pe.wait_ge(scaled, t - 1)
                for i in range(NCH):
                    mm = pe.transpose(banks[t % 2][:, i * P:(i + 1) * P], hsum[:, i, t * P:(t + 1) * P], ident[:])
                mm.then_inc(turned, 1)


def mixer_mlstm(nc, a, c, L, x, tap):
    with Stage(nc, "ml") as st:
        xcv = st.sb("xcv", [P, KT, ALLTOK])
        z = st.sb("z", [P, KT, SEQ])
        q = st.sb("q", [P, KT, SEQ])
        hsum = st.sb("hsum", [P, NCH, D])
        with Stage(nc, "ml2") as s1:
            m = Parts()
            m.b, m.cc = s1.sb("b", [P, CHUNKS, 2, MH]), s1.sb("cc", [P, CHUNKS, 2, MH])
            lower = s1.sb("lower", [P, P])
            neg = [s1.sb(f"neg{d}", [P, P]) for d in range(2)]
            edge = [s1.sb(f"edge{d}", [P, P]) for d in range(2)]
            load(nc, "mlload", [(lower[:], a["lower"]), (neg[0][:], a["neg_later0"]), (neg[1][:], a["neg_later1"]),
                                (edge[0][:], a["edge0"]), (edge[1][:], a["edge1"])])
            xm = s1.sb("xm", [P, KT, ALLTOK])
            with Stage(nc, "ml3") as s2:
                h = Split(s2, "h", [P, KT, ALLTOK])
                raw, gbias = s2.sb("raw", [P, CHUNKS, 16]), s2.sb("gbias", [P, 16])
                cw, cb = s2.sb("cw", [P, KT, 3]), s2.sb("cb", [P, KT, 1])
                load(nc, "mlload2", [(cw[:], a["c_conv"]), (cb[:], a["c_conv_b"]), (gbias[:, 0:8], broadcast_rows(a["c_bi"], 8)),
                                     (gbias[:, 8:16], broadcast_rows(a["c_bf"], 8))])
                pre_norm(nc, "ml", c, L, 0, x, h, SEQS)

                def conv(e, m_, b, banks, t):
                    for j, (t0, tw) in enumerate(SEQS):
                        ins = conv3(e, t[:, t0:t0 + tw], banks[0][j][:, 0:tw], lambda i: cw[:, m_, i:i + 1], tw)
                    return ins

                def keep(e, m_, b, banks, t):
                    e.activation(xcv[:, m_, :], t[:], ACT.Silu, bias=cb[:, m_, :])
                    for j, (t0, tw) in enumerate(SEQS):
                        ins = e.activation(xm[:, m_, t0:t0 + tw], banks[0][j][:, 0:tw], ACT.Copy)
                    return ins

                project(nc, "xm", a["w_c_xm"], [h.tiles(KT)], SEQS, [("vector", conv), ("scalar", keep)], unroll=4, max_sets=2, per_piece=4,
                        temps=lambda s, n: [s.sb(f"acc{i}", [P, ALLTOK]) for i in range(n)])
                project(nc, "mz", a["w_c_z"], [h.tiles(KT)], SEQS[1:],
                        [("scalar", lambda e, m_, b, banks, t: e.activation(z[:, m_, :], banks[0][0][:], ACT.Sigmoid))], unroll=4, raw_slots=2)
                narrow(nc, "mg", a["w_c_gates"], h.tiles(KT), SEQS, raw, c.ident)
                mlstm_gates(nc, "mgates", raw, gbias, (c.upper, lower), m, c.one)
            tap("xcv", xcv)
            tap("m_cc", m.cc)
            k = s1.sb("k", [P, KT, SEQ])
            ktok = xm[:].rearrange("p k t -> p (k t)").rearrange("p (c n) -> p c n", c=CHUNKS)
            vtok = s1.sb("vtok", [P, CHUNKS, MH, MD + 1])
            with Stage(nc, "ml4") as s2:
                mask = s2.sb("mask", [P, P])
                ws = []
                compact = [s2.sb(f"compact{i}", [P, KT, 4]) for i in range(3)]
                load(nc, "mlload3", [(mask[:], a["block4"])] + [(compact[i][:], a[n]) for i, n in enumerate(("c_wq", "c_wk", "c_wv"))])
                for i in range(3):
                    ws.append(s2.sb(f"w{i}", [P, KT, P]))
                    expand_blocks(nc, f"expand{i}", compact[i], mask, ws[i])
                mlstm_heads(nc, "mheads", xm, xcv, *ws, q, k, ktok, vtok)
            mlstm_scan(nc, "mscan", m, q, k, ktok, vtok, hsum, c.ident, neg, edge)
        tap("hsum", hsum)
        cn, ck = st.sb("cn", [P, KT]), st.sb("ck", [P, KT])
        load(nc, "mlload4", [(cn[:], a["c_norm"]), (ck[:], a["c_skip"])])
        mlstm_out(nc, "mout", hsum, xcv, z, cn, ck, q, c.ident, c.eps)
        y, sums = st.sb("y", [P, KT, SEQ]), st.sb("sums", [P, SEQ])
        out_parts = Split(st, "out", [P, KT, SEQ])
        split_up(nc, "out_parts", q, out_parts, KT)
        down(nc, "mlout", a["w_c_out"], out_parts.tiles(KT), y, sums, SEQS[1:], CTX)
        post_norm(nc, "mlp", c, L, 2, x, y, sums, SEQS[1:], CTX)


class Constants:
    pass


def build(nc, a, out, tap=lambda name, buf: None, start=0):
    Stage.number[0] = 0
    with Stage(nc, "whole") as st:
        c = Constants()
        pairs = []

        def const(name, shape):
            buf = st.sb(name, shape)
            pairs.append((buf[:], a[name]))
            return buf

        c.ident, c.flip, c.one, c.upper, c.neg_lower = (
            const(n, [P, P]) for n in ("ident", "flip", "one", "upper", "neg_lower"))
        c.eps_buf = const("eps", [P, 1])
        c.eps = c.eps_buf[:, 0:1]
        c.norm1, c.norm2 = const("norm1_w", [P, KT]), const("norm2_w", [P, KT])
        c.final = const("final_norm_w", [P, KT])
        c.ssm_norm = const("ssm_norm_w", [P, 16])
        c.conv_w, c.conv_b = const("conv_w", [P, 24, 4]), const("conv_b", [P, 24, 1])
        streams = st.sb("streams", [P, KT, ALLTOK])
        x = streams[:, :, CTX:ALLTOK]
        pairs += [(x, a["x"]), (streams[:, :, 0:CTX], a["ctx"])]
        load(nc, "load", pairs)
        c.sums = st.sb("sums", [P, ALLTOK])
        sum_squares(nc, "sums", KT, streams, c.sums[:])
        if start == 0:
            first_block(nc, a, x, c, tap)
        sums = c.sums[:, CTX:ALLTOK]
        rms_norm(nc, "final", KT, SEQ, lambda k: x[:, k, :], lambda k: x[:, k, :], c, sums,
                 gain=lambda k: c.final[:, k:k + 1], next_sums=sums)
        second_block(nc, a, c, streams, tap)
        with Stage(nc, "store") as last_stage:
            stored = last_stage.sem("stored")
            block = last_stage.cs.enter_context(nc.Block())

            @block.sync
            def _(sp):
                sp.dma_start(out, x).then_inc(stored, 16)
                sp.wait_ge(stored, 16)


def chan(v, extra=()):
    import numpy as np
    return np.ascontiguousarray(np.moveaxis(v.reshape(-1, P, *v.shape[1:]), 1, 0))


def by_tile(w, width=P):
    import numpy as np
    K, M = w.shape
    return np.ascontiguousarray(w.reshape(K // P, P, M // width, width).transpose(2, 1, 0, 3)).reshape(M // width, P, -1)


def shape_constants():
    import numpy as np
    i = np.arange(P)
    c = {"ident": np.eye(P), "flip": np.eye(P)[::-1], "one": np.ones((P, P)), "upper": i[:, None] <= i[None, :],
         "neg_lower": np.where(i[:, None] > i[None, :], NEG, 0.0), "eps": np.full((P, 1), EPS),
         "neg_row": np.ones((1, 3 * HEADS))}

    def bucket(dist):
        f = np.maximum(dist, 1).astype(np.float32)
        large = 16 + (np.log(f / np.float32(16)) / np.float32(np.log(128.0)) * np.float32(16)).astype(np.int32)
        return np.where(dist < 16, dist, np.minimum(large, 31))

    u = P - 1 - np.arange(2 * P)
    hot = np.zeros((33, TABLES, 2 * P))
    for t in range(TABLES):
        if t < 2 * DIL - 1:
            s, ok, dil = DIL * u + DIL - 1 - t, True, 1
        elif t == 2 * DIL - 1:
            s, ok, dil = u, True, DIL
        else:
            s, ok, dil = u // 4, u % 4 == 0, 16
        ok = ok & (s >= 0) & (s <= P)
        b = bucket(np.where(ok, s, 0) * dil)
        for w in range(2 * P):
            hot[b[w] if ok[w] else 32, t, w] = 1.0 if ok[w] else NEG
    c["bias_onehot"] = hot
    before, same = i[:, None] < i[None, :], i[:, None] == i[None, :]
    c["lower"] = i[:, None] >= i[None, :]
    c["blk64"] = i[:, None] // 64 == i[None, :] // 64
    c["block4"] = i[:, None] // 4 == i[None, :] // 4
    c["ln_eps"] = np.full((P, 1), LN_EPS)
    c["neg_later0"] = np.where(before, NEG, 0.0)
    c["neg_later1"] = np.where(before.T, NEG, 0.0)
    c["edge0"], c["edge1"] = (np.broadcast_to((i == e)[:, None], (P, P)) for e in (P - 1, 0))
    strict = np.zeros((P, 2, 2, 2 * P))
    for d, bf in enumerate((before, before.T)):
        for s, sign in enumerate((1.0, -1.0)):
            strict[:, d, s] = sign * np.concatenate([bf, bf | same], axis=1)
    c["strict"] = strict.reshape(P, 2, 4 * P)

    def level(m):
        return (i[:, None] // (2 * m) == i[None, :] // (2 * m)) & (i[:, None] // m % 2 == 1) & (i[None, :] // m % 2 == 0)

    c["x1"] = np.stack([-1.0 * level(1), -1.0 * level(1).T], axis=1)
    levels = np.stack([np.stack([level(m), level(m).T]) for m in (1, 2, 4, 8, 16, 32, 64)], axis=1).transpose(2, 0, 1, 3)
    c["levels"] = levels
    return {n: np.ascontiguousarray(v, np.float32) for n, v in c.items()}


def lay_out(i):
    import numpy as np
    f = {n: np.asarray(v) for n, v in i.items()}
    w = f["w_in"][0]
    cut = np.cumsum([1536, 1536, 1536, 2048, 3072, 32])
    a = {
        "x": chan(np.ascontiguousarray(f["x"][0].T)),
        "norm1_w": chan(f["norm1_w"][0]), "norm2_w": chan(f["norm2_w"][0]), "final_norm_w": chan(f["final_norm_w"]),
        "ssm_norm_w": chan(f["ssm_norm_w"][0]),
        "conv_w": chan(np.ascontiguousarray(f["conv_w"][0].T)), "conv_b": chan(f["conv_b"][0][:, None]),
        "dt_bias": f["dt_bias"][0], "a_log": f["a_log"][0], "d_skip": f["d_skip"][0], "rel_bias": f["rel_bias"],
        "w_qk": by_tile(w[:, :cut[1]]), "w_v": by_tile(w[:, cut[1]:cut[2]], 512), "w_z": by_tile(w[:, cut[2]:cut[3]], 512),
        "w_x": by_tile(w[:, cut[3]:cut[3] + 2048]), "w_bc": by_tile(w[:, cut[3] + 2048:cut[4]]), "w_dt": by_tile(w[:, cut[4]:cut[5]], 32),
        "w_merge": np.concatenate([by_tile(w[:, cut[5]:cut[5] + D]), by_tile(w[:, cut[5] + D:]),
                                   by_tile(f["w_attn_branch"][0]), by_tile(f["w_ssm_branch"][0])], axis=2),
        "w_out": by_tile(f["w_out"][0]),
        "w_ffn_in": np.concatenate([by_tile(f["w_ffn_in"][0][:, :2816]), by_tile(f["w_ffn_in"][0][:, 2816:])], axis=2),
        "w_ffn_out": by_tile(f["w_ffn_out"][0]),
    }
    a["ctx"] = chan(np.ascontiguousarray(f["ctx_2"][0].T))
    a["w_ada"] = np.concatenate([by_tile(f["ada_w_2"][i], 512) for i in range(2)], axis=0)
    a["ada_b"] = np.repeat(chan(f["ada_b_2"].reshape(-1))[:, :, None], 2, axis=2)
    a["cvec"] = np.ascontiguousarray(np.stack([chan(f["c_ctx_2"]), chan(f["c_2"][0])], axis=2))
    for i in range(2):
        for n in ("norm_mix_pre", "norm_mix_post", "norm_ffn_pre", "norm_ffn_post"):
            a[f"{n}{i}"] = chan(f[n + "_2"][i])
        up = f["ffn_up_2"][i]
        a[f"w_ffn_up{i}"] = np.concatenate([by_tile(up[:, :2816]), by_tile(up[:, 2816:])], axis=2)
        a[f"w_ffn_down{i}"] = by_tile(f["ffn_down_2"][i])
        a[f"ffn_conv{i}"] = chan(np.ascontiguousarray(f["ffn_conv_2"][i].reshape(9, -1).T))
        a[f"ffn_conv_b{i}"] = chan(f["ffn_conv_b_2"][i][:, None])
    w = f["ab_w_in_2"][0]
    a["w_ab_u"], a["w_ab_v"] = by_tile(w[:, :512]), by_tile(w[:, 512:1024], 512)
    a["w_ab_rkv"], a["w_ab_lora"], a["w_ab_out"] = by_tile(w[:, 1024:2560]), by_tile(w[:, 2560:]), by_tile(f["ab_w_out_2"][0])
    a["b_shift"] = chan(np.ascontiguousarray(f["b_shift_2"][0].T))
    a["a_ws"] = np.ascontiguousarray(f["a_ws_2"][0].transpose(2, 0, 1))
    a["a_bs"], a["a_gv"] = f["a_bs_2"][0].reshape(-1), f["a_gv_2"][0].reshape(-1)
    a["b_w_up"], a["b_a_up"] = f["b_w_up_2"][0].reshape(P, 512), f["b_a_up_2"][0].reshape(P, 512)
    a["b_g_up"] = f["b_g_up_2"][0]
    for n in ("b_w0", "b_a0"):
        a[n] = np.ascontiguousarray(f[n + "_2"][0].reshape(2, 4, P).transpose(2, 0, 1))
    for n in ("b_ka", "b_kk", "b_rk", "b_ln_g", "b_ln_b", "c_norm", "c_skip"):
        a[n] = chan(f[n + "_2"][0].reshape(-1))
    w = f["c_w_in_2"][0]
    a["w_c_xm"], a["w_c_z"], a["w_c_gates"] = by_tile(w[:, :D]), by_tile(w[:, D:2 * D]), by_tile(w[:, 2 * D:], 16)
    a["w_c_out"] = by_tile(f["c_w_out_2"][0])
    a["c_conv"], a["c_conv_b"] = chan(np.ascontiguousarray(f["c_conv_2"][0].T)), chan(f["c_conv_b_2"][0][:, None])
    a["c_bi"], a["c_bf"] = f["c_bi_2"][0].reshape(-1), f["c_bf_2"][0].reshape(-1)
    for n in ("c_wq", "c_wk", "c_wv"):
        a[n] = chan(f[n + "_2"][0].reshape(D, 4))
    return {n: np.ascontiguousarray(v) for n, v in a.items()}


SCRATCH = {"line_scratch": (HEADS, TABLES, 2 * P)}
OUT = (P, KT, SEQ)


def kernel(**inputs):
    import numpy as np
    import concourse.bacc as bacc
    from concourse.bass_utils import run_bass_kernel_spmd

    nc = bacc.Bacc("TRN2", target_bir_lowering=False, num_devices=1)
    arrays = {**lay_out(inputs), **shape_constants()}
    aps = {n: nc.dram_tensor(f"in_{n}", v.shape, mybir.dt.from_np(v.dtype), kind="ExternalInput").ap() for n, v in arrays.items()}
    aps.update({n: nc.dram_tensor(n, s, F32, kind="Internal").ap() for n, s in SCRATCH.items()})
    out = nc.dram_tensor("out", OUT, F32, kind="ExternalOutput").ap()
    build(nc, aps, out)
    r = run_bass_kernel_spmd(nc, [{f"in_{n}": v for n, v in arrays.items()}], core_ids=[0])
    y = r.results[0]["out"]
    return np.ascontiguousarray(np.moveaxis(y, 1, 0).reshape(D, SEQ).T)[None]
```
